# Optimizing a Trainium2 kernel written in Bass

```python
import jax, jax.numpy as jnp
from jax import lax
import numpy as np

D_MODEL = 1024
BATCH = 1
SEQ = 512
DEPTH = 2

N_MIXERS = 2
N_A_LAYERS = (DEPTH + 1) // 2
N_B_LAYERS = DEPTH // 2

ATT_HEADS = 16
ATT_KV_HEADS = 4
HEAD_DIM = D_MODEL // ATT_HEADS
GROUP = ATT_HEADS // ATT_KV_HEADS
IDX_HEADS = 8
IDX_DIM = 64
TOPK_MAX = 256
Q_BLOCK = 128
ROPE_THETA = 10000.0
Q_COLS = ATT_HEADS * HEAD_DIM
KV_COLS = ATT_KV_HEADS * HEAD_DIM
IQ_COLS = IDX_HEADS * IDX_DIM
IK_COLS = IDX_DIM
IW_COLS = IDX_HEADS
IN_COLS = Q_COLS + 2 * KV_COLS + IQ_COLS + IK_COLS + IW_COLS

RWKV_HEAD = 64
RWKV_HEADS = D_MODEL // RWKV_HEAD
DECAY_LORA = 64
ICL_LORA = 64
GATE_LORA = 160
LNX_EPS = 64e-5

D_FF = 4 * D_MODEL
NORM_EPS = 1e-6


def rms_norm(x, g):
    xf = x.astype(jnp.float32)
    y = xf * lax.rsqrt(jnp.mean(xf * xf, axis=-1, keepdims=True) + NORM_EPS)
    return (y * g.astype(jnp.float32)).astype(x.dtype)

def rope_tables(length, dim):
    inv = 1.0 / (ROPE_THETA ** (jnp.arange(0, dim, 2, dtype=jnp.float32) / dim))
    ang = jnp.arange(length, dtype=jnp.float32)[:, None] * inv[None, :]
    return jnp.cos(ang), jnp.sin(ang)

def apply_rope(x, cos, sin):
    shape = (1, cos.shape[0]) + (1,) * (x.ndim - 3) + (cos.shape[1],)
    c = cos.reshape(shape)
    s = sin.reshape(shape)
    xf = x.astype(jnp.float32)
    x1, x2 = jnp.split(xf, 2, axis=-1)
    return jnp.concatenate([x1 * c - x2 * s, x2 * c + x1 * s], axis=-1).astype(x.dtype)

def dsa_mixer(h, w_in, w_o):
    B, L, _ = h.shape
    top_k = min(TOPK_MAX, L // 4)
    qb_len = min(Q_BLOCK, L)
    n_blk = L // qb_len
    proj = h @ w_in
    o0 = Q_COLS
    o1 = o0 + KV_COLS
    o2 = o1 + KV_COLS
    o3 = o2 + IQ_COLS
    o4 = o3 + IK_COLS
    q = proj[..., :o0].reshape(B, L, ATT_HEADS, HEAD_DIM)
    k = proj[..., o0:o1].reshape(B, L, ATT_KV_HEADS, HEAD_DIM)
    v = proj[..., o1:o2].reshape(B, L, ATT_KV_HEADS, HEAD_DIM)
    qi = proj[..., o2:o3].reshape(B, L, IDX_HEADS, IDX_DIM)
    ki = proj[..., o3:o4]
    wi = proj[..., o4:] * (IDX_HEADS ** -0.5 * IDX_DIM ** -0.5)
    cos, sin = rope_tables(L, HEAD_DIM)
    q = apply_rope(q, cos, sin)
    k = apply_rope(k, cos, sin)
    cos_i, sin_i = rope_tables(L, IDX_DIM)
    qi = apply_rope(qi, cos_i, sin_i)
    ki = apply_rope(ki, cos_i, sin_i)

    def to_blocks(a):
        return jnp.moveaxis(a.reshape((B, n_blk, qb_len) + a.shape[2:]), 1, 0)

    s_pos = jnp.arange(L, dtype=jnp.int32)

    def block_fn(args):
        q_blk, qi_blk, wi_blk, start = args
        t_pos = start + jnp.arange(qb_len, dtype=jnp.int32)
        rel = jax.nn.relu(jnp.einsum('bthd,bsd->bths', qi_blk, ki).astype(jnp.float32))
        score = jnp.einsum('bths,bth->bts', rel, wi_blk.astype(jnp.float32))
        causal = s_pos[None, :] <= t_pos[:, None]
        score = jnp.where(causal[None], score, -jnp.inf)
        _, sel = lax.top_k(score, top_k)
        valid = sel <= t_pos[None, :, None]
        k_sel = jax.vmap(lambda kb, ib: kb[ib])(k, sel)
        v_sel = jax.vmap(lambda vb, ib: vb[ib])(v, sel)
        qg = q_blk.reshape(B, qb_len, ATT_KV_HEADS, GROUP, HEAD_DIM)
        logits = jnp.einsum('btngd,btknd->btngk', qg, k_sel).astype(jnp.float32) * (HEAD_DIM ** -0.5)
        logits = jnp.where(valid[:, :, None, None, :], logits, -jnp.inf)
        p = jax.nn.softmax(logits, axis=-1).astype(v_sel.dtype)
        o = jnp.einsum('btngk,btknd->btngd', p, v_sel)
        return o.reshape(B, qb_len, ATT_HEADS * HEAD_DIM)

    starts = jnp.arange(n_blk, dtype=jnp.int32) * qb_len
    o = lax.map(block_fn, (to_blocks(q), to_blocks(qi), to_blocks(wi), starts))
    o = jnp.moveaxis(o, 0, 1).reshape(B, L, ATT_HEADS * HEAD_DIM)
    return o @ w_o

def token_shift(x):
    return jnp.pad(x, ((0, 0), (1, 0), (0, 0)))[:, :-1]

def rwkv7_mixer(h, mu, w_rkv, w0, w1, w2, a0, a1, a2, g1, g2, k_k, k_a, r_k, lnx_w, lnx_b, w_o):
    B, L, D = h.shape
    H, N = RWKV_HEADS, RWKV_HEAD
    f32 = jnp.float32
    xx = token_shift(h) - h
    xs = h[None] + xx[None] * mu[:, None, None, :]
    r, k, v = jnp.einsum('cbld,cde->cble', xs[:3], w_rkv)
    xw, xa, xg = xs[3], xs[4], xs[5]
    w_log = -jax.nn.softplus(-(w0 + jnp.tanh(xw @ w1) @ w2).astype(f32)) - 0.5
    decay = jnp.exp(-jnp.exp(w_log))
    a = jax.nn.sigmoid((a0 + (xa @ a1) @ a2).astype(f32))
    g = jax.nn.sigmoid(xg @ g1) @ g2
    kf = k.astype(f32)
    kk = (kf * k_k.astype(f32)).reshape(B, L, H, N)
    kk = kk * lax.rsqrt(jnp.maximum(jnp.sum(kk * kk, axis=-1, keepdims=True), 1e-24))
    kf = kf * (1.0 + (a - 1.0) * k_a.astype(f32))

    def heads(z):
        return z.reshape(B, L, H, N)

    rh, wh, kh, vh, ah = heads(r.astype(f32)), heads(decay), heads(kf), heads(v.astype(f32)), heads(a)
    bh = kk * ah

    def step(state, inp):
        r_t, w_t, k_t, v_t, kk_t, b_t = inp
        sa = jnp.einsum('bhvk,bhk->bhv', state, -kk_t)
        state = (state * w_t[:, :, None, :] + sa[..., None] * b_t[:, :, None, :]
                 + v_t[..., None] * k_t[:, :, None, :])
        y = jnp.einsum('bhvk,bhk->bhv', state, r_t)
        return state, y

    def tm(z):
        return jnp.moveaxis(z, 1, 0)

    state0 = jnp.zeros((B, H, N, N), f32)
    _, y = lax.scan(step, state0, (tm(rh), tm(wh), tm(kh), tm(vh), tm(kk), tm(bh)))
    y = jnp.moveaxis(y, 0, 1)
    mean = jnp.mean(y, axis=-1, keepdims=True)
    var = jnp.mean(jnp.square(y - mean), axis=-1, keepdims=True)
    y = ((y - mean) * lax.rsqrt(var + LNX_EPS) * lnx_w.astype(f32).reshape(H, N)
         + lnx_b.astype(f32).reshape(H, N))
    bonus = jnp.sum(rh * kh * r_k.astype(f32), axis=-1, keepdims=True) * vh
    out = (y + bonus).reshape(B, L, D).astype(h.dtype) * g
    return out @ w_o

def sqrelu_mlp(h, w_up, w_down):
    u = jax.nn.relu(h @ w_up)
    return (u * u) @ w_down

def first_inputs(seed: int = 0) -> dict:
    key = jax.random.key(seed)
    ks = jax.random.split(key, 32)
    D = D_MODEL

    def nrm(k, shape, scale):
        return jax.random.normal(k, shape, jnp.float32) * scale

    nA, nB = N_A_LAYERS, N_B_LAYERS
    return {
        "x": nrm(ks[0], (BATCH, SEQ, D), 1.0),
        "mixer_norm": 1.0 + nrm(ks[1], (DEPTH, D), 0.02),
        "mlp_norm": 1.0 + nrm(ks[2], (DEPTH, D), 0.02),
        "mlp_w_up": nrm(ks[3], (DEPTH, D, D_FF), D ** -0.5),
        "mlp_w_down": nrm(ks[4], (DEPTH, D_FF, D), D_FF ** -0.5),
        "final_norm": 1.0 + nrm(ks[5], (D,), 0.02),
        "dsa_w_in": nrm(ks[6], (nA, D, IN_COLS), D ** -0.5),
        "dsa_w_o": nrm(ks[7], (nA, Q_COLS, D), Q_COLS ** -0.5),
        "rwkv_mu": jax.random.uniform(ks[8], (nB, 6, D), jnp.float32),
        "rwkv_w_rkv": nrm(ks[9], (nB, 3, D, D), D ** -0.5),
        "rwkv_w0": jnp.linspace(-6.0, -1.0, D, dtype=jnp.float32)[None, :] + nrm(ks[10], (nB, D), 0.1),
        "rwkv_w1": nrm(ks[11], (nB, D, DECAY_LORA), D ** -0.5),
        "rwkv_w2": nrm(ks[12], (nB, DECAY_LORA, D), 0.1 * DECAY_LORA ** -0.5),
        "rwkv_a0": nrm(ks[13], (nB, D), 0.1),
        "rwkv_a1": nrm(ks[14], (nB, D, ICL_LORA), D ** -0.5),
        "rwkv_a2": nrm(ks[15], (nB, ICL_LORA, D), 0.1 * ICL_LORA ** -0.5),
        "rwkv_g1": nrm(ks[16], (nB, D, GATE_LORA), D ** -0.5),
        "rwkv_g2": nrm(ks[17], (nB, GATE_LORA, D), GATE_LORA ** -0.5),
        "rwkv_k_k": 0.85 + nrm(ks[18], (nB, D), 0.02),
        "rwkv_k_a": 1.0 + nrm(ks[19], (nB, D), 0.02),
        "rwkv_r_k": -0.04 + nrm(ks[20], (nB, RWKV_HEADS, RWKV_HEAD), 0.02),
        "rwkv_lnx_w": 1.0 + nrm(ks[21], (nB, D), 0.02),
        "rwkv_lnx_b": nrm(ks[22], (nB, D), 0.02),
        "rwkv_w_o": nrm(ks[23], (nB, D, D), D ** -0.5),
    }

def first_block(x, mixer_norm, mlp_norm, mlp_w_up, mlp_w_down, final_norm, dsa_w_in, dsa_w_o,
              rwkv_mu, rwkv_w_rkv, rwkv_w0, rwkv_w1, rwkv_w2, rwkv_a0, rwkv_a1, rwkv_a2,
              rwkv_g1, rwkv_g2, rwkv_k_k, rwkv_k_a, rwkv_r_k, rwkv_lnx_w, rwkv_lnx_b, rwkv_w_o):
    for i in range(DEPTH):
        h = rms_norm(x, mixer_norm[i])
        j = i // N_MIXERS
        if i % N_MIXERS == 0:
            x = x + dsa_mixer(h, dsa_w_in[j], dsa_w_o[j])
        else:
            x = x + rwkv7_mixer(h, rwkv_mu[j], rwkv_w_rkv[j], rwkv_w0[j], rwkv_w1[j], rwkv_w2[j],
                                rwkv_a0[j], rwkv_a1[j], rwkv_a2[j], rwkv_g1[j], rwkv_g2[j],
                                rwkv_k_k[j], rwkv_k_a[j], rwkv_r_k[j], rwkv_lnx_w[j],
                                rwkv_lnx_b[j], rwkv_w_o[j])
        x = x + sqrelu_mlp(rms_norm(x, mlp_norm[i]), mlp_w_up[i], mlp_w_down[i])
    return rms_norm(x, final_norm)


DEPTH_2 = 1

MIX_WIDTH = D_MODEL
CONV_WIDTH = MIX_WIDTH // 2
CONV_GROUPS = 8
CONV_K = 3
MLSTM_HEADS = 4
MLSTM_V_DIM = (MIX_WIDTH - CONV_WIDTH) // MLSTM_HEADS
MLSTM_QK_DIM = MLSTM_V_DIM // 2
CHUNK = 128
D_FF_2 = 2816
FFN_RESIDUAL_SCALE = 0.5
EPS = 1e-6
NEG_INF = -1e30
IN_SIZES = (CONV_WIDTH, CONV_WIDTH, CONV_WIDTH,
            MLSTM_HEADS * MLSTM_QK_DIM, MLSTM_HEADS * MLSTM_QK_DIM,
            MLSTM_HEADS * MLSTM_V_DIM, MLSTM_HEADS * MLSTM_V_DIM,
            2 * MLSTM_HEADS, 2 * MLSTM_HEADS)
W_IN_COLS = sum(IN_SIZES)


def rmsnorm(x, g):
    x32 = x.astype(jnp.float32)
    y = x32 * lax.rsqrt(jnp.mean(x32 * x32, axis=-1, keepdims=True) + EPS)
    return (y * g.astype(jnp.float32)).astype(x.dtype)

def swiglu(x, w_in, w_out):
    gate, up = jnp.split(x @ w_in, 2, axis=-1)
    return (jax.nn.silu(gate) * up) @ w_out

def mlstm_chunkwise(q, k, v, li, lf):
    B, H, S, DK = q.shape
    DV = v.shape[-1]
    NC = S // CHUNK
    q = q.reshape(B, H, NC, CHUNK, DK)
    k = k.reshape(B, H, NC, CHUNK, DK)
    v = v.reshape(B, H, NC, CHUNK, DV)
    li = li.reshape(B, H, NC, CHUNK)
    lf = lf.reshape(B, H, NC, CHUNK)
    b = jnp.cumsum(lf, axis=-1)
    g = b[..., -1]
    causal = jnp.tril(jnp.ones((CHUNK, CHUNK), dtype=bool))
    D = jnp.where(causal, b[..., :, None] - b[..., None, :] + li[..., None, :], NEG_INF)
    m_intra = jnp.max(D, axis=-1)
    w = g[..., None] - b + li
    m_chunk = jnp.max(w, axis=-1)
    e = jnp.exp(w - m_chunk[..., None])
    C_chunk = jnp.einsum('bhcl,bhclk,bhclv->bhckv', e, k, v)
    n_chunk = jnp.einsum('bhcl,bhclk->bhck', e, k)

    def step(carry, inp):
        C, n, m = carry
        g_c, Cc, nc, mc = inp
        m_new = jnp.maximum(g_c + m, mc)
        a = jnp.exp(g_c + m - m_new)
        s = jnp.exp(mc - m_new)
        C_new = a[..., None, None] * C + s[..., None, None] * Cc
        n_new = a[..., None] * n + s[..., None] * nc
        return (C_new, n_new, m_new), (C, n, m)

    init = (jnp.zeros((B, H, DK, DV), jnp.float32),
            jnp.zeros((B, H, DK), jnp.float32),
            jnp.full((B, H), NEG_INF, jnp.float32))
    xs = (jnp.moveaxis(g, 2, 0), jnp.moveaxis(C_chunk, 2, 0),
          jnp.moveaxis(n_chunk, 2, 0), jnp.moveaxis(m_chunk, 2, 0))
    _, (C_prev, n_prev, m_prev) = lax.scan(step, init, xs)
    C_prev = jnp.moveaxis(C_prev, 0, 2)
    n_prev = jnp.moveaxis(n_prev, 0, 2)
    m_prev = jnp.moveaxis(m_prev, 0, 2)

    m_inter = b + m_prev[..., None]
    m_t = jnp.maximum(m_inter, m_intra)
    P = jnp.exp(D - m_t[..., None]) * jnp.einsum('bhctk,bhcsk->bhcts', q, k)
    inter = jnp.exp(m_inter - m_t)
    numer = inter[..., None] * jnp.einsum('bhctk,bhckv->bhctv', q, C_prev) \
        + jnp.einsum('bhcts,bhcsv->bhctv', P, v)
    denom = inter * jnp.einsum('bhctk,bhck->bhct', q, n_prev) + jnp.sum(P, axis=-1)
    h = numer / jnp.maximum(jnp.abs(denom), jnp.exp(-m_t))[..., None]
    return h.reshape(B, H, S, DV)

def mixer(xn, w_in, conv_w, conv_b, gate_i_bias, gate_f_bias, head_gain, w_out):
    Bsz, S, _ = xn.shape
    H, DK, DV = MLSTM_HEADS, MLSTM_QK_DIM, MLSTM_V_DIM
    split_points = [int(p) for p in np.cumsum(IN_SIZES)[:-1]]
    bg, cg, hc, q, k, v, o, ig, fg = jnp.split(xn @ w_in, split_points, axis=-1)

    u = cg * hc
    u = lax.conv_general_dilated(u, conv_w[:, None, :].astype(u.dtype), window_strides=(1,),
                                 padding=[(1, 1)], dimension_numbers=('NWC', 'WIO', 'NWC'),
                                 feature_group_count=CONV_WIDTH)
    y_conv = bg * (u + conv_b.astype(u.dtype))

    def heads(t, d):
        return t.reshape(Bsz, S, H, d).transpose(0, 2, 1, 3).astype(jnp.float32)
    qh = heads(q, DK) * (DK ** -0.5)
    kh = heads(k, DK)
    vh = heads(v, DV)
    li = (ig.astype(jnp.float32) + gate_i_bias.astype(jnp.float32)).reshape(Bsz, S, 2, H).transpose(2, 0, 3, 1)
    lf = jax.nn.log_sigmoid(fg.astype(jnp.float32) + gate_f_bias.astype(jnp.float32)).reshape(Bsz, S, 2, H).transpose(2, 0, 3, 1)
    h_fwd = mlstm_chunkwise(qh, kh, vh, li[0], lf[0])
    flip = lambda t: jnp.flip(t, axis=2)
    h_bwd = flip(mlstm_chunkwise(flip(qh), flip(kh), flip(vh), flip(li[1]), flip(lf[1])))
    h = h_fwd + h_bwd
    h = h * lax.rsqrt(jnp.mean(h * h, axis=-1, keepdims=True) + EPS) \
        * head_gain.astype(jnp.float32).reshape(H, 1, DV)
    h = h.transpose(0, 2, 1, 3).reshape(Bsz, S, H * DV).astype(xn.dtype)
    y_mlstm = jax.nn.sigmoid(o) * h

    return jnp.concatenate([y_conv, y_mlstm], axis=-1) @ w_out

def second_inputs(seed: int = 0) -> dict:
    key = jax.random.key(seed)
    ks = jax.random.split(key, 20)
    H = MLSTM_HEADS

    def nrm(k, shape, scale):
        return jax.random.normal(k, shape, jnp.float32) * scale

    def gain(k, n):
        return 1.0 + 0.05 * jax.random.normal(k, (DEPTH_2, n), jnp.float32)

    f_bias = jnp.tile(jnp.linspace(3.0, 6.0, H, dtype=jnp.float32), 2)[None, :] + nrm(ks[12], (DEPTH_2, 2 * H), 0.1)
    return {
        'x': jax.random.normal(ks[0], (BATCH, SEQ, D_MODEL), jnp.float32),
        'norm_ffn1_pre': gain(ks[1], D_MODEL),
        'norm_ffn1_post': gain(ks[2], D_MODEL),
        'w_ffn1_in': nrm(ks[3], (DEPTH_2, D_MODEL, 2 * D_FF_2), D_MODEL ** -0.5),
        'w_ffn1_out': nrm(ks[4], (DEPTH_2, D_FF_2, D_MODEL), D_FF_2 ** -0.5),
        'norm_mix_pre': gain(ks[5], D_MODEL),
        'norm_mix_post': gain(ks[6], D_MODEL),
        'w_mix_in': nrm(ks[7], (DEPTH_2, D_MODEL, W_IN_COLS), D_MODEL ** -0.5),
        'conv_w': nrm(ks[8], (DEPTH_2, CONV_K, CONV_WIDTH), CONV_K ** -0.5),
        'conv_b': nrm(ks[9], (DEPTH_2, CONV_WIDTH), 0.02),
        'gate_i_bias': nrm(ks[10], (DEPTH_2, 2 * H), 0.1),
        'gate_f_bias': f_bias,
        'mlstm_norm': gain(ks[11], H * MLSTM_V_DIM),
        'w_mix_out': nrm(ks[13], (DEPTH_2, MIX_WIDTH, D_MODEL), MIX_WIDTH ** -0.5),
        'norm_ffn2_pre': gain(ks[14], D_MODEL),
        'norm_ffn2_post': gain(ks[15], D_MODEL),
        'w_ffn2_in': nrm(ks[16], (DEPTH_2, D_MODEL, 2 * D_FF_2), D_MODEL ** -0.5),
        'w_ffn2_out': nrm(ks[17], (DEPTH_2, D_FF_2, D_MODEL), D_FF_2 ** -0.5),
    }

def second_block(x, norm_ffn1_pre, norm_ffn1_post, w_ffn1_in, w_ffn1_out,
              norm_mix_pre, norm_mix_post, w_mix_in, conv_w, conv_b,
              gate_i_bias, gate_f_bias, mlstm_norm, w_mix_out,
              norm_ffn2_pre, norm_ffn2_post, w_ffn2_in, w_ffn2_out):
    for l in range(DEPTH_2):
        h = swiglu(rmsnorm(x, norm_ffn1_pre[l]), w_ffn1_in[l], w_ffn1_out[l])
        x = x + FFN_RESIDUAL_SCALE * rmsnorm(h, norm_ffn1_post[l])
        h = mixer(rmsnorm(x, norm_mix_pre[l]), w_mix_in[l], conv_w[l], conv_b[l],
                  gate_i_bias[l], gate_f_bias[l], mlstm_norm[l], w_mix_out[l])
        x = x + rmsnorm(h, norm_mix_post[l])
        h = swiglu(rmsnorm(x, norm_ffn2_pre[l]), w_ffn2_in[l], w_ffn2_out[l])
        x = x + FFN_RESIDUAL_SCALE * rmsnorm(h, norm_ffn2_post[l])
    return x


def setup_inputs(seed=0):
    out = dict(first_inputs(seed))
    for name, value in second_inputs(seed + 1).items():
        if name != "x":
            out[name + "_2"] = value
    return out


def reference(
    x, mixer_norm, mlp_norm, mlp_w_up, mlp_w_down, final_norm, dsa_w_in, dsa_w_o, rwkv_mu,
    rwkv_w_rkv, rwkv_w0, rwkv_w1, rwkv_w2, rwkv_a0, rwkv_a1, rwkv_a2, rwkv_g1, rwkv_g2,
    rwkv_k_k, rwkv_k_a, rwkv_r_k, rwkv_lnx_w, rwkv_lnx_b, rwkv_w_o, norm_ffn1_pre_2,
    norm_ffn1_post_2, w_ffn1_in_2, w_ffn1_out_2, norm_mix_pre_2, norm_mix_post_2, w_mix_in_2,
    conv_w_2, conv_b_2, gate_i_bias_2, gate_f_bias_2, mlstm_norm_2, w_mix_out_2,
    norm_ffn2_pre_2, norm_ffn2_post_2, w_ffn2_in_2, w_ffn2_out_2,
):
    x = first_block(
        x, mixer_norm, mlp_norm, mlp_w_up, mlp_w_down, final_norm, dsa_w_in, dsa_w_o, rwkv_mu,
        rwkv_w_rkv, rwkv_w0, rwkv_w1, rwkv_w2, rwkv_a0, rwkv_a1, rwkv_a2, rwkv_g1, rwkv_g2,
        rwkv_k_k, rwkv_k_a, rwkv_r_k, rwkv_lnx_w, rwkv_lnx_b, rwkv_w_o,
    )
    return second_block(
        x, norm_ffn1_pre_2, norm_ffn1_post_2, w_ffn1_in_2, w_ffn1_out_2, norm_mix_pre_2,
        norm_mix_post_2, w_mix_in_2, conv_w_2, conv_b_2, gate_i_bias_2, gate_f_bias_2,
        mlstm_norm_2, w_mix_out_2, norm_ffn2_pre_2, norm_ffn2_post_2, w_ffn2_in_2, w_ffn2_out_2,
    )


_drawn_inputs = setup_inputs


def setup_inputs(seed=0):
    import zlib

    import numpy as np

    out = dict(_drawn_inputs(seed))
    spreads = {}
    factors = {'rwkv_w1': 6.418,
     'rwkv_w2': 6.699,
     'rwkv_lnx_w': 4.32,
     'rwkv_lnx_b': 3.651,
     'conv_b_2': 4.972,
     'gate_i_bias_2': 8.0,
     'mlstm_norm_2': 3.249,
     'norm_ffn2_post_2': 3.633}
    for name, (base, spread) in spreads.items():
        noise = np.random.default_rng([zlib.crc32(name.encode()), seed]).standard_normal(out[name].shape)
        drawn = base * np.exp(spread * noise) if base else spread * noise
        out[name] = __import__('jax').numpy.asarray(drawn.astype(out[name].dtype))
    for name, factor in factors.items():
        out[name] = (out[name] * factor).astype(out[name].dtype)
    return out
```

```python
import numpy as np
from contextlib import ExitStack
import concourse.bass as bass
from concourse import mybir
from concourse.alu_op_type import AluOpType as ALU

F32 = mybir.dt.float32
F32R = mybir.dt.float32r
I32 = mybir.dt.int32
ACT = mybir.ActivationFunctionType
AX = mybir.AxisListType

P = 128
T = 512
D = 1024
KT = D // P
NB = T // P
HD = 64
PIECE = 2048
NEG = -1e30
SCORE_OUT = float(np.float32(-3.0e38))
SCORE_TAKEN = float(np.float32(-3.3e38))

TOPK = min(256, T // 4)
D_FF, D_FF2 = 4 * D, 2816
Q_COLS, KV_COLS, IQ_COLS, IK_COLS, IW_COLS = 1024, 256, 512, 64, 8
IDX_HEADS = 8

VECS = [("mixer_norm", 16), ("mlp_norm", 16), ("final_norm", 8), ("rwkv_mu", 48), ("rwkv_w0", 8),
        ("rwkv_a0", 8), ("rwkv_k_k", 8), ("rwkv_k_a", 8), ("rwkv_r_k", 8),
        ("rwkv_lnx_w", 8), ("rwkv_lnx_b", 8),
        ("norm_ffn1_pre_2", 8), ("norm_ffn1_post_2", 8), ("norm_mix_pre_2", 8), ("norm_mix_post_2", 8),
        ("norm_ffn2_pre_2", 8), ("norm_ffn2_post_2", 8), ("conv_w_2", 12), ("conv_b_2", 4),
        ("mlstm_norm_2", 4), ("gates", 1)]
VROWS = sum(n for _, n in VECS)
VAT = {}
_at = 0
for _name, _n in VECS:
    VAT[_name] = _at
    _at += _n


def constants():
    i = np.arange(P)
    k, m = i[:, None], i[None, :]
    c = {}
    c["ident"] = (k == m)
    c["ones"] = np.ones((P, P))
    c["swap"] = (k == (m // 64) * 64 + (m % 64 + 32) % 64)
    c["blockones"] = (k // 64 == m // 64)
    c["causal_bias"] = np.where(m <= k, 0.0, NEG)
    c["causal_score"] = np.where(m <= k, 0.0, SCORE_OUT)
    c["s_lt_t"] = (k < m)
    c["s_le_t"] = (k <= m)
    c["s_ge_t"] = (k >= m)
    for lv in range(7):
        b = 1 << lv
        c[f"level{lv}"] = (k // (2 * b) == m // (2 * b)) & (k // b % 2 == 1) & (m // b % 2 == 0)
    c["level0T"] = c["level0"].T
    c["head_col"] = np.concatenate([np.zeros((P, 16)), (i < 64)[:, None], (i >= 64)[:, None], np.zeros((P, 14))], 1)
    c["one_col"] = np.concatenate([np.zeros((P, 32)), np.ones((P, 1)), np.zeros((P, 31))], 1)
    hr = np.zeros((P, KT * P))
    for j in range(KT):
        hr[2 * j, j * P:j * P + 64] = 1
        hr[2 * j + 1, j * P + 64:(j + 1) * P] = 1
    c["head_row"] = hr
    rr = np.zeros((P, 4 * P))
    for h in range(4):
        rr[[h, 32 + h], h * P:(h + 1) * P] = 1
    c["row_pick"] = rr
    c["eps"] = np.concatenate([np.full((P, 1), 1e-6), np.full((P, 1), 64e-5)], 1)
    reset = np.ones((P, T))
    reset[:, ::P] = 0
    c["chunk_start"] = reset
    return {n: np.asarray(a, np.float32) for n, a in c.items()}


def rope_table():
    inv = (1.0 / (np.float32(10000.0) ** (np.arange(0, HD, 2, dtype=np.float32) / np.float32(HD)))).astype(np.float32)
    ang = np.arange(T, dtype=np.float32)[:, None] * inv[None, :]
    cos, sin = np.cos(ang).astype(np.float32).T, np.sin(ang).astype(np.float32).T
    return np.concatenate([np.concatenate([cos] * 4, 0), np.concatenate([-sin, sin] * 2, 0)], 1)


_CONST = constants()
GROUPS = {"core": ["ident", "ones", "eps", "one_col"],
          "dsa": ["swap", "causal_bias", "causal_score"],
          "rwkv": ["blockones", "s_lt_t", "s_le_t"] + [f"level{lv}" for lv in range(7)]
                  + ["level0T", "head_col", "head_row", "chunk_start"],
          "mix": ["s_le_t", "s_ge_t", "row_pick"]}


def const_group(g):
    return np.concatenate([_CONST[n] for n in GROUPS[g]], 1)


class Engine:

    def __init__(self, engine, sem, step=1):
        self.e, self.sem, self.step, self.n = engine, sem, step, 0

    def done(self, ins):
        self.n += self.step
        ins.then_inc(self.sem, self.step)
        return (self.sem, self.n)

    def wait(self, *counts):
        for c in counts:
            if c is not None:
                self.e.wait_ge(c[0], c[1])


class Turns:

    def __init__(self, bufs):
        self.bufs, self.at, self.read, self.kept = bufs, -1, [None] * len(bufs), set()

    def next(self, keep=False):
        self.at = (self.at + 1) % len(self.bufs)
        while self.at in self.kept:
            self.at = (self.at + 1) % len(self.bufs)
        if keep:
            self.kept.add(self.at)
        return self.at

    def give_back(self, i):
        self.kept.discard(i)

    def __getitem__(self, i):
        return self.bufs[i]


class Program:
    def __init__(self, nc, io):
        self.nc, self.io = nc, io
        self.ctx = ExitStack()

    def sb(self, name, shape, dt=F32, ctx=None, **kw):
        return (ctx or self.ctx).enter_context(self.nc.sbuf_tensor(name, shape, dt, **kw))

    def build(self):
        with self.ctx:
            self.setup()
            stages = [("dsa", self.dsa), ("mlp0", lambda: self.mlp(0)), ("rwkv", self.rwkv),
                      ("mlp1", lambda: self.mlp(1)), ("final", self.final_norm),
                      ("ffn1", lambda: self.ffn("1")), ("mix", self.mixer), ("ffn2", lambda: self.ffn("2"))]
            names = [n for n, _ in stages] + [None]
            self.then = names[0]
            self.load_x()
            for at, (_, stage) in enumerate(stages):
                self.then = names[at + 1]
                stage()
            self.store()
            self.op_ctx.close()

    def setup(self):
        nc, ctx = self.nc, self.ctx

        def line(engine, name, step=1):
            return Engine(engine, ctx.enter_context(nc.semaphore(name)), step)

        self.S = Engine(nc.sync, None)
        self.V = line(nc.vector, "vector_done")
        self.A = line(nc.scalar, "scalar_done")
        self.G = line(nc.gpsimd, "gpsimd_done")
        self.M = line(nc.tensor, "tensor_done")
        self.load_small = line(None, "small_loaded", 16)
        self.x_loaded = [line(None, f"x_loaded{i}", 16) for i in range(2)]
        self.stored = line(None, "stored", 16)

        self.X = self.sb("x_t", [P, KT, T])
        self.consts = {}
        self.load_constants("core")
        self.vecs = self.sb("vecs", [P, VROWS])
        self.stat = self.sb("stat", [P, 6, NB])
        self.diag = self.sb("diag", [P, NB, P])
        self.ssq = self.sb("ssq", [P, T])
        self.ssq2 = self.sb("ssq_gained", [P, T])
        self.gain2 = self.sb("final_and_pre_gain", [P, KT])
        self.scratch = Turns([self.sb(f"scratch{i}", [P, T]) for i in range(6)])
        self.raw = [self.sb(f"raw{i}", [P, PIECE]) for i in range(3)]
        self.raw_in = [line(None, f"raw_loaded{i}", 16) for i in range(3)]
        psum = [ctx.enter_context(nc.psum_tensor(f"bank{i}", [P, T], F32)) for i in range(8)]
        self.bank = Turns(psum)
        self.x_ready = [None] * KT
        self.h_ready = [None] * KT
        self.h_used = [None] * KT
        self.rb = self.diag[:, :, :].rearrange("p b t -> p (b t)")
        self.scopes = 0
        self.pieces, self.loaded, self.split_at, self.at = [], 0, 0, 0
        self.w_landed, self.w_cut, self.w_used, self.raw_read = {}, {}, {}, {}
        self.open_operands()

    def open_operands(self):
        self.scopes += 1
        self.op_ctx = ExitStack()
        n = self.scopes
        self.Hh = self.sb(f"h_hi{n}", [P, KT, T], F32R, self.op_ctx)
        self.Hl = self.sb(f"h_lo{n}", [P, KT, T], F32R, self.op_ctx)
        self.Wh = [self.sb(f"w_hi{n}_{i}", [P, PIECE], F32R, self.op_ctx) for i in range(2)]
        self.Wl = [self.sb(f"w_lo{n}_{i}", [P, PIECE], F32R, self.op_ctx) for i in range(2)]

    def load_constants(self, group, ctx=None):
        cols = sum(_CONST[n].shape[1] for n in GROUPS[group])
        t = self.sb(f"const_{group}", [P, cols], F32, ctx)
        mark = self.load_small.done(self.A.e.dma_start(t[:, :], self.io[f"const_{group}"]))
        at = 0
        for n in GROUPS[group]:
            w = _CONST[n].shape[1]
            self.consts[n] = t[:, at:at + w]
            at += w
        return mark

    def c(self, name, rows=P):
        return self.consts[name][0:rows, :]

    def vec(self, name, j):
        return self.vecs[:, VAT[name] + j:VAT[name] + j + 1]

    def plan_weights(self, start):
        io, plan = self.io, self.pieces

        def tiles(name, w, r0, nk, c0, nc_, split=True):
            src = w[r0:r0 + nk * P, c0:c0 + nc_].rearrange("(k p) n -> p k n", p=P)
            plan.append((name, [(slice(0, P), 0, nk, nc_, nc_, src)], split))

        def linear(name, w, rows, c0, cols):
            for cg in range(0, cols, 512):
                n = min(512, cols - cg)
                for r in range(0, rows, 512):
                    tiles(name, w, r, min(4, (rows - r) // P), c0 + cg, n)

        w_in = io["dsa_w_in"][0]
        o2, o3 = Q_COLS + 2 * KV_COLS, Q_COLS + 2 * KV_COLS + IQ_COLS
        ki = w_in[:, o3:o3 + 64].rearrange("(k p) n -> p k n", p=P)
        kiw = w_in[:, o3:o3 + 72].rearrange("(k p) n -> p k n", p=P)
        plan.append(("ki", [(slice(0, P), 0, KT, 64, 136, ki), (slice(0, P), 64, KT, 72, 136, kiw)], True))
        linear("qi", w_in, D, o2, IQ_COLS)
        linear("q", w_in, D, 0, Q_COLS)
        linear("kv", w_in, D, Q_COLS, 2 * KV_COLS)
        w_o = io["dsa_w_o"][0]
        for cg in range(2):
            for kg in range(2):
                parts = []
                for u in range(2):
                    rows = w_o[(8 * kg + 4 * u) * HD:(8 * kg + 4 * u + 4) * HD, cg * 512:cg * 512 + 512]
                    parts.append((slice(64 * u, 64 * u + 64), 0, 4, 512, 512, rows.rearrange("(i p) n -> p i n", p=HD)))
                plan.append(("wo", parts, True))

        def mlp(l):
            for g in range(0, D_FF, 2048):
                linear("up", io["mlp_w_up"][l], D, g, 2048)
                linear("down", io["mlp_w_down"][l][g:g + 2048, :], 2048, 0, D)
        mlp(0)
        plan_rwkv = [("wa1", ["rwkv_w1", "rwkv_a1"]), ("g1", ["rwkv_g1"])]
        for name, ws in plan_rwkv:
            n = sum(io[w].shape[2] for w in ws)
            parts, at = [], 0
            for w in ws:
                k = io[w].shape[2]
                parts.append((slice(0, P), at, KT, k, n, io[w][0].rearrange("(k p) n -> p k n", p=P)))
                at += k
            plan.append((name, parts, False))
        for name, c in (("v", 2), ("r", 0), ("k", 1)):
            linear(name, io["rwkv_w_rkv"][0][c], D, 0, D)
        g2 = io["rwkv_g2"][0]
        plan.append(("g2", [(slice(0, P), 0, 1, D, D, g2[0:P, :]), (slice(0, 32), D, 1, D, D, g2[P:160, :])], False))
        linear("rwkv_wo", io["rwkv_w_o"][0], D, 0, D)
        mlp(1)

        def ffn(tag):
            w1, w2 = io[f"w_ffn{tag}_in_2"][0], io[f"w_ffn{tag}_out_2"][0]
            for g0, gn in ((0, 12), (12, 10)):
                for f in range(g0, g0 + gn, 2):
                    for r in range(0, D, 512):
                        parts = [(slice(0, P), u * 256, 4, 256, 512,
                                  w1[r:r + 512, u * D_FF2 + f * P:u * D_FF2 + f * P + 256]
                                  .rearrange("(k p) n -> p k n", p=P)) for u in range(2)]
                        plan.append(("gu", parts, True))
                linear("ffn_out", w2[g0 * P:(g0 + gn) * P, :], gn * P, 0, D)
        ffn("1")
        wm = io["w_mix_in_2"][0]
        plan.append(("gates", [(slice(0, P), 1024, KT, 16, 16, wm[:, 3072:3088].rearrange("(k p) n -> p k n", p=P))], "gates"))
        linear("mq", wm, D, 1536, 512)
        linear("mv", wm, D, 2048, 512)
        linear("cg", wm, D, 512, 512)
        linear("hc", wm, D, 1024, 512)
        linear("bg", wm, D, 0, 512)
        linear("mo", wm, D, 2560, 512)
        linear("mix_out", io["w_mix_out_2"][0], D, 0, D)
        ffn("2")
        for _ in range(start):
            self.load_piece()

    def load_piece(self):
        i = self.loaded
        if i >= len(self.pieces) or (i >= 3 and i - 3 not in self.raw_read):
            return
        self.loaded += 1
        slot = i % 3
        S = self.S
        if i >= 3:
            S.wait(*self.raw_read[i - 3])
        for rows, at, nk, n, width, src in self.pieces[i][1]:
            if nk == 1:
                dst = self.raw[slot][rows, at:at + n]
            else:
                base = at // width * width
                dst = (self.raw[slot][rows, base:base + nk * width]
                       .rearrange("p (k w) -> p k w", k=nk)[:, :, at - base:at - base + n])
            mark = self.raw_in[slot].done(S.e.dma_start(dst, src))
        self.w_landed[i] = mark

    def split_piece(self):
        i = self.split_at
        if i >= len(self.pieces) or i > self.at + 1:
            return
        A, G, V = self.A, self.G, self.V
        name, parts, split = self.pieces[i]
        if self.hold_split and split and name != "k":
            return
        self.split_at += 1
        landed = self.w_landed[i]
        slot, w = i % 3, i % 2
        if split is False:
            return
        n = sum(nk * n for _, _, nk, n, _, _ in parts)
        if name == "wo":
            n //= 2
        raw = self.raw[slot]
        if split == "gates":
            z = raw[:, 0:1024].rearrange("p (k w) -> p k w", k=KT)
            src = raw[:, 1024:1024 + 16 * KT].rearrange("p (k w) -> p k w", k=KT)
            G.wait(landed, *self.raw_read.get(i - 3, ()))
            zero = G.done(G.e.memset(raw[:, 0:1024], 0.0))
            G.wait(zero)
            for q in range(4):
                m = G.done(G.e.tensor_copy(z[:, :, 32 * q:32 * q + 4], src[:, :, 4 * q:4 * q + 4]))
            A.wait(m)
            n = 1024
        used = self.w_used.get(i - 2)
        A.wait(landed, used)
        G.wait(landed, used)
        if name == "q":
            for k in range(4):
                r_, h_, l_ = (t[:, 512 * k:512 * k + 512] for t in (raw, self.Wh[w], self.Wl[w]))
                r_ = r_.rearrange("p (u i c) -> p u i c", u=2, i=4)
                h_, l_ = (t.rearrange("p (i u c) -> p u i c", u=2, i=4) for t in (h_, l_))
                hi = A.done(A.e.activation(h_, r_, ACT.Copy))
                G.wait(hi)
                lo = G.done(G.e.tensor_tensor(l_, r_, h_, ALU.subtract))
        else:
            hi = A.done(A.e.activation(self.Wh[w][:, 0:n], raw[:, 0:n], ACT.Copy))
            G.wait(hi)
            lo = G.done(G.e.tensor_tensor(self.Wl[w][:, 0:n], raw[:, 0:n], self.Wh[w][:, 0:n], ALU.subtract))
        self.raw_read[i] = (hi, lo)
        self.w_cut[i] = (hi, lo)
        self.load_piece()

    hold_split = False
    ssq_used = ssq_ready = ssq2_ready = stat_used = rb_used = None

    def piece(self, name, wait=True):
        i = self.at
        assert self.pieces[i][0] == name, (self.pieces[i][0], name)
        while self.split_at <= min(i + 1, len(self.pieces) - 1):
            was = self.split_at
            self.split_piece()
            if was == self.split_at:
                break
        self.at += 1
        if self.pieces[i][2] is False:
            self.M.wait(self.w_landed[i])
        else:
            self.M.wait(*self.w_cut[i])
        return i, self.Wh[i % 2], self.Wl[i % 2]

    def end_piece(self, i, mark):
        self.w_used[i] = mark
        if self.pieces[i][2] is False:
            self.raw_read[i] = (mark,)
            self.load_piece()
            self.load_piece()

    def mm3(self, out, wh, wl, xh, xl, first, last):
        mm = self.M.e.matmul
        mm(out, wl, xh, start=first, stop=False)
        mm(out, wh, xl, start=False, stop=False)
        return mm(out, wh, xh, start=False, stop=last)

    def linear(self, name, kt_all, groups, xh, xl, evacuate, xwait, xread=None, each_piece=None, each_strip=None,
               cols=512):
        M = self.M
        for cg in range(groups):
            nt = cols // P
            banks = [self.bank.next(keep=True) for _ in range(nt)]
            M.wait(*(self.bank.read[x] for x in banks))
            for k0 in range(0, kt_all, 4):
                nk = min(4, kt_all - k0)
                i, wh, wl = self.piece(name)
                for o in range(nt):
                    for k in range(nk):
                        kt = k0 + k
                        if o == 0 and cg == 0:
                            M.wait(xwait(kt))
                        s = slice(k * cols + o * P, k * cols + o * P + P)
                        mm = self.mm3(self.bank[banks[o]][:, :], wh[:, s], wl[:, s], xh[:, kt, :], xl[:, kt, :],
                                      kt == 0, kt == kt_all - 1)
                    if kt == kt_all - 1:
                        mark = M.done(mm)
                        evacuate(cg * 4 + o, banks[o], mark)
                    elif o == nt - 1:
                        mark = M.done(mm)
                    if each_strip:
                        each_strip()
                self.end_piece(i, mark)
                if xread is not None and cg == groups - 1:
                    xread(k0, nk, mark)
                if each_piece:
                    each_piece()

    def load_x(self):
        A, V, M, nc = self.A, self.V, self.M, self.nc
        x = self.io["x"][0]
        with ExitStack() as s:
            xin = self.sb("x_in", [P, NB, D], F32, s)
            x_in = []
            for half in range(2):
                w = slice(half * 512, half * 512 + 512)
                x_in.append(self.x_loaded[half].done(self.S.e.dma_start(xin[:, :, w], x[:, w].rearrange("(b p) d -> p b d", p=P))))
                if half == 0:
                    self.plan_weights(1)
            for _ in range(2):
                self.load_piece()
            vin = self.sb("vecs_in", [P, 2, P], F32, s)
            m2 = self.load_small.done(A.e.dma_start(vin[:, 0, :], self.io["vecs"][0:P, :]))
            m2 = self.load_small.done(A.e.dma_start(vin[0:VROWS - P, 1, :], self.io["vecs"][P:VROWS, :]))
            M.wait(m2)
            ident = self.c("ident")
            b = self.bank.next()
            M.wait(self.bank.read[b])
            M.e.transpose(self.bank[b][:, 0:P], vin[:, 0, :], ident)
            mk = M.done(M.e.transpose(self.bank[b][:, P:VROWS], vin[0:VROWS - P, 1, :],
                                     ident[0:VROWS - P, 0:VROWS - P]))
            V.wait(mk)
            self.vecs_ready = V.done(V.e.tensor_copy(self.vecs[:, :], self.bank[b][:, 0:VROWS]))
            self.bank.read[b] = self.vecs_ready
            V.wait(self.vecs_ready)
            n, f = VAT["norm_ffn1_pre_2"], VAT["final_norm"]
            self.gain2_ready = V.done(V.e.tensor_tensor(self.gain2[:, :], self.vecs[:, n:n + KT], self.vecs[:, f:f + KT],
                                                       ALU.mult))
            A.wait(self.vecs_ready)
            self.bank.give_back(b)
            self.split_piece()
            for j in range(KT):
                b = self.bank.next()
                M.wait(self.bank.read[b])
                M.wait(x_in[j // 4])
                for t in range(NB):
                    mm = M.e.transpose(self.bank[b][:, t * P:(t + 1) * P], xin[:, t, j * P:(j + 1) * P], ident)
                mk = M.done(mm)
                V.wait(mk)
                self.x_ready[j] = V.done(V.e.tensor_copy(self.X[:, j, :], self.bank[b][:, :]))
                self.bank.read[b] = self.x_ready[j]
                self.bank.give_back(b)
                if j:
                    self.square_and_operand(j - 1)
            self.square_and_operand(KT - 1)
            self.all_wait(mk)

    def all_wait(self, *counts):
        for engine in (self.A, self.V, self.G, self.M, self.S):
            engine.wait(*counts)

    def store(self):
        V, M, A = self.V, self.M, self.A
        ident = self.c("ident")
        with ExitStack() as s:
            xo = self.sb("x_out", [P, NB, D], F32, s)
            for t in range(NB):
                for half in range(2):
                    b = self.bank.next()
                    M.wait(self.bank.read[b])
                    for jj in range(4):
                        j = half * 4 + jj
                        M.wait(self.x_ready[j])
                        mm = M.e.transpose(self.bank[b][:, jj * P:(jj + 1) * P], self.X[:, j, t * P:(t + 1) * P], ident)
                    mk = M.done(mm)
                    V.wait(mk)
                    cp = V.done(V.e.tensor_copy(xo[:, t, half * 512:half * 512 + 512], self.bank[b][:, :]))
                    self.bank.read[b] = cp
                    self.bank.give_back(b)
                self.S.wait(cp)
                out = self.stored.done(self.S.e.dma_start(self.io["out"][0][t * P:(t + 1) * P, :], xo[:, t, :]))
            self.S.wait(out)

    def add_square(self, j, src=None, mark=None, adder=None):
        src = self.X[:, j, :] if src is None else src
        mark = self.x_ready[j] if mark is None else mark
        self.ssq_ready = self.add_square_to(self.ssq, j, src, mark, self.ssq_ready, adder or self.V)
        if self.then == "final":
            self.ssq2_ready = self.add_square_to(self.ssq2, j, src, mark, self.ssq2_ready, adder or self.V,
                                                 self.vec("final_norm", j))

    def add_square_to(self, ssq, j, src, mark, ssq_ready, adder, gain=1.0):
        A = self.A
        if j == 0:
            A.wait(mark, self.ssq_used)
            return A.done(A.e.activation(ssq[:, :], src, ACT.Square, scale=gain))
        s = self.scratch.next()
        A.wait(self.scratch.read[s])
        A.wait(mark)
        sq = A.done(A.e.activation(self.scratch[s][:, :], src, ACT.Square, scale=gain))
        adder.wait(sq, ssq_ready)
        self.scratch.read[s] = adder.done(adder.e.tensor_tensor(ssq[:, :], ssq[:, :], self.scratch[s][:, :], ALU.add))
        return self.scratch.read[s]

    def gain(self, j):
        return {"dsa": lambda: self.vec("mixer_norm", j), "mlp0": lambda: self.vec("mlp_norm", j),
                "mlp1": lambda: self.vec("mlp_norm", 8 + j), "final": lambda: self.gain2[:, j:j + 1],
                "ffn1": lambda: self.vec("norm_ffn1_pre_2", j), "mix": lambda: self.vec("norm_mix_pre_2", j),
                "ffn2": lambda: self.vec("norm_ffn2_pre_2", j)}.get(self.then, lambda: None)()

    def square_and_operand(self, j):
        self.operand(j)
        self.add_square(j, adder=self.G)

    def operand(self, j):
        gain = self.gain(j)
        if gain is None:
            return
        A, V = self.A, self.V
        A.wait(self.x_ready[j], self.h_used[j])
        A.wait(self.gain2_ready if self.then == "final" else None)
        hi = A.done(A.e.activation(self.Hh[:, j, :], self.X[:, j, :], ACT.Copy, scale=gain))
        V.wait(hi)
        self.h_ready[j] = V.done(V.e.scalar_tensor_tensor(out=self.Hl[:, j, :], in0=self.X[:, j, :], scalar=gain,
                                                          in1=self.Hh[:, j, :], op0=ALU.mult, op1=ALU.subtract))

    def by_token(self, b, ssq, row, eps):
        A, V, M = self.A, self.V, self.M
        for t in range(NB):
            mm = M.e.matmul(self.bank[b][:, row * NB + t:row * NB + t + 1], ssq[:, t * P:(t + 1) * P],
                            self.c("ones")[:, 0:1], start=True, stop=True)
        return M.done(mm)

    def root(self, src, mark, row, eps):
        A, V = self.A, self.V
        st = self.stat[:, row, :]
        A.wait(mark, self.vecs_ready, self.stat_used)
        m = A.done(A.e.activation(st, src, ACT.Sqrt, bias=self.c("eps")[:, eps:eps + 1], scale=1.0 / D))
        V.wait(m)
        return m, V.done(V.e.reciprocal(st, st))

    def rstd_sums(self):
        M = self.M
        b = self.bank.next()
        M.wait(self.bank.read[b])
        M.wait(self.ssq_ready)
        mk = self.ssq_used = self.by_token(b, self.ssq, 0, 0)
        self.bank.read[b], m = self.root(self.bank[b][:, 0:NB], mk, 0, 0)
        return m

    def rstd_spread(self, row, mark):
        V, M = self.V, self.M
        V.wait(mark, self.rb_used)
        m = V.done(V.e.tensor_tensor(self.diag[:, :, :],
                                    self.c("ident").unsqueeze(1).to_broadcast([P, NB, P]),
                                    self.stat[:, row, :].unsqueeze(2).to_broadcast([P, NB, P]), ALU.mult))
        b = self.bank.next()
        M.wait(self.bank.read[b])
        M.wait(m)
        mk = self.rb_used = M.done(M.e.matmul(self.bank[b][:, :], self.c("ones"), self.diag[:, :, :], start=True, stop=True))
        return b, mk

    def rstd(self):
        return self.rstd_spread(0, self.rstd_sums())

    def keep_rstd(self, b, mark):
        V = self.V
        V.wait(mark)
        self.rb_ready = V.done(V.e.tensor_copy(self.rb, self.bank[b][:, :]))
        self.bank.read[b] = self.rb_ready

    def rstd_between(self):
        yield
        m = self.rstd_sums()
        yield
        yield
        self.keep_rstd(*self.rstd_spread(0, m))

    def split_h(self, j, s, mark):
        A, V = self.A, self.V
        src = self.scratch[s][:, :]
        A.wait(mark, self.h_used[j])
        hi = A.done(A.e.activation(self.Hh[:, j, :], src, ACT.Copy))
        V.wait(hi, self.h_used[j])
        lo = V.done(V.e.tensor_tensor(self.Hl[:, j, :], src, self.Hh[:, j, :], ALU.subtract))
        self.scratch.read[s] = lo
        self.h_ready[j] = lo

    def h_wait(self, kt):
        return self.h_ready[kt]

    def h_read(self, k0, nk, mark):
        for k in range(k0, k0 + nk):
            self.h_used[k] = mark

    def add_to_x(self, square):
        def evacuate(o, b, mark):
            V = self.V
            V.wait(mark, self.x_ready[o])
            self.x_ready[o] = V.done(V.e.tensor_tensor(self.X[:, o, :], self.bank[b][:, :], self.X[:, o, :], ALU.add))
            self.bank.read[b] = self.x_ready[o]
            self.bank.give_back(b)
            if square:
                self.add_square(o)
                if o >= 4:
                    self.operand(o - 4)
                if o == KT - 1:
                    for j in range(4, KT):
                        self.operand(j)
        return evacuate

    def rope(self, b, mark, out):
        A, V, M = self.A, self.V, self.M
        s, s2 = self.scratch.next(), self.scratch.next()
        A.wait(self.scratch.read[s])
        V.wait(self.scratch.read[s2])
        A.wait(mark)
        G = self.G
        raw = A.done(A.e.activation(self.scratch[s][:, :], self.bank[b][:, :], ACT.Copy))
        self.bank.read[b] = raw
        self.bank.give_back(b)
        b2 = self.bank.next()
        M.wait(self.bank.read[b2])
        M.wait(raw, self.rope_loaded)
        sw = M.done(M.e.matmul(self.bank[b2][:, :], self.c("swap"), self.scratch[s][:, :], start=True, stop=True))
        G.wait(raw, self.rope_loaded)
        m1 = G.done(G.e.tensor_tensor(out, self.scratch[s][:, :], self.rope_t[:, 0:T], ALU.mult))
        V.wait(sw)
        m2 = V.done(V.e.tensor_tensor(self.scratch[s2][:, :], self.bank[b2][:, :], self.rope_t[:, T:2 * T], ALU.mult))
        self.bank.read[b2] = m2
        self.bank.give_back(b2)
        G.wait(m2, m1)
        m3 = G.done(G.e.tensor_tensor(out, out, self.scratch[s2][:, :], ALU.add))
        self.scratch.read[s] = m3
        self.scratch.read[s2] = m3
        return m3

    def dsa(self):
        A, V, M, G = self.A, self.V, self.M, self.G
        with ExitStack() as s:
            sb = lambda n, sh, dt=F32: self.sb(n, sh, dt, s)
            self.rope_t = sb("rope", [P, 2 * T])
            Q, K, Vt = sb("q_t", [P, KT, T]), sb("k_t", [P, 2, T]), sb("v", [P, NB, KV_COLS])
            QI, KI, WI = sb("qi_t", [P, 4, T]), sb("ki_t", [P, T]), sb("wi", [P, NB, IW_COLS])
            self.load_constants("dsa", s)
            width = [P * (b + 1) for b in range(NB)]
            SC = [sb(f"score{b}", [P, width[b]]) for b in range(NB)]
            BI = [self.c("causal_bias")] + [sb(f"bias{b}", [P, width[b]]) for b in range(1, NB)]
            top = [sb(f"top{b}", [P, 8]) for b in range(NB)]
            self.rope_loaded = self.load_small.done(A.e.dma_start(self.rope_t[:, :], self.io["rope"]))
            i, wh, wl = self.piece("ki")
            kb = self.bank.next()
            M.wait(self.bank.read[kb])
            for kt in range(KT):
                M.wait(self.h_ready[kt])
                c = kt * 136
                mm = self.mm3(self.bank[kb][:, :], wh[:, c:c + P], wl[:, c:c + P], self.Hh[:, kt, :], self.Hl[:, kt, :],
                              kt == 0, kt == KT - 1)
            ki_m = M.done(mm)
            rstd_m = self.rstd_sums()
            wb = self.bank.next()
            M.wait(self.bank.read[wb])
            for t in range(NB):
                for kt in range(KT):
                    c, ts = kt * 136 + P, slice(t * P, t * P + P)
                    mm = self.mm3(self.bank[wb][:, 8 * t:8 * t + 8], self.Hh[:, kt, ts], self.Hl[:, kt, ts],
                                  wh[:, c:c + 8], wl[:, c:c + 8], kt == 0, kt == KT - 1)
            wi_m = M.done(mm)
            self.end_piece(i, wi_m)
            rb, rb_m = self.rstd_spread(0, rstd_m)
            V.wait(rb_m, self.rope_loaded)
            rope3 = self.rope_t[:, :].rearrange("p (c t) -> p c t", c=2)
            self.rope_loaded = V.done(V.e.tensor_tensor(
                rope3, rope3, self.bank[rb][:, :].unsqueeze(1).to_broadcast([P, 2, T]), ALU.mult))
            self.bank.read[rb] = self.rope_loaded
            V.wait(wi_m, rstd_m)
            wi = V.done(V.e.scalar_tensor_tensor(
                out=WI[:, :, :], in0=self.bank[wb][:, 0:32].rearrange("p (b h) -> p b h", b=NB),
                scalar=IDX_HEADS ** -0.5 * HD ** -0.5, in1=self.stat[:, 0, :].unsqueeze(2).to_broadcast([P, NB, IDX_HEADS]),
                op0=ALU.mult, op1=ALU.mult))
            self.bank.read[wb] = wi
            self.bank.give_back(wb)
            ki = self.rope(kb, ki_m, KI[:, :])
            qi = {}

            def qi_out(o, b, mark):
                qi[o] = self.rope(b, mark, QI[:, o, :])
            self.linear("qi", KT, 1, self.Hh, self.Hl, qi_out, self.h_wait)

            scores = []

            def score_steps():
                acc = [None] * NB
                for h in range(IDX_HEADS):
                    p0 = HD * (h % 2)
                    for b in range(1, NB):
                        n = width[b]
                        k = self.bank.next()
                        M.wait(self.bank.read[k])
                        M.wait(qi[h // 2], ki)
                        mk = M.done(M.e.matmul(self.bank[k][:, 0:n], QI[p0:p0 + HD, h // 2, b * P:(b + 1) * P],
                                              KI[p0:p0 + HD, 0:n], start=True, stop=True))
                        r = self.scratch.next()
                        A.wait(self.scratch.read[r])
                        A.wait(mk)
                        rl = A.done(A.e.activation(self.scratch[r][:, 0:n], self.bank[k][:, 0:n], ACT.Relu))
                        self.bank.read[k] = rl
                        self.bank.give_back(k)
                        V.wait(rl, wi, acc[b])
                        w = WI[:, b, h:h + 1]
                        if h == 0:
                            acc[b] = V.done(V.e.tensor_scalar(SC[b][:, :], self.scratch[r][:, 0:n], w, None, ALU.mult))
                        else:
                            acc[b] = V.done(V.e.scalar_tensor_tensor(out=SC[b][:, :], in0=self.scratch[r][:, 0:n], scalar=w,
                                                                    in1=SC[b][:, :], op0=ALU.mult, op1=ALU.add))
                        self.scratch.read[r] = acc[b]
                    yield
                for b in range(1, NB):
                    V.wait(acc[b], self.rope_loaded)
                    d = SC[b][:, b * P:(b + 1) * P]
                    acc[b] = V.done(V.e.tensor_tensor(d, d, self.c("causal_score"), ALU.add))
                mx = [None] * NB
                for r in range(TOPK // 8):
                    for b in range(1, NB):
                        V.wait(acc[b])
                        mx[b] = V.done(V.e.max(top[b][:, :], SC[b][:, :]))
                    for b in range(1, NB):
                        V.wait(mx[b])
                        acc[b] = V.done(V.e.match_replace(SC[b][:, :], top[b][:, :], SC[b][:, :], SCORE_TAKEN))
                    yield
                for b in range(1, NB):
                    V.wait(acc[b])
                    scores.append(V.done(V.e.tensor_scalar(BI[b][:, :], SC[b][:, :], SCORE_TAKEN, NEG, ALU.not_equal, ALU.mult)))

            steps = score_steps()

            def some_steps(n=4):
                for _ in range(n):
                    next(steps, None)

            qm = {}
            for g in range(2):
                banks = [self.bank.next(keep=True) for _ in range(4)]
                M.wait(*(self.bank.read[x] for x in banks))
                for k0 in range(0, KT, 4):
                    i, wh, wl = self.piece("q")
                    for o in range(4):
                        for k in range(4):
                            c = k * 512 + o * P
                            mm = self.mm3(self.bank[banks[o]][:, :], wh[:, c:c + P], wl[:, c:c + P],
                                          self.Hh[:, k0 + k, :], self.Hl[:, k0 + k, :], k0 + k == 0, k0 + k == KT - 1)
                        if k0 + k == KT - 1:
                            mark = M.done(mm)
                            qm[4 * g + o] = self.rope(banks[o], mark, Q[:, 4 * g + o, :])
                        elif o == 3:
                            mark = M.done(mm)
                    self.end_piece(i, mark)
                    some_steps()
            kb = [self.bank.next(keep=True) for _ in range(2)]
            M.wait(*(self.bank.read[x] for x in kb))
            vb = [self.bank.next(keep=True) for _ in range(NB)]
            M.wait(*(self.bank.read[x] for x in vb))
            km, vm = [], []
            for k0 in range(0, KT, 4):
                i, wh, wl = self.piece("kv")
                for o in range(2):
                    for k in range(4):
                        c, kt = k * 512 + o * P, k0 + k
                        mm = self.mm3(self.bank[kb[o]][:, :], wh[:, c:c + P], wl[:, c:c + P],
                                      self.Hh[:, kt, :], self.Hl[:, kt, :], kt == 0, kt == KT - 1)
                    if k0:
                        km.append(M.done(mm))
                for t in range(NB):
                    for k in range(4):
                        c, kt, ts = k * 512 + KV_COLS, k0 + k, slice(t * P, t * P + P)
                        mm = self.mm3(self.bank[vb[t]][:, 0:KV_COLS], self.Hh[:, kt, ts], self.Hl[:, kt, ts],
                                      wh[:, c:c + KV_COLS], wl[:, c:c + KV_COLS], kt == 0, kt == KT - 1)
                    if k0:
                        vm.append(M.done(mm))
                mark = M.done(mm) if not k0 else vm[-1]
                self.end_piece(i, mark)
                some_steps()
            for k in range(KT):
                self.h_used[k] = vm[-1]
            kr = [self.rope(kb[o], km[o], K[:, o, :]) for o in range(2)]
            vr = []
            for t in range(NB):
                A.wait(vm[t], rstd_m)
                vr.append(A.done(A.e.activation(Vt[:, t, :], self.bank[vb[t]][:, 0:KV_COLS], ACT.Copy,
                                                scale=self.stat[:, 0, t:t + 1])))
                self.bank.read[vb[t]] = vr[-1]
                self.bank.give_back(vb[t])
            for _ in steps:
                pass

            small = sb("softmax", [P, 4, 4])
            Pm = Turns([sb(f"prob{i}", [P, T]) for i in range(3)])
            PT = Turns([sb(f"prob_t{i}", [P, T]) for i in range(2)])
            items = [(q, u, b) for q in range(KT) for u in range(2) for b in range(NB)]
            st, obank = {}, {}

            def logits(n):
                q, u, b = items[n]
                g, w, p0 = q // 4, width[b], HD * u
                k = self.bank.next()
                M.wait(self.bank.read[k])
                M.wait(qm[q], kr[g])
                mk = M.done(M.e.matmul(self.bank[k][:, 0:w], Q[p0:p0 + HD, q, b * P:(b + 1) * P], K[p0:p0 + HD, g, 0:w],
                                      start=True, stop=True))
                r = Pm.next()
                V.wait(Pm.read[r])
                sm = small[:, n % 4, :]
                V.wait(mk, *scores, self.rope_loaded)
                if n >= 4:
                    V.wait(st[n - 4][3])
                m = V.done(V.e.tensor_tensor_reduce(Pm[r][:, 0:w], self.bank[k][:, 0:w], BI[b][:, :], -HD ** -0.5, 3.0e38,
                                                   ALU.add, ALU.min, sm[:, 0:1]))
                self.bank.read[k] = m
                self.bank.give_back(k)
                A.wait(m)
                m = A.done(A.e.activation(Pm[r][:, 0:w], Pm[r][:, 0:w], ACT.Exp, bias=sm[:, 0:1], scale=-1.0,
                                         accum_out=sm[:, 1:2]))
                V.wait(m)
                m = V.done(V.e.reciprocal(sm[:, 2:3], sm[:, 1:2]))
                V.wait(m)
                m = V.done(V.e.tensor_scalar(Pm[r][:, 0:w], Pm[r][:, 0:w], sm[:, 2:3], None, ALU.mult))
                st[n] = (r, m, None, m)

            def transposes(n):
                q, u, b = items[n]
                r, m = st[n][0:2]
                k = self.bank.next()
                M.wait(self.bank.read[k])
                M.wait(m)
                for j in range(b + 1):
                    mm = M.e.transpose(self.bank[k][:, j * P:(j + 1) * P], Pm[r][:, j * P:(j + 1) * P], self.c("ident"))
                mk = M.done(mm)
                Pm.read[r] = mk
                x = A if n % 2 else V
                t = PT.next()
                x.wait(PT.read[t])
                x.wait(mk)
                w = width[b]
                if n % 2:
                    cp = A.done(A.e.activation(PT[t][:, 0:w], self.bank[k][:, 0:w], ACT.Copy))
                else:
                    cp = V.done(V.e.tensor_copy(PT[t][:, 0:w], self.bank[k][:, 0:w]))
                self.bank.read[k] = cp
                self.bank.give_back(k)
                st[n] = (t, cp, None, st[n][3])

            def values(n):
                q, u, b = items[n]
                t, cp = st[n][0:2]
                if u == 0 and b == 0:
                    obank[q] = o_sum[q % 2]
                    M.wait(o_read[q % 2])
                ob, kvh = obank[q], 2 * (q // 4) + u
                M.wait(cp, *vr)
                for j in range(b + 1):
                    mm = M.e.matmul(ob[HD * u:HD * u + HD, b * P:(b + 1) * P], Vt[:, j, kvh * HD:(kvh + 1) * HD],
                                    PT[t][:, j * P:(j + 1) * P], start=(j == 0), stop=(j == b))
                mk = M.done(mm)
                PT.read[t] = mk
                if u == 1 and b == NB - 1:
                    A.wait(mk, self.h_used[q])
                    hi = A.done(A.e.activation(self.Hh[:, q, :], ob, ACT.Copy))
                    V.wait(hi, self.h_used[q])
                    lo = V.done(V.e.tensor_tensor(self.Hl[:, q, :], ob, self.Hh[:, q, :], ALU.subtract))
                    o_read[q % 2] = lo
                    self.h_ready[q] = lo

            ob2 = [self.bank.next(keep=True) for _ in range(2)]
            M.wait(*(self.bank.read[x] for x in ob2))
            o_sum, o_read = [self.bank[b][:, :] for b in ob2], [None, None]
            N = len(items)
            for n in range(N + 4):
                if n < N:
                    logits(n)
                if 2 <= n < N + 2:
                    transposes(n - 2)
                if 3 <= n < N + 3:
                    values(n - 3)
            for b, m in zip(ob2, o_read):
                self.bank.read[b] = m
                self.bank.give_back(b)
            self.stat_used = vr[-1]
            values_taken = self.h_ready[KT - 1]
            self.linear("wo", KT, 2, self.Hh, self.Hl, self.add_to_x(True), lambda kt, at=list(self.h_ready): at[kt], self.h_read)
            self.all_wait(values_taken)

    def mlp(self, l):
        A, V, M, G = self.A, self.V, self.M, self.G
        with ExitStack() as s:
            NU = 16
            Uh, Ul = self.sb(f"u_hi{l}", [P, NU, T], F32R, s), self.sb(f"u_lo{l}", [P, NU, T], F32R, s)
            um, ur = [None] * NU, [None] * NU
            for g in range(D_FF // P // NU):
                def up_out(o, b, mark):
                    r = self.scratch.next()
                    V.wait(self.scratch.read[r])
                    V.wait(mark, self.rb_ready)
                    m = V.done(V.e.scalar_tensor_tensor(out=self.scratch[r][:, :], in0=self.bank[b][:, :], scalar=0.0,
                                                       in1=self.rb, op0=ALU.max, op1=ALU.mult))
                    self.bank.read[b] = m
                    self.bank.give_back(b)
                    self.square_split(self.scratch, r, m, Uh[:, o, :], Ul[:, o, :], um, ur, o)
                self.linear("up", KT, NU // 4, self.Hh, self.Hl, up_out, self.h_wait,
                            self.h_read if g == 1 else None, None, None if g else self.stepper(self.rstd_between()))

                def u_read(k0, nk, mark):
                    for k in range(k0, k0 + nk):
                        ur[k] = mark
                self.linear("down", NU, 2, Uh, Ul, self.add_to_x(g == 1), lambda k: um[k], u_read)
            self.all_wait(ur[NU - 1])

    def stepper(self, steps):
        return lambda: next(steps, None)

    def square_split(self, ring, r, m, hi_out, lo_out, um, ur, o):
        A, V = self.A, self.V
        A.wait(m)
        sq = A.done(A.e.activation(ring[r][:, :], ring[r][:, :], ACT.Square))
        A.wait(sq, ur[o])
        hi = A.done(A.e.activation(hi_out, ring[r][:, :], ACT.Copy))
        V.wait(hi, ur[o])
        lo = V.done(V.e.tensor_tensor(lo_out, ring[r][:, :], hi_out, ALU.subtract))
        ring.read[r] = lo
        um[o] = lo

    def rwkv(self):
        A, V, M, G = self.A, self.V, self.M, self.G
        right = ExitStack()
        sbr = lambda n, sh: self.sb(n, sh, F32, right, side="right")
        R, K, Vt = sbr("rw_r", [P, KT, T]), sbr("rw_k", [P, KT, T]), sbr("rw_v", [P, NB, D])
        TW, TA, SG = sbr("rw_tanh_w", [HD, T]), sbr("rw_a_in", [HD, T]), sbr("rw_sig_g", [P, 2, T])
        omu = sbr("rw_one_less_mu", [P, 48])
        rm, km, vm = [None] * KT, [None] * KT, []

        with ExitStack() as s:
            H = self.sb("rw_h", [P, KT, T + 1], F32, s)
            z = V.done(V.e.memset(H[:, :, 0:1], 0.0))
            mu0 = VAT["rwkv_mu"]
            om = V.done(V.e.tensor_scalar(omu[:, :], self.vecs[:, mu0:mu0 + 48], -1.0, 1.0, ALU.mult, ALU.add))
            b, mk = self.rstd()
            hm = []
            V.wait(mk)
            for j in range(KT):
                V.wait(self.x_ready[j])
                hm.append(V.done(V.e.scalar_tensor_tensor(out=H[:, j, 1:T + 1], in0=self.X[:, j, :],
                                                         scalar=self.vec("mixer_norm", 8 + j), in1=self.bank[b][:, :],
                                                         op0=ALU.mult, op1=ALU.mult)))
            self.bank.read[b] = hm[-1]
            self.bank.give_back(b)

            def shifted(c, j):
                r = self.scratch.next()
                V.wait(self.scratch.read[r])
                V.wait(hm[j], om, z)
                o = self.scratch[r][:, :]
                m = V.done(V.e.tensor_scalar(o, H[:, j, 1:T + 1], omu[:, 8 * c + j:8 * c + j + 1], None, ALU.mult))
                V.wait(m)
                return r, V.done(V.e.scalar_tensor_tensor(out=o, in0=H[:, j, 0:T], scalar=self.vec("rwkv_mu", 8 * c + j),
                                                         in1=o, op0=ALU.mult, op1=ALU.add))

            i, _, _ = self.piece("wa1")
            raw = self.raw[i % 3]
            for c, at, out, fn in ((3, 0, TW, ACT.Tanh), (4, HD, TA, ACT.Copy)):
                b = self.bank.next()
                M.wait(self.bank.read[b])
                for j in range(KT):
                    r, m = shifted(c, j)
                    M.wait(m)
                    mk = M.done(M.e.matmul(self.bank[b][0:HD, :], raw[:, 2 * HD * j + at:2 * HD * j + at + HD],
                                          self.scratch[r][:, :], start=(j == 0), stop=(j == KT - 1)))
                    self.scratch.read[r] = mk
                A.wait(mk)
                lora = A.done(A.e.activation(out[:, :], self.bank[b][0:HD, :], fn))
                self.bank.read[b] = lora
                self.bank.give_back(b)
            self.end_piece(i, mk)
            i, _, _ = self.piece("g1")
            raw = self.raw[i % 3]
            b, b2 = self.bank.next(keep=True), self.bank.next()
            M.wait(self.bank.read[b])
            M.wait(self.bank.read[b2])
            for j in range(KT):
                r, m = shifted(5, j)
                M.wait(m)
                M.e.matmul(self.bank[b][:, :], raw[:, 160 * j:160 * j + P], self.scratch[r][:, :],
                           start=(j == 0), stop=(j == KT - 1))
                mk = M.done(M.e.matmul(self.bank[b2][0:32, :], raw[:, 160 * j + P:160 * j + 160],
                                      self.scratch[r][:, :], start=(j == 0), stop=(j == KT - 1)))
                self.scratch.read[r] = mk
            self.end_piece(i, mk)
            A.wait(mk)
            A.done(A.e.activation(SG[:, 0, :], self.bank[b][:, :], ACT.Sigmoid))
            lora = A.done(A.e.activation(SG[0:32, 1, :], self.bank[b2][0:32, :], ACT.Sigmoid))
            self.bank.read[b] = lora
            self.bank.give_back(b)
            self.bank.read[b2] = lora
            self.bank.give_back(b2)

            def mix(c):
                for j in range(KT):
                    r, m = shifted(c, j)
                    self.split_h(j, r, m)

            mix(2)
            for g in range(2):
                banks = [self.bank.next(keep=True) for _ in range(NB)]
                M.wait(*(self.bank.read[x] for x in banks))
                for k0 in range(0, KT, 4):
                    i, wh, wl = self.piece("v")
                    for k in range(4):
                        for t in range(NB):
                            kt, ts, w = k0 + k, slice(t * P, t * P + P), slice(k * T, k * T + T)
                            if t == 0 and g == 0:
                                M.wait(self.h_ready[kt])
                            mm = self.mm3(self.bank[banks[t]][:, :], self.Hh[:, kt, ts], self.Hl[:, kt, ts],
                                          wh[:, w], wl[:, w], kt == 0, kt == KT - 1)
                    mk = M.done(mm)
                    self.end_piece(i, mk)
                    if g:
                        self.h_read(k0, 4, mk)
                for t in range(NB):
                    A.wait(mk)
                    vm.append(A.done(A.e.activation(Vt[:, t, g * T:g * T + T], self.bank[banks[t]][:, :], ACT.Copy)))
                    self.bank.read[banks[t]] = vm[-1]
                    self.bank.give_back(banks[t])

            def keep(dst, marks):
                def evacuate(o, b, mark):
                    A.wait(mark)
                    marks[o] = A.done(A.e.activation(dst[:, o, :], self.bank[b][:, :], ACT.Copy))
                    self.bank.read[b] = marks[o]
                    self.bank.give_back(b)
                return evacuate
            mix(0)
            self.linear("r", KT, 2, self.Hh, self.Hl, keep(R, rm), self.h_wait, self.h_read)
            mix(1)
            self.hold_split = True
            self.linear("k", KT, 2, self.Hh, self.Hl, keep(K, km), self.h_wait, self.h_read)
            self.all_wait(self.h_ready[KT - 1], self.h_used[KT - 1], km[KT - 1])
        self.op_ctx.close()

        with ExitStack() as s:
            sb = lambda n, sh: self.sb(n, sh, F32, s)
            W2 = sb("rw_w2a2", [HD, 2, D])
            self.load_constants("rwkv", s)
            self.load_small.done(A.e.dma_start(W2[:, 0, :], self.io["rwkv_w2"][0]))
            cin = self.load_small.done(A.e.dma_start(W2[:, 1, :], self.io["rwkv_a2"][0]))
            c = self.c
            mask = lambda n: c(n).bitcast(I32).unsqueeze(1).to_broadcast([P, NB, P])
            ident4 = c("ident").unsqueeze(1).to_broadcast([P, NB, P])
            AT = [sb(f"rw_at{i}", [P, T]) for i in range(2)]
            BT = [sb(f"rw_bt{i}", [P, T]) for i in range(1)]
            BK = [sb(f"rw_bk{i}", [P, 2, NB, P]) for i in range(2)]
            GM = [[sb(f"rw_g{i}{u}", [P, 3, NB, P]) for u in range(2)] for i in range(2)]
            LT = [sb(f"rw_lt{u}", [P, NB, P]) for u in range(2)]
            X_ = [sb(f"rw_x{u}", [P, NB, P]) for u in range(2)]
            XT = [[sb(f"rw_xt{i}{u}", [P, NB, P]) for u in range(2)] for i in range(2)]
            IT = [sb(f"rw_it{u}", [P, NB, P]) for u in range(2)]
            RN = sb("rw_kk_rstd", [16, T])
            ST = [sb(f"rw_state{i}", [P, P]) for i in range(2)]
            RH, SA = sb("rw_rhs", [P, P]), sb("rw_sa", [P, P])
            PM, PE_ = [sb(f"rw_mid{i}", [P, NB]) for i in range(2)], [sb(f"rw_end{i}", [P, NB]) for i in range(2)]
            omka = sb("rw_one_less_ka", [P, KT])
            small = [None]
            ka0 = VAT["rwkv_k_a"]
            V.wait(cin, self.vecs_ready)
            V.done(V.e.tensor_scalar(omka[:, :], self.vecs[:, ka0:ka0 + KT], -1.0, 1.0, ALU.mult, ALU.add))
            zero = []
            for i in range(2):
                for u in range(2):
                    zero.append(G.done(G.e.memset(GM[i][u][:, :, :, :], 0.0)))
            for u in range(2):
                zero.append(G.done(G.e.memset(LT[u][:, :, :], 0.0)))
            zero = zero[-1]

            b = self.bank.next(keep=True)
            M.wait(self.bank.read[b])
            for j in range(KT):
                r = self.scratch.next()
                A.wait(self.scratch.read[r])
                A.wait(km[j])
                m = A.done(A.e.activation(self.scratch[r][:, :], K[:, j, :], ACT.Square, scale=self.vec("rwkv_k_k", j)))
                M.wait(m, cin)
                mk = M.done(M.e.matmul(self.bank[b][0:16, :], c("head_col")[:, 16 - 2 * j:32 - 2 * j],
                                      self.scratch[r][:, :], start=(j == 0), stop=(j == KT - 1)))
                self.scratch.read[r] = mk
            V.wait(mk)
            m = V.done(V.e.tensor_scalar(RN[:, :], self.bank[b][0:16, :], 1e-24, None, ALU.max))
            self.bank.read[b] = m
            self.bank.give_back(b)
            A.wait(m)
            m = A.done(A.e.activation(RN[:, :], RN[:, :], ACT.Sqrt))
            V.wait(m)
            rn = V.done(V.e.reciprocal(RN[:, :], RN[:, :]))

            vb = self.bank.next(keep=True)
            M.wait(self.bank.read[vb])
            pair = {}

            def prepare(j):
                i = j % 2
                d = pair[j] = {}
                vec = self.vec
                states_end = pair[j - 2]["end"] if j >= 2 else ()
                before = pair[j - 1] if j else {}

                def sc(writer=V):
                    r = self.scratch.next()
                    writer.wait(self.scratch.read[r])
                    return r, self.scratch[r][:, :]
                k1, k2 = self.bank.next(), self.bank.next()
                M.wait(self.bank.read[k1])
                M.wait(self.bank.read[k2])
                M.wait(lora, cin)
                js = slice(j * P, j * P + P)
                M.e.matmul(self.bank[k1][:, :], W2[:, 0, js], TW[:, :], start=True, stop=True)
                mk = M.done(M.e.matmul(self.bank[k2][:, :], W2[:, 1, js], TA[:, :], start=True, stop=True))
                rw, w = sc(A)
                A.wait(mk)
                ws = A.done(A.e.activation(w, self.bank[k1][:, :], ACT.Sigmoid, bias=vec("rwkv_w0", j)))
                self.bank.read[k1] = ws
                self.bank.give_back(k1)
                ra, a = sc(A)
                am = A.done(A.e.activation(a, self.bank[k2][:, :], ACT.Sigmoid, bias=vec("rwkv_a0", j)))
                self.bank.read[k2] = am
                self.bank.give_back(k2)
                yield
                V.wait(ws)
                m = V.done(V.e.tensor_scalar(w, w, -float(np.exp(-0.5)), None, ALU.mult))
                V.wait(m)
                rc, cl = sc()
                m = V.done(V.e.tensor_tensor_scan(cl, c("chunk_start"), w, 0.0, ALU.mult, ALU.add))
                cl3 = cl.rearrange("p (c t) -> p c t", c=NB)
                mid = cl3[:, :, 63:64]
                A.wait(m, *states_end)
                d["pm"] = A.done(A.e.activation(PM[i][:, :].unsqueeze(2), mid, ACT.Exp))
                V.wait(m)
                rd, dc = sc()
                m = V.done(V.e.tensor_tensor(dc.rearrange("p (c t) -> p c t", c=NB), cl3,
                                            mid.to_broadcast([P, NB, P]), ALU.subtract))
                self.scratch.read[rc] = m
                V.wait(d["pm"])
                V.wait(m)
                m2 = V.done(V.e.tensor_tensor(w, dc, w, ALU.subtract))
                r1, e1 = sc(A)
                A.wait(m, m2)
                m1 = A.done(A.e.activation(e1, dc, ACT.Exp))
                m3 = A.done(A.e.activation(w, w, ACT.Exp))
                m2 = A.done(A.e.activation(dc, dc, ACT.Exp, scale=-1.0))
                e2, e3 = dc, w
                yield
                V.wait(m1, *states_end)
                V.wait(d["pm"])
                d["pe"] = V.done(V.e.tensor_tensor(PE_[i][:, 0:NB - 1].unsqueeze(2),
                                                  e1.rearrange("p (c t) -> p c t", c=NB)[:, 0:NB - 1, P - 1:P],
                                                  PM[i][:, 1:NB].unsqueeze(2), ALU.mult))
                rk, kk = sc()
                V.wait(km[j], am)
                kk_m = V.done(V.e.tensor_scalar(kk, K[:, j, :], vec("rwkv_k_k", j), None, ALU.mult))
                bt = BT[0]
                V.wait(before.get("bt_read"))
                t1 = V.done(V.e.tensor_scalar(bt[:, :], a, vec("rwkv_k_a", j), omka[:, j:j + 1], ALU.mult, ALU.add))
                V.wait(t1, kk_m)
                kf = V.done(V.e.tensor_tensor(K[:, j, :], K[:, j, :], bt[:, :], ALU.mult))
                kb = self.bank.next()
                M.wait(self.bank.read[kb])
                M.wait(rn)
                mk = M.done(M.e.matmul(self.bank[kb][:, :], c("head_row", 16)[:, js], RN[:, :], start=True, stop=True))
                V.wait(mk, kk_m)
                kn = V.done(V.e.tensor_tensor(kk, kk, self.bank[kb][:, :], ALU.mult))
                self.bank.read[kb] = kn
                self.bank.give_back(kb)
                V.wait(kf, rm[j], t1)
                bo = V.done(V.e.scalar_tensor_tensor(out=bt[:, :], in0=R[:, j, :], scalar=vec("rwkv_r_k", j),
                                                    in1=K[:, j, :], op0=ALU.mult, op1=ALU.mult))
                kb = self.bank.next()
                M.wait(self.bank.read[kb])
                M.wait(bo)
                mk = M.done(M.e.matmul(self.bank[kb][:, :], c("blockones"), bt[:, :], start=True, stop=True))
                V.wait(kn, m3, *states_end)
                d["at"] = V.done(V.e.scalar_tensor_tensor(out=AT[i][:, :], in0=kk, scalar=-1.0, in1=e3, op0=ALU.mult, op1=ALU.mult))
                V.wait(kn)
                m = V.done(V.e.tensor_tensor(kk, kk, a, ALU.mult))
                yield
                V.wait(m, m2, mk)
                d["bt"] = V.done(V.e.tensor_tensor(bt[:, :], kk, e2, ALU.mult))
                self.scratch.read[rk] = d["bt"]
                V.wait(mk, d["at"], m)
                bs = V.done(V.e.tensor_copy(a, self.bank[kb][:, :]))
                self.bank.read[kb] = bs
                self.bank.give_back(kb)
                kb = self.bank.next()
                M.wait(self.bank.read[kb])
                M.wait(vm[-1])
                for t in range(NB):
                    mm = M.e.transpose(self.bank[kb][:, t * P:t * P + P], Vt[:, t, js], c("ident"))
                mk = M.done(mm)
                V.wait(mk, bs)
                bv = V.done(V.e.tensor_tensor(a, a, self.bank[kb][:, :], ALU.mult))
                self.bank.read[kb] = bv
                self.bank.give_back(kb)
                V.wait(m2, kf)
                kt = V.done(V.e.tensor_tensor(K[:, j, :], K[:, j, :], e2, ALU.mult))
                V.wait(m1, rm[j], bo)
                rt = d["rt"] = V.done(V.e.tensor_tensor(R[:, j, :], R[:, j, :], e1, ALU.mult))
                self.scratch.read[rw] = d["at"]
                self.scratch.read[rd] = kt
                self.scratch.read[r1] = rt
                yield
                for x, (src, mark) in enumerate(((bt, d["bt"]), (K[:, j, :], kt))):
                    kb = self.bank.next()
                    M.wait(self.bank.read[kb])
                    M.wait(mark)
                    for t in range(NB):
                        mm = M.e.transpose(self.bank[kb][:, t * P:t * P + P], src[:, t * P:t * P + P], c("ident"))
                    mk = M.done(mm)
                    A.wait(mk, *states_end)
                    d["bk"] = A.done(A.e.activation(BK[i][:, x, :, :], self.bank[kb][:, :], ACT.Copy))
                    self.bank.read[kb] = d["bk"]
                    self.bank.give_back(kb)
                yield
                d["g"] = [None] * 2
                lt = [None] * 2
                for u in range(2):
                    hs = slice(HD * u, HD * u + HD)
                    for n, (left, right_, mk_, msk) in enumerate((
                            (bt, AT[i], None, "s_lt_t"), (bt, R[:, j, :], None, "s_le_t"),
                            (K[:, j, :], AT[i], None, "s_lt_t"), (K[:, j, :], R[:, j, :], None, "s_le_t"))):
                        kb = self.bank.next()
                        M.wait(self.bank.read[kb])
                        M.wait(d["bt"], d["at"], kt, rt)
                        for t in range(NB):
                            ts = slice(t * P, t * P + P)
                            mm = M.e.matmul(self.bank[kb][:, ts], left[hs, ts], right_[hs, ts], start=True, stop=True)
                        mk = M.done(mm)
                        V.wait(mk, zero, cin)
                        dst = LT[u] if n == 0 else GM[i][u][:, n - 1, :, :]
                        if n:
                            V.wait(*states_end)
                        else:
                            V.wait(before["lt_read"][u] if j else None)
                        m = V.done(V.e.copy_predicated(dst if n else dst[:, :, :], mask(msk),
                                                      self.bank[kb][:, :].rearrange("p (c t) -> p c t", c=NB)))
                        self.bank.read[kb] = m
                        self.bank.give_back(kb)
                        if n == 0:
                            lt[u] = m
                        d["g"][u] = m
                        d["bt_read"] = mk
                        yield
                V.wait(mk, bv)
                d["bv"] = V.done(V.e.tensor_copy(K[:, j, :], a))
                self.scratch.read[ra] = d["bv"]
                x, xt, it = [None] * 2, [None] * 2, [None] * 2
                for u in range(2):
                    G.wait(before.get("x_read"), self.vecs_ready)
                    x[u] = G.done(G.e.tensor_copy(X_[u][:, :, :], ident4))
                    G.wait(*states_end)
                    xt[u] = G.done(G.e.tensor_copy(XT[i][u][:, :, :], ident4))
                    it[u] = G.done(G.e.tensor_copy(IT[u][:, :, :], ident4))
                    V.wait(lt[u], xt[u])
                    xt[u] = V.done(V.e.copy_predicated(XT[i][u][:, :, :], mask("level0T"), LT[u][:, :, :]))
                d["lt_read"] = [None] * 2
                for lv in range(7):
                    its = [None] * 2
                    for u in range(2):
                        kb = self.bank.next()
                        M.wait(self.bank.read[kb])
                        M.wait(lt[u], x[u])
                        for t in range(NB):
                            rhs = c("ident") if lv == 0 else X_[u][:, t, :]
                            mm = M.e.matmul(self.bank[kb][:, t * P:t * P + P], LT[u][:, t, :], rhs, start=True, stop=True)
                        mk = M.done(mm)
                        dst, was = (X_, x) if lv == 0 else (IT, it)
                        V.wait(mk, was[u])
                        m = V.done(V.e.copy_predicated(dst[u][:, :, :], mask(f"level{lv}"),
                                                      self.bank[kb][:, :].rearrange("p (c t) -> p c t", c=NB)))
                        self.bank.read[kb] = m
                        self.bank.give_back(kb)
                        if lv == 0:
                            x[u] = m
                        its[u] = m
                        d["lt_read"][u] = mk
                        yield
                    if lv == 0:
                        continue
                    for u in range(2):
                        M.wait(its[u], xt[u], x[u])
                        ks = []
                        for q in range(2 if lv < 6 else 1):
                            kb = self.bank.next()
                            M.wait(self.bank.read[kb])
                            for t in range(NB):
                                left, rhs = (IT[u], XT[i][u]) if q == 0 else (XT[i][u], IT[u])
                                mm = M.e.matmul(self.bank[kb][:, t * P:t * P + P], left[:, t, :], rhs[:, t, :],
                                                start=True, stop=True)
                            ks.append(kb)
                        mk = M.done(mm)
                        A.wait(mk)
                        xt[u] = A.done(A.e.activation(XT[i][u][:, :, :], self.bank[ks[0]][:, :], ACT.Copy))
                        self.bank.read[ks[0]] = xt[u]
                        self.bank.give_back(ks[0])
                        if lv < 6:
                            x[u] = A.done(A.e.activation(X_[u][:, :, :], self.bank[ks[1]][:, :], ACT.Copy))
                            self.bank.read[ks[1]] = x[u]
                            self.bank.give_back(ks[1])
                            G.wait(mk)
                            it[u] = G.done(G.e.tensor_copy(IT[u][:, :, :], ident4))
                        yield
                d["x_read"] = mk
                d["xt"] = xt

            def states(j):
                i = j % 2
                d = pair[j]
                st = None
                for ch in range(NB):
                    cs = slice(ch * P, ch * P + P)
                    S0, S1 = ST[ch % 2], ST[(ch + 1) % 2]
                    kb = self.bank.next()
                    M.wait(self.bank.read[kb])
                    M.wait(st, d["g"][1], d["at"], vm[-1])
                    if ch:
                        M.e.matmul(self.bank[kb][:, 0:P], AT[i][:, cs], S0[:, :], start=True, stop=False)
                    for u in range(2):
                        hs = slice(HD * u, HD * u + HD)
                        v = Vt[:, ch, j * P + HD * u:j * P + HD * u + HD]
                        mm = M.e.matmul(self.bank[kb][:, hs], GM[i][u][:, 1, ch, :], v, start=(ch == 0),
                                        stop=(ch == 0 or u == 1))
                    mk = M.done(mm)
                    A.wait(mk, small[0])
                    rh = A.done(A.e.activation(RH[:, :], self.bank[kb][:, 0:P], ACT.Copy))
                    self.bank.read[kb] = rh
                    self.bank.give_back(kb)
                    yield
                    kb = self.bank.next()
                    M.wait(self.bank.read[kb])
                    M.wait(rh, *d["xt"])
                    for u in range(2):
                        hs = slice(HD * u, HD * u + HD)
                        mm = M.e.matmul(self.bank[kb][:, hs], XT[i][u][:, ch, :], RH[:, hs], start=True, stop=True)
                    xr = mk = M.done(mm)
                    A.wait(mk)
                    sa = A.done(A.e.activation(SA[:, :], self.bank[kb][:, 0:P], ACT.Copy))
                    self.bank.read[kb] = sa
                    self.bank.give_back(kb)
                    yield
                    kb, kc = self.bank.next(), self.bank.next()
                    M.wait(self.bank.read[kb])
                    M.wait(self.bank.read[kc])
                    M.wait(sa, d["bk"], d["rt"])
                    if ch < NB - 1:
                        M.e.matmul(self.bank[kb][:, 0:P], BK[i][:, 0, ch, :], SA[:, :], start=True, stop=False)
                        mk = M.done(M.e.matmul(self.bank[kb][:, 0:P], BK[i][:, 1, ch, :], Vt[:, ch, j * P:j * P + P],
                                              start=False, stop=True))
                        V.wait(mk, st, d["pe"])
                        if ch:
                            m = V.done(V.e.tensor_tensor(S1[:, :], self.bank[kb][:, 0:P], S0[:, :], ALU.add))
                            V.wait(m)
                            src = S1[:, :]
                        else:
                            V.wait(small[0])
                            src = self.bank[kb][:, 0:P]
                        stn = V.done(V.e.scalar_tensor_tensor(out=S1[:, :], in0=src, scalar=PE_[i][:, ch:ch + 1],
                                                             in1=c("blockones"), op0=ALU.mult, op1=ALU.mult))
                        self.bank.read[kb] = stn
                        self.bank.give_back(kb)
                    if ch:
                        M.e.matmul(self.bank[kc][:, 0:P], S0[:, :], R[:, j, cs], start=True, stop=False)
                    for u in range(2):
                        hs = slice(HD * u, HD * u + HD)
                        v = Vt[:, ch, j * P + HD * u:j * P + HD * u + HD]
                        out = self.bank[kc][hs, 0:P]
                        M.e.matmul(out, SA[:, hs], GM[i][u][:, 0, ch, :], start=(ch == 0), stop=False)
                        mm = M.e.matmul(out, v, GM[i][u][:, 2, ch, :], start=False, stop=True)
                    mk = M.done(mm)
                    small[0] = mk
                    A.wait(mk)
                    ym = A.done(A.e.activation(R[:, j, cs], self.bank[kc][:, 0:P], ACT.Copy))
                    self.bank.read[kc] = ym
                    self.bank.give_back(kc)
                    st = stn
                    yield
                d["end"] = (mk, stn)
                kb = self.bank.next()
                M.wait(self.bank.read[kb])
                M.wait(ym)
                mk = M.done(M.e.matmul(self.bank[kb][:, :], c("blockones"), R[:, j, :], start=True, stop=True))
                V.wait(mk, ym)
                rm[j] = V.done(V.e.scalar_tensor_tensor(out=R[:, j, :], in0=self.bank[kb][:, :], scalar=-1.0 / HD,
                                                       in1=R[:, j, :], op0=ALU.mult, op1=ALU.add))
                self.bank.read[kb] = rm[j]
                self.bank.give_back(kb)
                r = self.scratch.next()
                A.wait(self.scratch.read[r])
                A.wait(rm[j])
                m = A.done(A.e.activation(self.scratch[r][:, :], R[:, j, :], ACT.Square))
                M.wait(m)
                mk = M.done(M.e.matmul(self.bank[vb][0:16, :], c("head_col")[:, 16 - 2 * j:32 - 2 * j],
                                      self.scratch[r][:, :], start=(j == 0), stop=(j == KT - 1)))
                self.scratch.read[r] = mk
                d["var"] = mk

            for j in range(KT + 1):
                a = prepare(j) if j < KT else iter(())
                b = states(j - 1) if j else iter(())
                done = object()
                while True:
                    x, y = next(a, done), next(b, done)
                    if x is done and y is done:
                        break
            A.wait(pair[KT - 1]["var"], rn)
            M.wait(rn)
            m = A.done(A.e.activation(RN[:, :], self.bank[vb][0:16, :], ACT.Sqrt, bias=c("eps")[0:16, 1:2], scale=1.0 / HD))
            self.bank.read[vb] = m
            self.bank.give_back(vb)
            V.wait(m)
            rs = V.done(V.e.reciprocal(RN[:, :], RN[:, :]))
            for j in range(KT):
                js = slice(j * P, j * P + P)
                kb = self.bank.next()
                M.wait(self.bank.read[kb])
                M.wait(rs)
                mk = M.done(M.e.matmul(self.bank[kb][:, :], c("head_row", 16)[:, js], RN[:, :], start=True, stop=True))
                V.wait(mk, rm[j])
                m = V.done(V.e.scalar_tensor_tensor(out=R[:, j, :], in0=R[:, j, :], scalar=self.vec("rwkv_lnx_w", j),
                                                   in1=self.bank[kb][:, :], op0=ALU.mult, op1=ALU.mult))
                self.bank.read[kb] = m
                self.bank.give_back(kb)
                V.wait(m, pair[j]["bv"])
                rm[j] = V.done(V.e.scalar_tensor_tensor(out=R[:, j, :], in0=R[:, j, :], scalar=self.vec("rwkv_lnx_b", j),
                                                       in1=K[:, j, :], op0=ALU.add, op1=ALU.add))
            self.all_wait(mk, rm[KT - 1], *pair[KT - 1]["end"])
        self.open_operands()
        self.hold_split = False
        i, _, _ = self.piece("g2")
        raw = self.raw[i % 3]
        for j in range(KT):
            js = slice(j * P, j * P + P)
            kb = self.bank.next()
            M.wait(self.bank.read[kb])
            M.wait(lora)
            M.e.matmul(self.bank[kb][:, :], raw[:, js], SG[:, 0, :], start=True, stop=False)
            mk = M.done(M.e.matmul(self.bank[kb][:, :], raw[0:32, D + j * P:D + j * P + P], SG[0:32, 1, :],
                                  start=False, stop=True))
            r = self.scratch.next()
            V.wait(self.scratch.read[r])
            V.wait(mk, rm[j])
            m = V.done(V.e.tensor_tensor(self.scratch[r][:, :], R[:, j, :], self.bank[kb][:, :], ALU.mult))
            self.bank.read[kb] = m
            self.bank.give_back(kb)
            self.split_h(j, r, m)
        self.end_piece(i, mk)
        rwkv_read = self.h_ready[KT - 1]
        self.linear("rwkv_wo", KT, 2, self.Hh, self.Hl, self.add_to_x(True), self.h_wait, self.h_read)
        self.all_wait(mk, rwkv_read)
        right.close()

    def final_norm(self):
        pass

    def two_rstds(self):
        V, M = self.V, self.M
        yield
        b = self.bank.next()
        M.wait(self.bank.read[b])
        M.wait(self.ssq_ready, self.ssq2_ready)
        self.by_token(b, self.ssq, 0, 0)
        mk = self.ssq_used = self.by_token(b, self.ssq2, 1, 0)
        sums = self.bank[b][:, 0:2 * NB].rearrange("p (r t) -> p r t", r=2)
        st = self.stat
        _, m = self.root(sums[:, 0, :], mk, 0, 0)
        V.wait(m)
        s2 = V.done(V.e.tensor_tensor(st[:, 1, :], sums[:, 1, :], st[:, 0, :], ALU.mult))
        self.bank.read[b] = s2
        V.wait(s2)
        s2 = V.done(V.e.tensor_tensor(st[:, 1, :], st[:, 1, :], st[:, 0, :], ALU.mult))
        _, s2 = self.root(st[:, 1, :], s2, 2, 0)
        V.wait(s2)
        s2 = V.done(V.e.tensor_tensor(st[:, 3, :], st[:, 2, :], st[:, 0, :], ALU.mult))
        yield
        b, mk = self.rstd_spread(0, m)
        yield
        V.wait(mk)
        for j in range(KT):
            V.wait(self.x_ready[j], self.h_ready[j])
            self.x_ready[j] = V.done(V.e.scalar_tensor_tensor(out=self.X[:, j, :], in0=self.X[:, j, :],
                                                           scalar=self.vec("final_norm", j), in1=self.bank[b][:, :],
                                                           op0=ALU.mult, op1=ALU.mult))
        self.bank.read[b] = self.x_ready[KT - 1]
        self.keep_rstd(*self.rstd_spread(3, s2))

    def post_norm(self, Y, name, scale):
        V = self.V
        b, mk = self.rstd()
        V.wait(mk)
        for j in range(KT):
            r = self.scratch.next()
            V.wait(self.scratch.read[r])
            m = V.done(V.e.scalar_tensor_tensor(out=self.scratch[r][:, :], in0=Y[:, j, :], scalar=self.vec(name, j),
                                               in1=self.bank[b][:, :], op0=ALU.mult, op1=ALU.mult))
            V.wait(m, self.x_ready[j])
            self.x_ready[j] = V.done(V.e.scalar_tensor_tensor(out=self.X[:, j, :], in0=self.scratch[r][:, :], scalar=scale,
                                                           in1=self.X[:, j, :], op0=ALU.mult, op1=ALU.add))
            self.scratch.read[r] = self.x_ready[j]
            if self.then and j:
                self.square_and_operand(j - 1)
        if self.then:
            self.square_and_operand(KT - 1)
        self.bank.read[b] = m
        return m

    def ffn(self, tag):
        A, V, M = self.A, self.V, self.M
        rstd = self.stepper(self.two_rstds() if tag == "1" else self.rstd_between())
        with ExitStack() as s:
            NU = 12
            Uh, Ul = self.sb(f"f_hi{tag}", [P, NU, T], F32R, s), self.sb(f"f_lo{tag}", [P, NU, T], F32R, s)
            Y = self.sb(f"f_out{tag}", [P, KT, T], F32, s)
            um, ur, ym = [None] * NU, [None] * NU, [None] * KT
            for g, nu in enumerate((NU, D_FF2 // P - NU)):
                gate = {}

                def gate_up(o, b, mark):
                    f, part = o // 4 * 2 + o % 2, o % 4 // 2
                    if part == 0:
                        r = self.scratch.next()
                        V.wait(self.scratch.read[r])
                        V.wait(mark, self.rb_ready)
                        m = V.done(V.e.tensor_tensor(self.scratch[r][:, :], self.bank[b][:, :], self.rb, ALU.mult))
                        self.bank.read[b] = m
                        self.bank.give_back(b)
                        A.wait(m)
                        m = A.done(A.e.activation(self.scratch[r][:, :], self.scratch[r][:, :], ACT.Silu))
                        V.wait(m)
                        m = V.done(V.e.tensor_tensor(self.scratch[r][:, :], self.scratch[r][:, :], self.rb, ALU.mult))
                        gate[f] = (r, m)
                        return
                    r, m = gate[f]
                    V.wait(m, mark)
                    gu = V.done(V.e.tensor_tensor(self.scratch[r][:, :], self.scratch[r][:, :], self.bank[b][:, :], ALU.mult))
                    self.bank.read[b] = gu
                    self.bank.give_back(b)
                    A.wait(gu, ur[f])
                    hi = A.done(A.e.activation(Uh[:, f, :], self.scratch[r][:, :], ACT.Copy))
                    V.wait(hi, ur[f])
                    um[f] = V.done(V.e.tensor_tensor(Ul[:, f, :], self.scratch[r][:, :], Uh[:, f, :], ALU.subtract))
                    self.scratch.read[r] = um[f]
                self.linear("gu", KT, nu // 2, self.Hh, self.Hl, gate_up, self.h_wait, self.h_read if g else None,
                            None, None if g else rstd)

                def u_read(k0, nk, mark):
                    for k in range(k0, k0 + nk):
                        ur[k] = mark

                def out(o, b, mark):
                    V.wait(mark, ym[o])
                    if g == 0:
                        ym[o] = V.done(V.e.tensor_copy(Y[:, o, :], self.bank[b][:, :]))
                    else:
                        ym[o] = V.done(V.e.tensor_tensor(Y[:, o, :], Y[:, o, :], self.bank[b][:, :], ALU.add))
                        self.add_square(o, Y[:, o, :], ym[o])
                    self.bank.read[b] = ym[o]
                    self.bank.give_back(b)
                self.linear("ffn_out", nu, 2, Uh, Ul, out, lambda k: um[k], u_read)
            y_read = self.post_norm(Y, f"norm_ffn{tag}_post_2", 0.5)
            self.all_wait(ur[0], ur[NU - 1], ur[7], y_read)

    def mixer(self):
        A, V, M, G = self.A, self.V, self.M, self.G
        NH, DK = 4, 64
        with ExitStack() as s:
            sb = lambda n, sh: self.sb(n, sh, F32, s)
            cin = self.load_constants("mix", s)
            c = self.c
            QK, Vt, OS = sb("mx_qk", [P, 4, T]), sb("mx_v", [P, NB, T]), sb("mx_o", [P, 4, T])
            U = sb("mx_u", [P, 4, T + 2])
            S_, NS = sb("mx_s", [P, NB, T]), sb("mx_num", [P, 2, NH, T])
            GT = sb("mx_gates", [P, T])
            row = lambda n: sb(f"mx_row_{n}", [HD, T])
            ones_r, lf, e, u, l, dz = row("one"), row("lf"), row("e"), row("u"), row("l"), row("dz")
            cn, nm, en = row("c"), row("nm"), row("en")
            CT = sb("mx_ct", [P, NB, HD])
            V.wait(cin)
            pad = V.done(V.e.memset(U[:, :, 0:T + 2:T + 1], 0.0))
            on = V.done(V.e.memset(ones_r[:, :], 1.0))

            i, wh, wl = self.piece("gates")
            b = self.bank.next()
            M.wait(self.bank.read[b])
            for kt in range(KT):
                M.wait(self.h_ready[kt])
                w = slice(kt * P, kt * P + P)
                mm = self.mm3(self.bank[b][:, :], wh[:, w], wl[:, w], self.Hh[:, kt, :], self.Hl[:, kt, :],
                              kt == 0, kt == KT - 1)
            mk = M.done(mm)
            self.end_piece(i, mk)
            rstd_m = self.rstd_sums()
            self.keep_rstd(*self.rstd_spread(0, rstd_m))
            V.wait(mk, self.rb_ready)
            gm = V.done(V.e.tensor_tensor(GT[:, :], self.bank[b][:, :], self.rb, ALU.mult))
            A.wait(gm)
            gm2 = A.done(A.e.activation(GT[:, :], GT[:, :], ACT.Identity, bias=self.vec("gates", 0)))
            self.bank.read[b] = gm
            self.bank.give_back(b)

            def gate_rows():
                F, B = slice(0, 32), slice(32, 64)

                def v(ins):
                    m = V.done(ins)
                    V.wait(m)
                    return m
                V.wait(gm2, on)
                v(V.e.tensor_copy(cn[F, :], GT[0:32, :]))
                v(V.e.tensor_copy(cn[B, :], GT[32:64, ::-1]))
                v(V.e.tensor_copy(lf[F, :], GT[64:96, :]))
                m = v(V.e.tensor_copy(lf[B, :], GT[96:128, ::-1]))
                yield
                A.wait(m)
                m = A.done(A.e.activation(e[:, :], lf[:, :], ACT.Abs))
                A.wait(m)
                m = A.done(A.e.activation(e[:, :], e[:, :], ACT.Exp, scale=-1.0))
                V.wait(m)
                m = v(V.e.tensor_scalar(u[:, :], e[:, :], 1.0, None, ALU.add))
                A.wait(m)
                lm = A.done(A.e.activation(l[:, :], u[:, :], ACT.Ln))
                yield
                V.wait(lm)
                v(V.e.tensor_scalar(u[:, :], u[:, :], -1.0, None, ALU.add))
                v(V.e.tensor_scalar(dz[:, :], u[:, :], 0.0, None, ALU.is_equal))
                v(V.e.tensor_tensor(u[:, :], u[:, :], dz[:, :], ALU.add))
                v(V.e.reciprocal(u[:, :], u[:, :]))
                yield
                v(V.e.tensor_tensor(l[:, :], l[:, :], u[:, :], ALU.mult))
                v(V.e.tensor_tensor(l[:, :], l[:, :], dz[:, :], ALU.add))
                v(V.e.tensor_tensor(l[:, :], l[:, :], e[:, :], ALU.mult))
                v(V.e.scalar_tensor_tensor(out=lf[:, :], in0=lf[:, :], scalar=0.0, in1=l[:, :],
                                           op0=ALU.min, op1=ALU.subtract))
                v(V.e.tensor_tensor_scan(u[:, :], ones_r[:, :], lf[:, :], 0.0, ALU.mult, ALU.add))
                yield
                v(V.e.tensor_tensor(cn[:, :], cn[:, :], u[:, :], ALU.subtract))
                v(V.e.tensor_tensor_scan(l[:, :], cn[:, :], cn[:, :], -3.0e38, ALU.max, ALU.max))
                v(V.e.tensor_tensor(u[:, :], u[:, :], l[:, :], ALU.add))
                yield
                v(V.e.tensor_copy(e[:, :], cn[:, :]))
                v(V.e.tensor_copy(e[B, :], cn[B, ::-1]))
                v(V.e.tensor_scalar(nm[F, :], l[F, :], -1.0, None, ALU.mult))
                v(V.e.tensor_scalar(nm[B, :], l[B, ::-1], -1.0, None, ALU.mult))
                v(V.e.tensor_copy(dz[F, :], u[F, :]))
                m = v(V.e.tensor_copy(dz[B, :], u[B, ::-1]))
                A.wait(m)
                em = A.done(A.e.activation(en[:, :], dz[:, :], ACT.Exp, scale=-1.0))
                b = self.bank.next()
                M.wait(self.bank.read[b])
                M.wait(m, self.vecs_ready)
                for t in range(NB):
                    mm = M.e.transpose(self.bank[b][:, HD * t:HD * t + HD], e[:, t * P:t * P + P], c("ident", HD)[:, 0:HD])
                mk = M.done(mm)
                V.wait(mk)
                cm = V.done(V.e.tensor_copy(CT[:, :, :], self.bank[b][:, 0:NB * HD]))
                self.bank.read[b] = cm
                self.bank.give_back(b)
                rows.extend([em, cm, m])

            rows = []
            steps = gate_rows()
            step = lambda: next(steps, None)

            qk, vt, og, um, ym = [None] * 4, [None] * NB, [None] * 4, [None] * 4, [None] * 4

            def qk_out(o, b, mark):
                V.wait(mark)
                qk[o] = V.done(V.e.tensor_tensor(QK[:, o, :], self.bank[b][:, :], self.rb, ALU.mult))
                self.bank.read[b] = qk[o]
                self.bank.give_back(b)
            self.linear("mq", KT, 1, self.Hh, self.Hl, qk_out, self.h_wait, None, step)
            banks = [self.bank.next(keep=True) for _ in range(NB)]
            M.wait(*(self.bank.read[x] for x in banks))
            for k0 in range(0, KT, 4):
                i, wh, wl = self.piece("mv")
                for k in range(4):
                    for t in range(NB):
                        kt, ts, w = k0 + k, slice(t * P, t * P + P), slice(k * T, k * T + T)
                        mm = self.mm3(self.bank[banks[t]][:, :], self.Hh[:, kt, ts], self.Hl[:, kt, ts],
                                      wh[:, w], wl[:, w], kt == 0, kt == KT - 1)
                mk = M.done(mm)
                self.end_piece(i, mk)
                step()
            for t in range(NB):
                A.wait(mk)
                vt[t] = A.done(A.e.activation(Vt[:, t, :], self.bank[banks[t]][:, :], ACT.Copy,
                                              scale=self.stat[:, 0, t:t + 1]))
                self.bank.read[banks[t]] = vt[t]
                self.bank.give_back(banks[t])

            def cg_out(o, b, mark):
                V.wait(mark)
                um[o] = V.done(V.e.tensor_tensor(U[:, o, 1:T + 1], self.bank[b][:, :], self.rb, ALU.mult))
                self.bank.read[b] = um[o]
                self.bank.give_back(b)

            def hc_out(o, b, mark):
                V.wait(um[o])
                m = V.done(V.e.tensor_tensor(U[:, o, 1:T + 1], U[:, o, 1:T + 1], self.rb, ALU.mult))
                V.wait(mark, m)
                um[o] = V.done(V.e.tensor_tensor(U[:, o, 1:T + 1], U[:, o, 1:T + 1], self.bank[b][:, :], ALU.mult))
                self.bank.read[b] = um[o]
                self.bank.give_back(b)

            def bg_out(o, b, mark):
                r = self.scratch.next()
                V.wait(self.scratch.read[r])
                y = self.scratch[r][:, :]
                V.wait(um[o], pad)
                m = V.done(V.e.tensor_scalar(y, U[:, o, 0:T], self.vec("conv_w_2", o), self.vec("conv_b_2", o), ALU.mult, ALU.add))
                for tap in (1, 2):
                    V.wait(m)
                    m = V.done(V.e.scalar_tensor_tensor(out=y, in0=U[:, o, tap:tap + T], scalar=self.vec("conv_w_2", 4 * tap + o),
                                                       in1=y, op0=ALU.mult, op1=ALU.add))
                V.wait(m)
                m = V.done(V.e.tensor_tensor(y, y, self.rb, ALU.mult))
                V.wait(m, mark)
                ym[o] = V.done(V.e.tensor_tensor(U[:, o, 1:T + 1], y, self.bank[b][:, :], ALU.mult))
                self.bank.read[b] = ym[o]
                self.bank.give_back(b)
                self.scratch.read[r] = ym[o]

            def o_out(o, b, mark):
                V.wait(mark)
                m = V.done(V.e.tensor_tensor(OS[:, o, :], self.bank[b][:, :], self.rb, ALU.mult))
                self.bank.read[b] = m
                A.wait(m)
                og[o] = A.done(A.e.activation(OS[:, o, :], OS[:, o, :], ACT.Sigmoid))
                self.bank.give_back(b)
            for name, out in (("cg", cg_out), ("hc", hc_out), ("bg", bg_out), ("mo", o_out)):
                self.linear(name, KT, 1, self.Hh, self.Hl, out, self.h_wait, self.h_read if name == "mo" else None, step)
            for _ in steps:
                pass
            em, cm, nmm = rows

            for o in range(4):
                A.wait(ym[o], self.h_used[o])
                hi = A.done(A.e.activation(self.Hh[:, o, :], U[:, o, 1:T + 1], ACT.Copy))
                V.wait(hi)
                self.h_ready[o] = V.done(V.e.tensor_tensor(self.Hl[:, o, :], U[:, o, 1:T + 1], self.Hh[:, o, :], ALU.subtract))

            den = self.bank.next(keep=True)
            M.wait(self.bank.read[den])
            nk, den_mark = {}, None
            sread = [None] * NB
            for h in range(NH):
                p0, sm = DK * (h % 2), [None] * NB
                for si in range(NB):
                    b = self.bank.next()
                    M.wait(self.bank.read[b])
                    M.wait(qk[h // 2], qk[2 + h // 2])
                    mk = M.done(M.e.matmul(self.bank[b][:, :], QK[p0:p0 + DK, 2 + h // 2, si * P:si * P + P],
                                          QK[p0:p0 + DK, h // 2, :], start=True, stop=True))
                    A.wait(mk, sread[si])
                    sm[si] = A.done(A.e.activation(S_[:, si, :], self.bank[b][:, :], ACT.Copy, scale=DK ** -0.5))
                    self.bank.read[b] = sm[si]
                    self.bank.give_back(b)
                for d in range(2):
                    rows_d = slice(32 * d, 32 * d + 4)
                    b = self.bank.next(keep=True)
                    M.wait(self.bank.read[b])
                    M.wait(nmm, cin)
                    mk = M.done(M.e.matmul(self.bank[b][:, :], c("row_pick")[rows_d, h * P:h * P + P], nm[rows_d, :],
                                          start=True, stop=True))
                    nb = self.bank.next(keep=True)
                    M.wait(self.bank.read[nb])
                    order = range(NB) if d == 0 else range(NB - 1, -1, -1)
                    for n, si in enumerate(order):
                        ts = slice(si * P, T) if d == 0 else slice(0, si * P + P)
                        r = self.scratch.next()
                        V.wait(self.scratch.read[r])
                        w = self.scratch[r][:, ts]
                        V.wait(mk, cm)
                        m = V.done(V.e.tensor_scalar(w, self.bank[b][:, ts], CT[:, si, 32 * d + h:32 * d + h + 1], 0.0,
                                                    ALU.add, ALU.min))
                        A.wait(m)
                        m = A.done(A.e.activation(w, w, ACT.Exp))
                        G.wait(m, cin)
                        dg = self.scratch[r][:, si * P:si * P + P]
                        m2 = G.done(G.e.tensor_tensor(dg, dg, c("s_ge_t" if d else "s_le_t"), ALU.mult))
                        V.wait(m2, m, sm[si])
                        m = V.done(V.e.tensor_tensor(w, w, S_[:, si, ts], ALU.mult))
                        if d == 1:
                            sread[si] = m
                        M.wait(m, vt[si])
                        M.e.matmul(self.bank[nb][:, ts], Vt[:, si, h * P:h * P + P], w, start=(n == 0), stop=(n == NB - 1))
                        mm = M.done(M.e.matmul(self.bank[den][32 * d:32 * d + 32, ts], c("one_col")[:, 32 - h:64 - h], w,
                                              start=(n == 0 and h == 0), stop=(n == NB - 1 and h == NH - 1)))
                        self.scratch.read[r] = mm
                    self.bank.read[b] = m
                    self.bank.give_back(b)
                    A.wait(mm)
                    nk[d, h] = A.done(A.e.activation(NS[:, d, h, :], self.bank[nb][:, :], ACT.Copy))
                    self.bank.read[nb] = nk[d, h]
                    self.bank.give_back(nb)
            A.wait(mm)
            m = A.done(A.e.activation(e[:, :], self.bank[den][0:HD, :], ACT.Abs))
            self.bank.read[den] = m
            self.bank.give_back(den)
            V.wait(m, em)
            m = V.done(V.e.tensor_tensor(e[:, :], e[:, :], en[:, :], ALU.max))
            V.wait(m)
            rd = V.done(V.e.reciprocal(e[:, :], e[:, :]))
            ss = self.bank.next(keep=True)
            M.wait(self.bank.read[ss])
            for h in range(NH):
                for d in range(2):
                    rows_d = slice(32 * d, 32 * d + 4)
                    b = self.bank.next()
                    M.wait(self.bank.read[b])
                    M.wait(rd)
                    mk = M.done(M.e.matmul(self.bank[b][:, :], c("row_pick")[rows_d, h * P:h * P + P], e[rows_d, :],
                                          start=True, stop=True))
                    V.wait(mk, nk[d, h])
                    m = V.done(V.e.tensor_tensor(NS[:, d, h, :], NS[:, d, h, :], self.bank[b][:, :], ALU.mult))
                    self.bank.read[b] = m
                    self.bank.give_back(b)
                V.wait(m)
                nk[0, h] = V.done(V.e.tensor_tensor(NS[:, 0, h, :], NS[:, 0, h, :], NS[:, 1, h, :], ALU.add))
                r = self.scratch.next()
                A.wait(self.scratch.read[r])
                A.wait(nk[0, h])
                m = A.done(A.e.activation(self.scratch[r][:, :], NS[:, 0, h, :], ACT.Square))
                M.wait(m)
                mk = M.done(M.e.matmul(self.bank[ss][0:32, :], c("one_col")[:, 32 - h:64 - h], self.scratch[r][:, :],
                                      start=(h == 0), stop=(h == NH - 1)))
                self.scratch.read[r] = mk
            A.wait(mk)
            m = A.done(A.e.activation(u[0:32, :], self.bank[ss][0:32, :], ACT.Sqrt, bias=c("eps")[0:32, 0:1], scale=1.0 / P))
            self.bank.read[ss] = m
            self.bank.give_back(ss)
            V.wait(m)
            rs = V.done(V.e.reciprocal(u[0:32, :], u[0:32, :]))
            for h in range(NH):
                b = self.bank.next()
                M.wait(self.bank.read[b])
                M.wait(rs)
                mk = M.done(M.e.matmul(self.bank[b][:, :], c("row_pick")[0:4, h * P:h * P + P], u[0:4, :],
                                      start=True, stop=True))
                r = self.scratch.next()
                V.wait(self.scratch.read[r])
                V.wait(mk, nk[0, h], og[h])
                m = V.done(V.e.scalar_tensor_tensor(out=self.scratch[r][:, :], in0=NS[:, 0, h, :],
                                                   scalar=self.vec("mlstm_norm_2", h), in1=self.bank[b][:, :],
                                                   op0=ALU.mult, op1=ALU.mult))
                self.bank.read[b] = m
                self.bank.give_back(b)
                V.wait(m)
                m = V.done(V.e.tensor_tensor(self.scratch[r][:, :], self.scratch[r][:, :], OS[:, h, :], ALU.mult))
                self.split_h(4 + h, r, m)

            Y, ym = NS[:, :, :, :].rearrange("p d h t -> p (d h) t"), [None] * KT

            def out(o, b, mark):
                V.wait(mark, self.h_ready[KT - 1])
                ym[o] = V.done(V.e.tensor_copy(Y[:, o, :], self.bank[b][:, :]))
                self.bank.read[b] = ym[o]
                self.bank.give_back(b)
                self.add_square(o, Y[:, o, :], ym[o])
            self.stat_used = vt[-1]
            self.linear("mix_out", KT, 2, self.Hh, self.Hl, out, self.h_wait, self.h_read)
            self.all_wait(self.post_norm(Y, "norm_mix_post_2", 1.0), self.h_used[KT - 1])


_OUT = (1, T, D)
_MATS = ["dsa_w_in", "dsa_w_o", "mlp_w_up", "mlp_w_down", "rwkv_w_rkv", "rwkv_w1", "rwkv_w2", "rwkv_a1", "rwkv_a2",
         "rwkv_g1", "rwkv_g2", "rwkv_w_o", "w_ffn1_in_2", "w_ffn1_out_2", "w_mix_in_2", "w_mix_out_2",
         "w_ffn2_in_2", "w_ffn2_out_2"]


def host_arrays(inputs):
    rows = []
    for name, n in VECS:
        if name == "gates":
            row = np.zeros((1, P), np.float32)
            gi, gf = np.asarray(inputs["gate_i_bias_2"])[0], np.asarray(inputs["gate_f_bias_2"])[0]
            for q, part in enumerate((gi[0:4], gi[4:8], gf[0:4], gf[4:8])):
                row[0, 32 * q:32 * q + 4] = part
            rows.append(row)
        else:
            rows.append(np.asarray(inputs[name]).reshape(n, P))
    arrays = {"x": np.ascontiguousarray(inputs["x"]), "vecs": np.concatenate(rows, 0),
              "rope": rope_table()}
    for g in GROUPS:
        arrays[f"const_{g}"] = const_group(g)
    for name in _MATS:
        arrays[name] = np.ascontiguousarray(inputs[name])
    return arrays


def program(nc, arrays):
    io = {}
    for name, a in arrays.items():
        io[name] = nc.dram_tensor(f"in_{name}", a.shape, F32, kind="ExternalInput").ap()
    io["out"] = nc.dram_tensor("out", _OUT, F32, kind="ExternalOutput").ap()
    Program(nc, io).build()


def kernel(**inputs):
    import concourse.bacc as bacc
    from concourse.bass_utils import run_bass_kernel_spmd
    arrays = host_arrays(inputs)
    nc = bacc.Bacc("TRN2", target_bir_lowering=False, num_devices=1)
    program(nc, arrays)
    r = run_bass_kernel_spmd(nc, [{f"in_{n}": a for n, a in arrays.items()}], core_ids=[0])
    return r.results[0]["out"]
```

```python
import numpy as np
from contextlib import ExitStack
from itertools import chain
import concourse.bass as bass
from concourse import mybir
from concourse.alu_op_type import AluOpType as ALU

F32 = mybir.dt.float32
F32R = mybir.dt.float32r
I32 = mybir.dt.int32
ACT = mybir.ActivationFunctionType
AX = mybir.AxisListType

P = 128
T = 512
D = 1024
KT = D // P
NB = T // P
HD = 64
PIECE = 2048
NEG = -1e30
SCORE_OUT = float(np.float32(-3.0e38))
SCORE_TAKEN = float(np.float32(-3.3e38))

LEVELS = 7
TOPK = min(256, T // 4)
D_FF, D_FF2 = 4 * D, 2816
Q_COLS, KV_COLS, IQ_COLS, IK_COLS, IW_COLS = 1024, 256, 512, 64, 8
IDX_HEADS = 8

VECS = [("mixer_norm", 16), ("mlp_norm", 16), ("final_norm", 8), ("rwkv_mu", 48), ("rwkv_w0", 8),
        ("rwkv_a0", 8), ("rwkv_k_k", 8), ("rwkv_k_a", 8), ("rwkv_r_k", 8),
        ("rwkv_lnx_w", 8), ("rwkv_lnx_b", 8),
        ("norm_ffn1_pre_2", 8), ("norm_ffn1_post_2", 8), ("norm_mix_pre_2", 8), ("norm_mix_post_2", 8),
        ("norm_ffn2_pre_2", 8), ("norm_ffn2_post_2", 8), ("conv_w_2", 12), ("conv_b_2", 4),
        ("mlstm_norm_2", 4), ("gates", 1)]
VROWS = sum(n for _, n in VECS)
VAT = {}
_at = 0
for _name, _n in VECS:
    VAT[_name] = _at
    _at += _n


def constants():
    i = np.arange(P)
    k, m = i[:, None], i[None, :]
    c = {}
    c["ident"] = (k == m)
    c["ones"] = np.ones((P, P))
    c["swap"] = (k == (m // 64) * 64 + (m % 64 + 32) % 64)
    c["blockones"] = (k // 64 == m // 64)
    c["causal_bias"] = np.where(m <= k, 0.0, NEG)
    c["causal_score"] = np.where(m <= k, 0.0, SCORE_OUT)
    c["s_lt_t"] = (k < m)
    c["s_le_t"] = (k <= m)
    c["s_ge_t"] = (k >= m)
    for lv in range(LEVELS):
        b = 1 << lv
        level = (k // (2 * b) == m // (2 * b)) & (k // b % 2 == 1) & (m // b % 2 == 0)
        if lv:
            c[f"level{lv}"] = level[:, np.arange(P) // b % 2 == 0]
        else:
            c["level0"], c["level0T"] = level, level.T
    c["head_col"] = np.concatenate([np.zeros((P, 16)), (i < 64)[:, None], (i >= 64)[:, None], np.zeros((P, 14))], 1)
    c["one_col"] = np.concatenate([np.zeros((P, 32)), np.ones((P, 1)), np.zeros((P, 31))], 1)
    hr = np.zeros((P, KT * P))
    for j in range(KT):
        hr[2 * j, j * P:j * P + 64] = 1
        hr[2 * j + 1, j * P + 64:(j + 1) * P] = 1
    c["head_row"] = hr
    rr = np.zeros((P, 4 * P))
    for h in range(4):
        rr[[h, 32 + h], h * P:(h + 1) * P] = 1
    c["row_pick"] = rr
    c["eps"] = np.concatenate([np.full((P, 1), 1e-6), np.full((P, 1), 64e-5)], 1)
    reset = np.ones((P, T))
    reset[:, ::P] = 0
    c["chunk_start"] = reset
    return {n: np.asarray(a, np.float32) for n, a in c.items()}


def rope_table():
    inv = (1.0 / (np.float32(10000.0) ** (np.arange(0, HD, 2, dtype=np.float32) / np.float32(HD)))).astype(np.float32)
    ang = np.arange(T, dtype=np.float32)[:, None] * inv[None, :]
    cos, sin = np.cos(ang).astype(np.float32).T, np.sin(ang).astype(np.float32).T
    return np.concatenate([np.concatenate([cos] * 4, 0), np.concatenate([-sin, sin] * 2, 0)], 1)


_CONST = constants()
GROUPS = {"core": ["ident", "ones", "eps", "one_col"],
          "dsa": ["swap", "causal_bias", "causal_score"],
          "rwkv": ["blockones", "s_lt_t", "s_le_t"] + [f"level{lv}" for lv in range(LEVELS)]
                  + ["level0T", "head_col", "head_row"],
          "scan": ["chunk_start"],
          "mix": ["s_le_t", "s_ge_t", "row_pick"]}


def const_group(g):
    return np.concatenate([_CONST[n] for n in GROUPS[g]], 1)


class Engine:

    def __init__(self, engine, sem, step=1):
        self.e, self.sem, self.step, self.n = engine, sem, step, 0

    def done(self, ins):
        self.n += self.step
        ins.then_inc(self.sem, self.step)
        return (self.sem, self.n)

    def wait(self, *counts):
        for c in counts:
            if c is not None:
                self.e.wait_ge(c[0], c[1])


class Turns:

    def __init__(self, bufs):
        self.bufs, self.at, self.read, self.kept = bufs, -1, [None] * len(bufs), set()

    def next(self, keep=False):
        self.at = (self.at + 1) % len(self.bufs)
        while self.at in self.kept:
            self.at = (self.at + 1) % len(self.bufs)
        if keep:
            self.kept.add(self.at)
        return self.at

    def give_back(self, i):
        self.kept.discard(i)

    def __getitem__(self, i):
        return self.bufs[i]


class Program:
    def __init__(self, nc, io):
        self.nc, self.io = nc, io
        self.ctx = ExitStack()

    def sb(self, name, shape, dt=F32, ctx=None, **kw):
        return (ctx or self.ctx).enter_context(self.nc.sbuf_tensor(name, shape, dt, **kw))

    def build(self):
        with self.ctx:
            self.setup()
            stages = [("dsa", self.dsa), ("mlp0", lambda: self.mlp(0)), ("rwkv", self.rwkv),
                      ("mlp1", lambda: self.mlp(1)), ("final", self.final_norm),
                      ("ffn1", lambda: self.ffn("1")), ("mix", self.mixer), ("ffn2", lambda: self.ffn("2"))]
            names = [n for n, _ in stages] + [None]
            self.then = names[0]
            self.load_x()
            for at, (_, stage) in enumerate(stages):
                self.then = names[at + 1]
                stage()
            self.store()
            self.op_ctx.close()

    def setup(self):
        nc, ctx = self.nc, self.ctx

        def line(engine, name, step=1):
            return Engine(engine, ctx.enter_context(nc.semaphore(name)), step)

        self.S = Engine(nc.sync, None)
        self.V = line(nc.vector, "vector_done")
        self.A = line(nc.scalar, "scalar_done")
        self.G = line(nc.gpsimd, "gpsimd_done")
        self.M = line(nc.tensor, "tensor_done")
        self.load_small = line(None, "small_loaded", 16)
        self.x_loaded = [line(None, f"x_loaded{i}", 16) for i in range(2)]
        self.low_loaded = line(None, "low_rank_weights_loaded", 16)
        self.stored = line(None, "stored", 16)

        self.X = self.sb("x_t", [P, KT, T])
        self.consts = {}
        self.load_constants("core")
        self.vecs = self.sb("vecs", [P, VROWS])
        self.stat = self.sb("stat", [P, 6, NB])
        self.diag = self.sb("diag", [P, NB, P])
        self.ssq = self.sb("ssq", [P, T])
        self.ssq2 = self.sb("ssq_gained", [P, T])
        self.gain2 = self.sb("final_and_pre_gain", [P, KT])
        self.scratch = Turns([self.sb(f"scratch{i}", [P, T]) for i in range(6)])
        self.raw = [self.sb(f"raw{i}", [P, PIECE]) for i in range(3)]
        self.raw_in = [line(None, f"raw_loaded{i}", 16) for i in range(3)]
        psum = [ctx.enter_context(nc.psum_tensor(f"bank{i}", [P, T], F32)) for i in range(8)]
        self.bank = Turns(psum)
        self.x_ready = [None] * KT
        self.h_ready = [None] * KT
        self.h_used = [None] * KT
        self.rb = self.diag[:, :, :].rearrange("p b t -> p (b t)")
        self.scopes = 0
        self.pieces, self.loaded, self.split_at, self.at = [], 0, 0, 0
        self.w_landed, self.w_cut, self.w_used, self.raw_read = {}, {}, {}, {}
        self.open_operands()

    def open_operands(self):
        self.scopes += 1
        self.op_ctx = ExitStack()
        n = self.scopes
        self.Hh = self.sb(f"h_hi{n}", [P, KT, T], F32R, self.op_ctx)
        self.Hl = self.sb(f"h_lo{n}", [P, KT, T], F32R, self.op_ctx)
        self.Wh = [self.sb(f"w_hi{n}_{i}", [P, PIECE], F32R, self.op_ctx) for i in range(2)]
        self.Wl = [self.sb(f"w_lo{n}_{i}", [P, PIECE], F32R, self.op_ctx) for i in range(2)]

    def load_constants(self, group, ctx=None, **kw):
        cols = sum(_CONST[n].shape[1] for n in GROUPS[group])
        t = self.sb(f"const_{group}", [P, cols], F32, ctx, **kw)
        mark = self.load_small.done(self.A.e.dma_start(t[:, :], self.io[f"const_{group}"]))
        at = 0
        for n in GROUPS[group]:
            w = _CONST[n].shape[1]
            self.consts[n] = t[:, at:at + w]
            at += w
        return mark

    def c(self, name, rows=P):
        return self.consts[name][0:rows, :]

    def vec(self, name, j):
        return self.vecs[:, VAT[name] + j:VAT[name] + j + 1]

    def plan_weights(self, start):
        io, plan = self.io, self.pieces

        def tiles(name, w, r0, nk, c0, nc_, split=True):
            src = w[r0:r0 + nk * P, c0:c0 + nc_].rearrange("(k p) n -> p k n", p=P)
            plan.append((name, [(slice(0, P), 0, nk, nc_, nc_, src)], split))

        def linear(name, w, rows, c0, cols):
            for cg in range(0, cols, 512):
                n = min(512, cols - cg)
                for r in range(0, rows, 512):
                    tiles(name, w, r, min(4, (rows - r) // P), c0 + cg, n)

        w_in = io["dsa_w_in"][0]
        o2, o3 = Q_COLS + 2 * KV_COLS, Q_COLS + 2 * KV_COLS + IQ_COLS
        ki = w_in[:, o3:o3 + 64].rearrange("(k p) n -> p k n", p=P)
        kiw = w_in[:, o3:o3 + 72].rearrange("(k p) n -> p k n", p=P)
        plan.append(("ki", [(slice(0, P), 0, KT, 64, 136, ki), (slice(0, P), 64, KT, 72, 136, kiw)], True))
        linear("qi", w_in, D, o2, IQ_COLS)
        linear("q", w_in, D, 0, Q_COLS)
        linear("kv", w_in, D, Q_COLS, 2 * KV_COLS)
        w_o = io["dsa_w_o"][0]
        for cg in range(2):
            for kg in range(2):
                parts = []
                for u in range(2):
                    rows = w_o[(8 * kg + 4 * u) * HD:(8 * kg + 4 * u + 4) * HD, cg * 512:cg * 512 + 512]
                    parts.append((slice(64 * u, 64 * u + 64), 0, 4, 512, 512, rows.rearrange("(i p) n -> p i n", p=HD)))
                plan.append(("wo", parts, True))

        def mlp(l):
            for g in range(0, D_FF, 2048):
                linear("up", io["mlp_w_up"][l], D, g, 2048)
                linear("down", io["mlp_w_down"][l][g:g + 2048, :], 2048, 0, D)
        mlp(0)
        for name, c in (("v", 2), ("r", 0), ("k", 1)):
            linear(name, io["rwkv_w_rkv"][0][c], D, 0, D)
        g2 = io["rwkv_g2"][0]
        plan.append(("g2", [(slice(0, P), 0, 1, D, D, g2[0:P, :]), (slice(0, 32), D, 1, D, D, g2[P:160, :])], False))
        linear("rwkv_wo", io["rwkv_w_o"][0], D, 0, D)
        mlp(1)

        def ffn(tag):
            w1, w2 = io[f"w_ffn{tag}_in_2"][0], io[f"w_ffn{tag}_out_2"][0]
            for g0, gn in ((0, 12), (12, 10)):
                for f in range(g0, g0 + gn, 2):
                    for r in range(0, D, 512):
                        parts = [(slice(0, P), u * 256, 4, 256, 512,
                                  w1[r:r + 512, u * D_FF2 + f * P:u * D_FF2 + f * P + 256]
                                  .rearrange("(k p) n -> p k n", p=P)) for u in range(2)]
                        plan.append(("gu", parts, True))
                linear("ffn_out", w2[g0 * P:(g0 + gn) * P, :], gn * P, 0, D)
        ffn("1")
        wm = io["w_mix_in_2"][0]
        plan.append(("gates", [(slice(0, P), 1024, KT, 16, 16, wm[:, 3072:3088].rearrange("(k p) n -> p k n", p=P))], "gates"))
        linear("mq", wm, D, 1536, 512)
        linear("mv", wm, D, 2048, 512)
        linear("cg", wm, D, 512, 512)
        linear("hc", wm, D, 1024, 512)
        linear("bg", wm, D, 0, 512)
        linear("mo", wm, D, 2560, 512)
        linear("mix_out", io["w_mix_out_2"][0], D, 0, D)
        ffn("2")
        for _ in range(start):
            self.load_piece()

    def load_piece(self):
        i = self.loaded
        if i >= len(self.pieces) or (i >= 3 and i - 3 not in self.raw_read):
            return
        self.loaded += 1
        slot = i % 3
        S = self.S
        if i >= 3:
            S.wait(*self.raw_read[i - 3])
        for rows, at, nk, n, width, src in self.pieces[i][1]:
            if nk == 1:
                dst = self.raw[slot][rows, at:at + n]
            else:
                base = at // width * width
                dst = (self.raw[slot][rows, base:base + nk * width]
                       .rearrange("p (k w) -> p k w", k=nk)[:, :, at - base:at - base + n])
            mark = self.raw_in[slot].done(S.e.dma_start(dst, src))
        self.w_landed[i] = mark

    def split_piece(self):
        i = self.split_at
        if i >= len(self.pieces) or i > self.at + 1:
            return
        A, G, V = self.A, self.G, self.V
        name, parts, split = self.pieces[i]
        if self.hold_split and split and name != "k":
            return
        self.split_at += 1
        landed = self.w_landed[i]
        slot, w = i % 3, i % 2
        if split is False:
            return
        n = sum(nk * n for _, _, nk, n, _, _ in parts)
        if name == "wo":
            n //= 2
        raw = self.raw[slot]
        if split == "gates":
            z = raw[:, 0:1024].rearrange("p (k w) -> p k w", k=KT)
            src = raw[:, 1024:1024 + 16 * KT].rearrange("p (k w) -> p k w", k=KT)
            G.wait(landed, *self.raw_read.get(i - 3, ()))
            zero = G.done(G.e.memset(raw[:, 0:1024], 0.0))
            G.wait(zero)
            for q in range(4):
                m = G.done(G.e.tensor_copy(z[:, :, 32 * q:32 * q + 4], src[:, :, 4 * q:4 * q + 4]))
            A.wait(m)
            n = 1024
        used = self.w_used.get(i - 2)
        A.wait(landed, used)
        G.wait(landed, used)
        if name == "q":
            for k in range(4):
                r_, h_, l_ = (t[:, 512 * k:512 * k + 512] for t in (raw, self.Wh[w], self.Wl[w]))
                r_ = r_.rearrange("p (u i c) -> p u i c", u=2, i=4)
                h_, l_ = (t.rearrange("p (i u c) -> p u i c", u=2, i=4) for t in (h_, l_))
                hi = A.done(A.e.activation(h_, r_, ACT.Copy))
                G.wait(hi)
                lo = G.done(G.e.tensor_tensor(l_, r_, h_, ALU.subtract))
        else:
            hi = A.done(A.e.activation(self.Wh[w][:, 0:n], raw[:, 0:n], ACT.Copy))
            G.wait(hi)
            lo = G.done(G.e.tensor_tensor(self.Wl[w][:, 0:n], raw[:, 0:n], self.Wh[w][:, 0:n], ALU.subtract))
        self.raw_read[i] = (hi, lo)
        self.w_cut[i] = (hi, lo)
        self.load_piece()

    hold_split = False
    ssq_used = ssq_ready = ssq2_ready = stat_used = rb_used = None

    def piece(self, name, wait=True):
        i = self.at
        assert self.pieces[i][0] == name, (self.pieces[i][0], name)
        while self.split_at <= min(i + 1, len(self.pieces) - 1):
            was = self.split_at
            self.split_piece()
            if was == self.split_at:
                break
        self.at += 1
        if self.pieces[i][2] is False:
            self.M.wait(self.w_landed[i])
        else:
            self.M.wait(*self.w_cut[i])
        return i, self.Wh[i % 2], self.Wl[i % 2]

    def end_piece(self, i, mark):
        self.w_used[i] = mark
        if self.pieces[i][2] is False:
            self.raw_read[i] = (mark,)
            self.load_piece()
            self.load_piece()

    def mm3(self, out, wh, wl, xh, xl, first, last):
        mm = self.M.e.matmul
        mm(out, wl, xh, start=first, stop=False)
        mm(out, wh, xl, start=False, stop=False)
        return mm(out, wh, xh, start=False, stop=last)

    def linear(self, name, kt_all, groups, xh, xl, evacuate, xwait, xread=None, each_piece=None, each_strip=None,
               cols=512):
        M = self.M
        for cg in range(groups):
            nt = cols // P
            banks = [self.bank.next(keep=True) for _ in range(nt)]
            M.wait(*(self.bank.read[x] for x in banks))
            for k0 in range(0, kt_all, 4):
                nk = min(4, kt_all - k0)
                i, wh, wl = self.piece(name)
                for o in range(nt):
                    for k in range(nk):
                        kt = k0 + k
                        if o == 0 and cg == 0:
                            M.wait(xwait(kt))
                        s = slice(k * cols + o * P, k * cols + o * P + P)
                        mm = self.mm3(self.bank[banks[o]][:, :], wh[:, s], wl[:, s], xh[:, kt, :], xl[:, kt, :],
                                      kt == 0, kt == kt_all - 1)
                    if kt == kt_all - 1:
                        mark = M.done(mm)
                        evacuate(cg * 4 + o, banks[o], mark)
                    elif o == nt - 1:
                        mark = M.done(mm)
                    if each_strip:
                        each_strip()
                self.end_piece(i, mark)
                if xread is not None and cg == groups - 1:
                    xread(k0, nk, mark)
                if each_piece:
                    each_piece()

    def load_x(self):
        A, V, M, nc = self.A, self.V, self.M, self.nc
        x = self.io["x"][0]
        with ExitStack() as s:
            xin = self.sb("x_in", [P, NB, D], F32, s)
            x_in = []
            for half in range(2):
                w = slice(half * 512, half * 512 + 512)
                x_in.append(self.x_loaded[half].done(self.S.e.dma_start(xin[:, :, w], x[:, w].rearrange("(b p) d -> p b d", p=P))))
                if half == 0:
                    self.plan_weights(1)
            for _ in range(2):
                self.load_piece()
            vin = self.sb("vecs_in", [P, 2, P], F32, s)
            m2 = self.load_small.done(A.e.dma_start(vin[:, 0, :], self.io["vecs"][0:P, :]))
            m2 = self.load_small.done(A.e.dma_start(vin[0:VROWS - P, 1, :], self.io["vecs"][P:VROWS, :]))
            M.wait(m2)
            ident = self.c("ident")
            b = self.bank.next()
            M.wait(self.bank.read[b])
            M.e.transpose(self.bank[b][:, 0:P], vin[:, 0, :], ident)
            mk = M.done(M.e.transpose(self.bank[b][:, P:VROWS], vin[0:VROWS - P, 1, :],
                                     ident[0:VROWS - P, 0:VROWS - P]))
            V.wait(mk)
            self.vecs_ready = V.done(V.e.tensor_copy(self.vecs[:, :], self.bank[b][:, 0:VROWS]))
            self.bank.read[b] = self.vecs_ready
            V.wait(self.vecs_ready)
            n, f = VAT["norm_ffn1_pre_2"], VAT["final_norm"]
            self.gain2_ready = V.done(V.e.tensor_tensor(self.gain2[:, :], self.vecs[:, n:n + KT], self.vecs[:, f:f + KT],
                                                       ALU.mult))
            A.wait(self.vecs_ready)
            self.bank.give_back(b)
            self.split_piece()
            for j in range(KT):
                b = self.bank.next()
                M.wait(self.bank.read[b])
                M.wait(x_in[j // 4])
                for t in range(NB):
                    mm = M.e.transpose(self.bank[b][:, t * P:(t + 1) * P], xin[:, t, j * P:(j + 1) * P], ident)
                mk = M.done(mm)
                V.wait(mk)
                self.x_ready[j] = V.done(V.e.tensor_copy(self.X[:, j, :], self.bank[b][:, :]))
                self.bank.read[b] = self.x_ready[j]
                self.bank.give_back(b)
                if j:
                    self.square_and_operand(j - 1)
            self.square_and_operand(KT - 1)
            self.all_wait(mk)

    def all_wait(self, *counts):
        for engine in (self.A, self.V, self.G, self.S):
            engine.wait(*counts)

    def store(self):
        V, M, A = self.V, self.M, self.A
        ident = self.c("ident")
        with ExitStack() as s:
            xo = self.sb("x_out", [P, NB, D], F32, s)
            for t in range(NB):
                for half in range(2):
                    b = self.bank.next()
                    M.wait(self.bank.read[b])
                    for jj in range(4):
                        j = half * 4 + jj
                        M.wait(self.x_ready[j])
                        mm = M.e.transpose(self.bank[b][:, jj * P:(jj + 1) * P], self.X[:, j, t * P:(t + 1) * P], ident)
                    mk = M.done(mm)
                    V.wait(mk)
                    cp = V.done(V.e.tensor_copy(xo[:, t, half * 512:half * 512 + 512], self.bank[b][:, :]))
                    self.bank.read[b] = cp
                    self.bank.give_back(b)
                self.S.wait(cp)
                out = self.stored.done(self.S.e.dma_start(self.io["out"][0][t * P:(t + 1) * P, :], xo[:, t, :]))
            self.S.wait(out)

    def add_square(self, j, src=None, mark=None, adder=None):
        src = self.X[:, j, :] if src is None else src
        mark = self.x_ready[j] if mark is None else mark
        self.ssq_ready = self.add_square_to(self.ssq, j, src, mark, self.ssq_ready, adder or self.V)
        if self.then == "final":
            self.ssq2_ready = self.add_square_to(self.ssq2, j, src, mark, self.ssq2_ready, adder or self.V,
                                                 self.vec("final_norm", j))

    def add_square_to(self, ssq, j, src, mark, ssq_ready, adder, gain=1.0):
        A = self.A
        if j == 0:
            A.wait(mark, self.ssq_used)
            return A.done(A.e.activation(ssq[:, :], src, ACT.Square, scale=gain))
        s = self.scratch.next()
        A.wait(self.scratch.read[s])
        A.wait(mark)
        sq = A.done(A.e.activation(self.scratch[s][:, :], src, ACT.Square, scale=gain))
        adder.wait(sq, ssq_ready)
        self.scratch.read[s] = adder.done(adder.e.tensor_tensor(ssq[:, :], ssq[:, :], self.scratch[s][:, :], ALU.add))
        return self.scratch.read[s]

    def gain(self, j):
        return {"dsa": lambda: self.vec("mixer_norm", j), "mlp0": lambda: self.vec("mlp_norm", j),
                "mlp1": lambda: self.vec("mlp_norm", 8 + j), "final": lambda: self.gain2[:, j:j + 1],
                "ffn1": lambda: self.vec("norm_ffn1_pre_2", j), "mix": lambda: self.vec("norm_mix_pre_2", j),
                "ffn2": lambda: self.vec("norm_ffn2_pre_2", j)}.get(self.then, lambda: None)()

    def square_and_operand(self, j):
        self.operand(j)
        self.add_square(j, adder=self.G)

    def operand(self, j):
        gain = self.gain(j)
        if gain is None:
            return
        A, V = self.A, self.V
        A.wait(self.x_ready[j], self.h_used[j])
        A.wait(self.gain2_ready if self.then == "final" else None)
        hi = A.done(A.e.activation(self.Hh[:, j, :], self.X[:, j, :], ACT.Copy, scale=gain))
        V.wait(hi)
        self.h_ready[j] = V.done(V.e.scalar_tensor_tensor(out=self.Hl[:, j, :], in0=self.X[:, j, :], scalar=gain,
                                                          in1=self.Hh[:, j, :], op0=ALU.mult, op1=ALU.subtract))

    def by_token(self, b, ssq, row, eps):
        A, V, M = self.A, self.V, self.M
        for t in range(NB):
            mm = M.e.matmul(self.bank[b][:, row * NB + t:row * NB + t + 1], ssq[:, t * P:(t + 1) * P],
                            self.c("ones")[:, 0:1], start=True, stop=True)
        return M.done(mm)

    def root(self, src, mark, row, eps):
        A, V = self.A, self.V
        st = self.stat[:, row, :]
        A.wait(mark, self.vecs_ready, self.stat_used)
        m = A.done(A.e.activation(st, src, ACT.Sqrt, bias=self.c("eps")[:, eps:eps + 1], scale=1.0 / D))
        V.wait(m)
        return m, V.done(V.e.reciprocal(st, st))

    def rstd_sums(self):
        M = self.M
        b = self.bank.next()
        M.wait(self.bank.read[b])
        M.wait(self.ssq_ready)
        mk = self.ssq_used = self.by_token(b, self.ssq, 0, 0)
        self.bank.read[b], m = self.root(self.bank[b][:, 0:NB], mk, 0, 0)
        return m

    def rstd_spread(self, row, mark):
        V, M = self.V, self.M
        V.wait(mark, self.rb_used)
        m = V.done(V.e.tensor_tensor(self.diag[:, :, :],
                                    self.c("ident").unsqueeze(1).to_broadcast([P, NB, P]),
                                    self.stat[:, row, :].unsqueeze(2).to_broadcast([P, NB, P]), ALU.mult))
        b = self.bank.next()
        M.wait(self.bank.read[b])
        M.wait(m)
        mk = self.rb_used = M.done(M.e.matmul(self.bank[b][:, :], self.c("ones"), self.diag[:, :, :], start=True, stop=True))
        return b, mk

    def rstd(self):
        return self.rstd_spread(0, self.rstd_sums())

    def keep_rstd(self, b, mark):
        V = self.V
        V.wait(mark)
        self.rb_ready = V.done(V.e.tensor_copy(self.rb, self.bank[b][:, :]))
        self.bank.read[b] = self.rb_ready

    def rstd_between(self):
        yield
        m = self.rstd_sums()
        yield
        yield
        self.keep_rstd(*self.rstd_spread(0, m))

    def h_hi(self, j, s, mark):
        A = self.A
        A.wait(mark, self.h_used[j])
        return A.done(A.e.activation(self.Hh[:, j, :], self.scratch[s][:, :], ACT.Copy))

    def h_lo(self, j, s, hi):
        V = self.V
        V.wait(hi)
        self.h_ready[j] = V.done(V.e.tensor_tensor(self.Hl[:, j, :], self.scratch[s][:, :], self.Hh[:, j, :], ALU.subtract))
        self.scratch.read[s] = self.h_ready[j]

    def split_h(self, j, s, mark):
        self.h_lo(j, s, self.h_hi(j, s, mark))

    def h_wait(self, kt):
        return self.h_ready[kt]

    def h_read(self, k0, nk, mark):
        for k in range(k0, k0 + nk):
            self.h_used[k] = mark

    def add_to_x(self, square):
        def evacuate(o, b, mark):
            V = self.V
            V.wait(mark, self.x_ready[o])
            self.x_ready[o] = V.done(V.e.tensor_tensor(self.X[:, o, :], self.bank[b][:, :], self.X[:, o, :], ALU.add))
            self.bank.read[b] = self.x_ready[o]
            self.bank.give_back(b)
            if square:
                self.add_square(o)
                if o >= 4:
                    self.operand(o - 4)
                if o == KT - 1:
                    for j in range(4, KT):
                        self.operand(j)
        return evacuate

    def rope(self, b, mark, out):
        A, V, M = self.A, self.V, self.M
        s, s2 = self.scratch.next(), self.scratch.next()
        A.wait(self.scratch.read[s])
        V.wait(self.scratch.read[s2])
        A.wait(mark)
        G = self.G
        raw = A.done(A.e.activation(self.scratch[s][:, :], self.bank[b][:, :], ACT.Copy))
        self.bank.read[b] = raw
        self.bank.give_back(b)
        b2 = self.bank.next()
        M.wait(self.bank.read[b2])
        M.wait(raw, self.rope_loaded)
        sw = M.done(M.e.matmul(self.bank[b2][:, :], self.c("swap"), self.scratch[s][:, :], start=True, stop=True))
        G.wait(raw, self.rope_loaded)
        m1 = G.done(G.e.tensor_tensor(out, self.scratch[s][:, :], self.rope_t[:, 0:T], ALU.mult))
        V.wait(sw)
        m2 = V.done(V.e.tensor_tensor(self.scratch[s2][:, :], self.bank[b2][:, :], self.rope_t[:, T:2 * T], ALU.mult))
        self.bank.read[b2] = m2
        self.bank.give_back(b2)
        G.wait(m2, m1)
        m3 = G.done(G.e.tensor_tensor(out, out, self.scratch[s2][:, :], ALU.add))
        self.scratch.read[s] = m3
        self.scratch.read[s2] = m3
        return m3

    def dsa(self):
        A, V, M, G = self.A, self.V, self.M, self.G
        with ExitStack() as s:
            sb = lambda n, sh, dt=F32: self.sb(n, sh, dt, s)
            self.rope_t = sb("rope", [P, 2 * T])
            Q, K, Vt = sb("q_t", [P, KT, T]), sb("k_t", [P, 2, T]), sb("v", [P, NB, KV_COLS])
            QI, KI, WI = sb("qi_t", [P, 4, T]), sb("ki_t", [P, T]), sb("wi", [P, NB, IW_COLS])
            self.load_constants("dsa", s)
            width = [P * (b + 1) for b in range(NB)]
            SC = [sb(f"score{b}", [P, width[b]]) for b in range(NB)]
            BI = [self.c("causal_bias")] + [sb(f"bias{b}", [P, width[b]]) for b in range(1, NB)]
            top = [sb(f"top{b}", [P, 8]) for b in range(NB)]
            self.rope_loaded = self.load_small.done(A.e.dma_start(self.rope_t[:, :], self.io["rope"]))
            i, wh, wl = self.piece("ki")
            kb = self.bank.next()
            M.wait(self.bank.read[kb])
            for kt in range(KT):
                M.wait(self.h_ready[kt])
                c = kt * 136
                mm = self.mm3(self.bank[kb][:, :], wh[:, c:c + P], wl[:, c:c + P], self.Hh[:, kt, :], self.Hl[:, kt, :],
                              kt == 0, kt == KT - 1)
            ki_m = M.done(mm)
            rstd_m = self.rstd_sums()
            wb = self.bank.next()
            M.wait(self.bank.read[wb])
            for kt in range(KT):
                c = kt * 136 + IW_COLS
                mm = self.mm3(self.bank[wb][:, :], wh[:, c:c + P], wl[:, c:c + P], self.Hh[:, kt, :], self.Hl[:, kt, :],
                              kt == 0, kt == KT - 1)
            wi_m = M.done(mm)
            self.end_piece(i, wi_m)
            rb, rb_m = self.rstd_spread(0, rstd_m)
            V.wait(rb_m, self.rope_loaded)
            rope3 = self.rope_t[:, :].rearrange("p (c t) -> p c t", c=2)
            self.rope_loaded = V.done(V.e.tensor_tensor(
                rope3, rope3, self.bank[rb][:, :].unsqueeze(1).to_broadcast([P, 2, T]), ALU.mult))
            self.bank.read[rb] = self.rope_loaded
            r, quad = self.scratch.next(), slice(P - 32, P)
            A.wait(self.scratch.read[r])
            A.wait(wi_m)
            wi_t = A.done(A.e.activation(self.scratch[r][quad, :], self.bank[wb][quad, :], ACT.Copy))
            self.bank.read[wb] = wi_t
            wb = self.bank.next()
            M.wait(self.bank.read[wb])
            M.wait(wi_t)
            for t in range(NB):
                mm = M.e.transpose(self.bank[wb][:, 32 * t:32 * t + 32], self.scratch[r][quad, t * P:t * P + P],
                                   self.c("ident")[quad, quad])
            wi_m = self.scratch.read[r] = M.done(mm)
            V.wait(wi_m, rstd_m)
            wi = V.done(V.e.scalar_tensor_tensor(
                out=WI[:, :, :], in0=self.bank[wb][:, 0:P].rearrange("p (b h) -> p b h", b=NB)[:, :, 32 - IW_COLS:32],
                scalar=IDX_HEADS ** -0.5 * HD ** -0.5, in1=self.stat[:, 0, :].unsqueeze(2).to_broadcast([P, NB, IDX_HEADS]),
                op0=ALU.mult, op1=ALU.mult))
            self.bank.read[wb] = wi
            self.bank.give_back(wb)
            ki = self.rope(kb, ki_m, KI[:, :])
            qi = {}

            def qi_out(o, b, mark):
                qi[o] = self.rope(b, mark, QI[:, o, :])
            self.linear("qi", KT, 1, self.Hh, self.Hl, qi_out, self.h_wait)

            scores = []

            def score_steps():
                acc = [None] * NB
                for h in range(IDX_HEADS):
                    p0 = HD * (h % 2)
                    for b in range(1, NB):
                        n = width[b]
                        k = self.bank.next()
                        M.wait(self.bank.read[k])
                        M.wait(qi[h // 2], ki)
                        mk = M.done(M.e.matmul(self.bank[k][:, 0:n], QI[p0:p0 + HD, h // 2, b * P:(b + 1) * P],
                                              KI[p0:p0 + HD, 0:n], start=True, stop=True))
                        r = self.scratch.next()
                        A.wait(self.scratch.read[r])
                        A.wait(mk)
                        rl = A.done(A.e.activation(self.scratch[r][:, 0:n], self.bank[k][:, 0:n], ACT.Relu))
                        self.bank.read[k] = rl
                        self.bank.give_back(k)
                        V.wait(rl, wi, acc[b])
                        w = WI[:, b, h:h + 1]
                        if h == 0:
                            acc[b] = V.done(V.e.tensor_scalar(SC[b][:, :], self.scratch[r][:, 0:n], w, None, ALU.mult))
                        else:
                            acc[b] = V.done(V.e.scalar_tensor_tensor(out=SC[b][:, :], in0=self.scratch[r][:, 0:n], scalar=w,
                                                                    in1=SC[b][:, :], op0=ALU.mult, op1=ALU.add))
                        self.scratch.read[r] = acc[b]
                    yield
                for b in range(1, NB):
                    V.wait(acc[b], self.rope_loaded)
                    d = SC[b][:, b * P:(b + 1) * P]
                    acc[b] = V.done(V.e.tensor_tensor(d, d, self.c("causal_score"), ALU.add))
                mx = [None] * NB
                for r in range(TOPK // 8):
                    for b in range(1, NB):
                        V.wait(acc[b])
                        mx[b] = V.done(V.e.max(top[b][:, :], SC[b][:, :]))
                    for b in range(1, NB):
                        V.wait(mx[b])
                        acc[b] = V.done(V.e.match_replace(SC[b][:, :], top[b][:, :], SC[b][:, :], SCORE_TAKEN))
                    yield
                for b in range(1, NB):
                    V.wait(acc[b])
                    scores.append(V.done(V.e.tensor_scalar(BI[b][:, :], SC[b][:, :], SCORE_TAKEN, NEG, ALU.not_equal, ALU.mult)))

            steps = score_steps()

            def some_steps(n=5):
                for _ in range(n):
                    next(steps, None)

            qm = {}
            for g in range(2):
                banks = [self.bank.next(keep=True) for _ in range(4)]
                M.wait(*(self.bank.read[x] for x in banks))
                for k0 in range(0, KT, 4):
                    i, wh, wl = self.piece("q")
                    for o in range(4):
                        for k in range(4):
                            c = k * 512 + o * P
                            mm = self.mm3(self.bank[banks[o]][:, :], wh[:, c:c + P], wl[:, c:c + P],
                                          self.Hh[:, k0 + k, :], self.Hl[:, k0 + k, :], k0 + k == 0, k0 + k == KT - 1)
                        if k0 + k == KT - 1:
                            mark = M.done(mm)
                            qm[4 * g + o] = self.rope(banks[o], mark, Q[:, 4 * g + o, :])
                        elif o == 3:
                            mark = M.done(mm)
                    self.end_piece(i, mark)
                    some_steps()
            kb = [self.bank.next(keep=True) for _ in range(2)]
            M.wait(*(self.bank.read[x] for x in kb))
            vb = [self.bank.next(keep=True) for _ in range(NB)]
            M.wait(*(self.bank.read[x] for x in vb))
            km, vm = [], []
            for k0 in range(0, KT, 4):
                i, wh, wl = self.piece("kv")
                for o in range(2):
                    for k in range(4):
                        c, kt = k * 512 + o * P, k0 + k
                        mm = self.mm3(self.bank[kb[o]][:, :], wh[:, c:c + P], wl[:, c:c + P],
                                      self.Hh[:, kt, :], self.Hl[:, kt, :], kt == 0, kt == KT - 1)
                    if k0:
                        km.append(M.done(mm))
                for t in range(NB):
                    for k in range(4):
                        c, kt, ts = k * 512 + KV_COLS, k0 + k, slice(t * P, t * P + P)
                        mm = self.mm3(self.bank[vb[t]][:, 0:KV_COLS], self.Hh[:, kt, ts], self.Hl[:, kt, ts],
                                      wh[:, c:c + KV_COLS], wl[:, c:c + KV_COLS], kt == 0, kt == KT - 1)
                    if k0:
                        vm.append(M.done(mm))
                mark = M.done(mm) if not k0 else vm[-1]
                self.end_piece(i, mark)
                some_steps()
            for k in range(KT):
                self.h_used[k] = vm[-1]
            kr = [self.rope(kb[o], km[o], K[:, o, :]) for o in range(2)]
            vr = []
            for t in range(NB):
                A.wait(vm[t], rstd_m)
                vr.append(A.done(A.e.activation(Vt[:, t, :], self.bank[vb[t]][:, 0:KV_COLS], ACT.Copy,
                                                scale=self.stat[:, 0, t:t + 1])))
                self.bank.read[vb[t]] = vr[-1]
                self.bank.give_back(vb[t])
            for _ in steps:
                pass

            turned_behind, summed_behind, SM = 3, 2, 8
            small = sb("softmax", [P, SM, 4])
            Pm = Turns([sb(f"prob{i}", [P, T]) for i in range(4)])
            PT = Turns([sb(f"prob_t{i}", [P, T]) for i in range(3)])
            items = [(q, u, b) for q in range(KT) for u in range(2) for b in range(NB)]
            st, obank = {}, {}

            def logits(n):
                q, u, b = items[n]
                g, w, p0 = q // 4, width[b], HD * u
                k = self.bank.next()
                M.wait(self.bank.read[k])
                M.wait(qm[q], kr[g])
                mk = M.done(M.e.matmul(self.bank[k][:, 0:w], Q[p0:p0 + HD, q, b * P:(b + 1) * P], K[p0:p0 + HD, g, 0:w],
                                      start=True, stop=True))
                r = Pm.next()
                V.wait(Pm.read[r])
                sm = small[:, n % SM, :]
                V.wait(mk, *scores, self.rope_loaded)
                if n >= SM:
                    V.wait(st[n - SM][3])
                m = V.done(V.e.tensor_tensor_reduce(Pm[r][:, 0:w], self.bank[k][:, 0:w], BI[b][:, :], -HD ** -0.5, 3.0e38,
                                                   ALU.add, ALU.min, sm[:, 0:1]))
                self.bank.read[k] = m
                self.bank.give_back(k)
                A.wait(m)
                m = A.done(A.e.activation(Pm[r][:, 0:w], Pm[r][:, 0:w], ACT.Exp, bias=sm[:, 0:1], scale=-1.0,
                                         accum_out=sm[:, 1:2]))
                st[n] = (r, m)

            def normalise(n):
                r, m = st[n]
                w, sm = width[items[n][2]], small[:, n % SM, :]
                V.wait(m)
                m = V.done(V.e.reciprocal(sm[:, 2:3], sm[:, 1:2]))
                V.wait(m)
                m = V.done(V.e.tensor_scalar(Pm[r][:, 0:w], Pm[r][:, 0:w], sm[:, 2:3], None, ALU.mult))
                st[n] = (r, m, None, m)

            def transposes(n):
                q, u, b = items[n]
                r, m = st[n][0:2]
                k = self.bank.next()
                M.wait(self.bank.read[k])
                M.wait(m)
                for j in range(b + 1):
                    mm = M.e.transpose(self.bank[k][:, j * P:(j + 1) * P], Pm[r][:, j * P:(j + 1) * P], self.c("ident"))
                mk = M.done(mm)
                Pm.read[r] = mk
                x = A if n % 2 else V
                t = PT.next()
                x.wait(PT.read[t])
                x.wait(mk)
                w = width[b]
                if n % 2:
                    cp = A.done(A.e.activation(PT[t][:, 0:w], self.bank[k][:, 0:w], ACT.Copy))
                else:
                    cp = V.done(V.e.tensor_copy(PT[t][:, 0:w], self.bank[k][:, 0:w]))
                self.bank.read[k] = cp
                self.bank.give_back(k)
                st[n] = (t, cp, None, st[n][3])

            def values(n):
                q, u, b = items[n]
                t, cp = st[n][0:2]
                if u == 0 and b == 0:
                    obank[q] = o_sum[q % 2]
                    M.wait(o_read[q % 2])
                ob, kvh = obank[q], 2 * (q // 4) + u
                M.wait(cp, *vr)
                for j in range(b + 1):
                    mm = M.e.matmul(ob[HD * u:HD * u + HD, b * P:(b + 1) * P], Vt[:, j, kvh * HD:(kvh + 1) * HD],
                                    PT[t][:, j * P:(j + 1) * P], start=(j == 0), stop=(j == b))
                mk = M.done(mm)
                PT.read[t] = mk
                if u == 1 and b == NB - 1:
                    A.wait(mk, self.h_used[q])
                    hi = A.done(A.e.activation(self.Hh[:, q, :], ob, ACT.Copy))
                    V.wait(hi, self.h_used[q])
                    lo = V.done(V.e.tensor_tensor(self.Hl[:, q, :], ob, self.Hh[:, q, :], ALU.subtract))
                    o_read[q % 2] = lo
                    self.h_ready[q] = lo

            ob2 = [self.bank.next(keep=True) for _ in range(2)]
            M.wait(*(self.bank.read[x] for x in ob2))
            o_sum, o_read = [self.bank[b][:, :] for b in ob2], [None, None]
            N = len(items)
            for n in range(N + turned_behind + summed_behind):
                if n < N:
                    logits(n)
                if 1 <= n < N + 1:
                    normalise(n - 1)
                if turned_behind <= n < N + turned_behind:
                    transposes(n - turned_behind)
                if turned_behind + summed_behind <= n < N + turned_behind + summed_behind:
                    values(n - turned_behind - summed_behind)
            for b, m in zip(ob2, o_read):
                self.bank.read[b] = m
                self.bank.give_back(b)
            self.stat_used = vr[-1]
            values_taken = self.h_ready[KT - 1]
            self.linear("wo", KT, 2, self.Hh, self.Hl, self.add_to_x(True), lambda kt, at=list(self.h_ready): at[kt], self.h_read)
            self.all_wait(values_taken)

    def mlp(self, l):
        A, V, M, G = self.A, self.V, self.M, self.G
        with ExitStack() as s:
            NU = 16
            Uh, Ul = self.sb(f"u_hi{l}", [P, NU, T], F32R, s), self.sb(f"u_lo{l}", [P, NU, T], F32R, s)
            um, ur = [None] * NU, [None] * NU
            for g in range(D_FF // P // NU):
                def up_out(o, b, mark):
                    r = self.scratch.next()
                    V.wait(self.scratch.read[r])
                    V.wait(mark, self.rb_ready)
                    m = V.done(V.e.scalar_tensor_tensor(out=self.scratch[r][:, :], in0=self.bank[b][:, :], scalar=0.0,
                                                       in1=self.rb, op0=ALU.max, op1=ALU.mult))
                    self.bank.read[b] = m
                    self.bank.give_back(b)
                    self.square_split(self.scratch, r, m, Uh[:, o, :], Ul[:, o, :], um, ur, o)
                self.linear("up", KT, NU // 4, self.Hh, self.Hl, up_out, self.h_wait,
                            self.h_read if g == 1 else None, None, None if g else self.stepper(self.rstd_between()))

                def u_read(k0, nk, mark):
                    for k in range(k0, k0 + nk):
                        ur[k] = mark
                self.linear("down", NU, 2, Uh, Ul, self.add_to_x(g == 1), lambda k: um[k], u_read)
            self.all_wait(ur[NU - 1])

    def stepper(self, steps):
        return lambda: next(steps, None)

    def square_split(self, ring, r, m, hi_out, lo_out, um, ur, o):
        A, V = self.A, self.V
        A.wait(m)
        sq = A.done(A.e.activation(ring[r][:, :], ring[r][:, :], ACT.Square))
        A.wait(sq, ur[o])
        hi = A.done(A.e.activation(hi_out, ring[r][:, :], ACT.Copy))
        V.wait(hi, ur[o])
        lo = V.done(V.e.tensor_tensor(lo_out, ring[r][:, :], hi_out, ALU.subtract))
        ring.read[r] = lo
        um[o] = lo

    def rwkv(self):
        A, V, M, G = self.A, self.V, self.M, self.G
        right = ExitStack()
        sbr = lambda n, sh: self.sb(n, sh, F32, right, side="right")
        R, K, Vt = sbr("rw_r", [P, KT, T]), sbr("rw_k", [P, KT, T]), sbr("rw_v", [P, NB, D])
        TW, TA, SG = sbr("rw_tanh_w", [HD, T]), sbr("rw_a_in", [HD, T]), sbr("rw_sig_g", [P, 2, T])
        omu = sbr("rw_one_less_mu", [P, 48])
        rm, km, vm = [None] * KT, [None] * KT, []
        RN = sbr("rw_kk_rstd", [16, T])
        cin = self.load_constants("rwkv", right, side="right")

        with ExitStack() as s:
            H = self.sb("rw_h", [P, KT, T + 1], F32, s)
            z = V.done(V.e.memset(H[:, :, 0:1], 0.0))
            mu0 = VAT["rwkv_mu"]
            om = V.done(V.e.tensor_scalar(omu[:, :], self.vecs[:, mu0:mu0 + 48], -1.0, 1.0, ALU.mult, ALU.add))
            b, mk = self.rstd()
            hm = []
            V.wait(mk)
            for j in range(KT):
                V.wait(self.x_ready[j])
                hm.append(V.done(V.e.scalar_tensor_tensor(out=H[:, j, 1:T + 1], in0=self.X[:, j, :],
                                                         scalar=self.vec("mixer_norm", 8 + j), in1=self.bank[b][:, :],
                                                         op0=ALU.mult, op1=ALU.mult)))
            self.bank.read[b] = hm[-1]
            self.bank.give_back(b)

            def shifted(c, j):
                r = self.scratch.next()
                V.wait(self.scratch.read[r])
                V.wait(hm[j], om, z)
                o = self.scratch[r][:, :]
                m = V.done(V.e.tensor_scalar(o, H[:, j, 1:T + 1], omu[:, 8 * c + j:8 * c + j + 1], None, ALU.mult))
                V.wait(m)
                return r, V.done(V.e.scalar_tensor_tensor(out=o, in0=H[:, j, 0:T], scalar=self.vec("rwkv_mu", 8 * c + j),
                                                         in1=o, op0=ALU.mult, op1=ALU.add))

            WA = R[:, 0:2, :].rearrange("p k t -> p (k t)").rearrange("p (k c) -> p k c", k=KT)
            G1 = K[:, 0:3, :].rearrange("p k t -> p (k t)")[:, 0:160 * KT].rearrange("p (k c) -> p k c", k=KT)
            for dst, name in ((WA[:, :, 0:HD], "rwkv_w1"), (WA[:, :, HD:P], "rwkv_a1"), (G1, "rwkv_g1")):
                low_in = self.low_loaded.done(self.S.e.dma_start(dst, self.io[name][0].rearrange("(k p) n -> p k n", p=P)))
            sig = [None]

            def low_wa():
                M.wait(low_in)
                for c, at, out, fn in ((3, 0, TW, ACT.Tanh), (4, HD, TA, ACT.Copy)):
                    b = self.bank.next(keep=True)
                    M.wait(self.bank.read[b])
                    for j in range(KT):
                        r, m = shifted(c, j)
                        M.wait(m)
                        mk = self.scratch.read[r] = M.done(M.e.matmul(self.bank[b][0:HD, :], WA[:, j, at:at + HD],
                                                                      self.scratch[r][:, :], start=(j == 0),
                                                                      stop=(j == KT - 1)))
                        if j < KT - 1:
                            yield
                    A.wait(mk)
                    self.bank.read[b] = A.done(A.e.activation(out[:, :], self.bank[b][0:HD, :], fn))
                    self.bank.give_back(b)
                    yield

            def low_g():
                b, b2 = self.bank.next(keep=True), self.bank.next(keep=True)
                M.wait(self.bank.read[b])
                M.wait(self.bank.read[b2])
                for j in range(KT):
                    r, m = shifted(5, j)
                    M.wait(m)
                    M.e.matmul(self.bank[b][:, :], G1[:, j, 0:P], self.scratch[r][:, :],
                               start=(j == 0), stop=(j == KT - 1))
                    mk = self.scratch.read[r] = M.done(M.e.matmul(self.bank[b2][0:32, :], G1[:, j, P:160],
                                                                  self.scratch[r][:, :], start=(j == 0),
                                                                  stop=(j == KT - 1)))
                    if j < KT - 1:
                        yield
                A.wait(mk)
                self.bank.read[b] = A.done(A.e.activation(SG[:, 0, :], self.bank[b][:, :], ACT.Sigmoid))
                sig[0] = self.bank.read[b2] = A.done(A.e.activation(SG[0:32, 1, :], self.bank[b2][0:32, :], ACT.Sigmoid))
                self.bank.give_back(b)
                self.bank.give_back(b2)
                yield

            def mix(c, tiles):
                behind = None
                for j in tiles:
                    r, m = shifted(c, j)
                    hi = self.h_hi(j, r, m)
                    if behind:
                        self.h_lo(*behind)
                    behind = (j, r, hi)
                self.h_lo(*behind)

            first, rest = range(4), range(4, KT)
            self.split_piece()
            mix(2, range(KT))
            low = low_wa()
            for g in range(2):
                banks = [self.bank.next(keep=True) for _ in range(NB)]
                M.wait(*(self.bank.read[x] for x in banks))
                for k0 in range(0, KT, 4):
                    i, wh, wl = self.piece("v")
                    for k in range(4):
                        for t in range(NB):
                            kt, ts, w = k0 + k, slice(t * P, t * P + P), slice(k * T, k * T + T)
                            if t == 0 and g == 0:
                                M.wait(self.h_ready[kt])
                            mm = self.mm3(self.bank[banks[t]][:, :], self.Hh[:, kt, ts], self.Hl[:, kt, ts],
                                          wh[:, w], wl[:, w], kt == 0, kt == KT - 1)
                        if k == 3:
                            mk = M.done(mm)
                        for _ in range(0 if g == 0 and k0 == 0 else 2 if g == 1 and k0 == 0 else 1):
                            next(low)
                    self.end_piece(i, mk)
                    if g:
                        self.h_read(k0, 4, mk)
                        if k0 == 0:
                            mix(0, first)
                for t in range(NB):
                    A.wait(mk)
                    vm.append(A.done(A.e.activation(Vt[:, t, g * T:g * T + T], self.bank[banks[t]][:, :], ACT.Copy)))
                    self.bank.read[banks[t]] = vm[-1]
                    self.bank.give_back(banks[t])

            def keep(dst, marks):
                def evacuate(o, b, mark):
                    A.wait(mark)
                    marks[o] = A.done(A.e.activation(dst[:, o, :], self.bank[b][:, :], ACT.Copy))
                    self.bank.read[b] = marks[o]
                    self.bank.give_back(b)
                return evacuate
            mix(0, rest)

            def between_strips():
                low = low_g()
                for n in range(4 * KT // 2):
                    if 4 <= n < 12:
                        next(low)
                    yield

            def between_pieces():
                for n in range(4):
                    if n == 2:
                        mix(1, first)
                    yield
            self.linear("r", KT, 2, self.Hh, self.Hl, keep(R, rm), self.h_wait, self.h_read,
                        self.stepper(between_pieces()), self.stepper(between_strips()))
            mix(1, rest)
            lora = sig[0]
            self.hold_split = True
            knorm = self.bank.next(keep=True)
            M.wait(self.bank.read[knorm], cin)
            keep_k, squared = keep(K, km), {}

            def add_knorm(j):
                r, m = squared[j]
                M.wait(m)
                self.scratch.read[r] = M.done(M.e.matmul(
                    self.bank[knorm][0:16, :], self.c("head_col")[:, 16 - 2 * j:32 - 2 * j], self.scratch[r][:, :],
                    start=(j == 0), stop=(j == KT - 1)))
                return self.scratch.read[r]

            def evacuate_k(o, b, mark):
                keep_k(o, b, mark)
                r = self.scratch.next()
                A.wait(km[o], self.scratch.read[r])
                squared[o] = (r, A.done(A.e.activation(self.scratch[r][:, :], K[:, o, :], ACT.Square,
                                                       scale=self.vec("rwkv_k_k", o))))
                if o:
                    add_knorm(o - 1)
            self.linear("k", KT, 2, self.Hh, self.Hl, evacuate_k, self.h_wait, self.h_read)
            knorm_done = add_knorm(KT - 1)
            self.all_wait(self.h_ready[KT - 1], self.h_used[KT - 1], km[KT - 1])
        self.op_ctx.close()

        with ExitStack() as s:
            sb = lambda n, sh: self.sb(n, sh, F32, s)
            W2 = sb("rw_w2a2", [HD, 2, D])
            self.load_constants("scan", s)
            self.load_small.done(A.e.dma_start(W2[:, 0, :], self.io["rwkv_w2"][0]))
            cin = self.load_small.done(A.e.dma_start(W2[:, 1, :], self.io["rwkv_a2"][0]))
            c = self.c
            mask = lambda n: c(n).bitcast(I32).unsqueeze(1).to_broadcast([P, NB, P])
            ident4 = c("ident").unsqueeze(1).to_broadcast([P, NB, P])
            AT = [sb(f"rw_at{i}", [P, T]) for i in range(2)]
            BT = [sb(f"rw_bt{i}", [P, T]) for i in range(1)]
            BK = [sb(f"rw_bk{i}", [P, 2, NB, P]) for i in range(2)]
            GM = [[sb(f"rw_g{i}{u}", [P, 3, NB, P]) for u in range(2)] for i in range(2)]
            LT_ = [[sb(f"rw_lt{i}{u}", [P, NB, P]) for u in range(2)] for i in range(2)]
            X_ = [sb(f"rw_x{u}", [P, T]) for u in range(2)]
            XT = [[sb(f"rw_xt{i}{u}", [P, NB, P]) for u in range(2)] for i in range(2)]
            MX = [sb(f"rw_mx{u}", [P, NB, HD]) for u in range(2)]
            SQ = sb("rw_square", [P, T])
            ST = [sb(f"rw_state{i}", [P, P]) for i in range(2)]
            RH, SA = sb("rw_rhs", [P, P]), sb("rw_sa", [P, P])
            PM, PE_ = [sb(f"rw_mid{i}", [P, NB]) for i in range(2)], [sb(f"rw_end{i}", [P, NB]) for i in range(2)]
            omka = sb("rw_one_less_half_ka", [P, KT])
            half = sb("rw_halves", [P, 3 * KT])
            small = [None]
            ka0 = VAT["rwkv_k_a"]
            V.wait(cin, self.vecs_ready)
            V.done(V.e.tensor_scalar(omka[:, :], self.vecs[:, ka0:ka0 + KT], -0.5, 1.0, ALU.mult, ALU.add))
            for n, name in enumerate(("rwkv_w0", "rwkv_a0", "rwkv_k_a")):
                at = VAT[name]
                halves = V.done(V.e.tensor_scalar(half[:, n * KT:n * KT + KT], self.vecs[:, at:at + KT], 0.5, None, ALU.mult))
            A.wait(halves)
            zero = []
            for i in range(2):
                for u in range(2):
                    zero.append(G.done(G.e.memset(GM[i][u][:, :, :, :], 0.0)))
            for u in range(2):
                for i in range(2):
                    zero.append(G.done(G.e.memset(LT_[i][u][:, :, :], 0.0)))
            zero = zero[-1]

            b, mk = knorm, knorm_done
            V.wait(mk)
            m = V.done(V.e.tensor_scalar(RN[:, :], self.bank[b][0:16, :], 1e-24, None, ALU.max))
            self.bank.read[b] = m
            self.bank.give_back(b)
            A.wait(m)
            m = A.done(A.e.activation(RN[:, :], RN[:, :], ACT.Sqrt))
            V.wait(m)
            rn = V.done(V.e.reciprocal(RN[:, :], RN[:, :]))

            vb = self.bank.next(keep=True)
            M.wait(self.bank.read[vb])
            pair = {}

            def prepare(j):
                i = j % 2
                d = pair[j] = {}
                vec = self.vec
                states_end = pair[j - 2]["end"] if j >= 2 else ()
                before = pair[j - 1] if j else {}
                LT = LT_[i]

                def sc(writer=V):
                    r = self.scratch.next()
                    writer.wait(self.scratch.read[r])
                    return r, self.scratch[r][:, :]
                k1, k2 = self.bank.next(), self.bank.next()
                M.wait(self.bank.read[k1])
                M.wait(self.bank.read[k2])
                M.wait(lora, cin)
                js = slice(j * P, j * P + P)
                M.e.matmul(self.bank[k1][:, :], W2[:, 0, js], TW[:, :], start=True, stop=True)
                mk = M.done(M.e.matmul(self.bank[k2][:, :], W2[:, 1, js], TA[:, :], start=True, stop=True))
                rw, w = sc(A)
                A.wait(mk)
                ws = A.done(A.e.activation(w, self.bank[k1][:, :], ACT.Tanh, bias=half[:, j:j + 1], scale=0.5))
                self.bank.read[k1] = ws
                self.bank.give_back(k1)
                ra, a = sc(A)
                am = A.done(A.e.activation(a, self.bank[k2][:, :], ACT.Tanh, bias=half[:, KT + j:KT + j + 1], scale=0.5))
                self.bank.read[k2] = am
                self.bank.give_back(k2)
                yield
                V.wait(ws)
                m = V.done(V.e.tensor_scalar(w, w, -0.5 * float(np.exp(-0.5)), -0.5 * float(np.exp(-0.5)), ALU.mult, ALU.add))
                yield
                V.wait(m)
                rc, cl = sc()
                m = V.done(V.e.tensor_tensor_scan(cl, c("chunk_start"), w, 0.0, ALU.mult, ALU.add))
                cl3 = cl.rearrange("p (c t) -> p c t", c=NB)
                mid = cl3[:, :, 63:64]
                A.wait(m, *states_end)
                d["pm"] = A.done(A.e.activation(PM[i][:, :].unsqueeze(2), mid, ACT.Exp))
                yield
                V.wait(m)
                rd, dc = sc()
                m = V.done(V.e.tensor_tensor(dc.rearrange("p (c t) -> p c t", c=NB), cl3,
                                            mid.to_broadcast([P, NB, P]), ALU.subtract))
                self.scratch.read[rc] = m
                yield
                V.wait(d["pm"])
                V.wait(m)
                m2 = V.done(V.e.tensor_tensor(w, dc, w, ALU.subtract))
                r1, e1 = sc(A)
                A.wait(m, m2)
                m1 = A.done(A.e.activation(e1, dc, ACT.Exp))
                m3 = A.done(A.e.activation(w, w, ACT.Exp))
                m2 = A.done(A.e.activation(dc, dc, ACT.Exp, scale=-1.0))
                e2, e3 = dc, w
                yield
                V.wait(m1, *states_end)
                V.wait(d["pm"])
                d["pe"] = V.done(V.e.tensor_tensor(PE_[i][:, 0:NB - 1].unsqueeze(2),
                                                  e1.rearrange("p (c t) -> p c t", c=NB)[:, 0:NB - 1, P - 1:P],
                                                  PM[i][:, 1:NB].unsqueeze(2), ALU.mult))
                yield
                rk, kk = sc()
                V.wait(km[j], am)
                kk_m = V.done(V.e.tensor_scalar(kk, K[:, j, :], vec("rwkv_k_k", j), None, ALU.mult))
                bt = BT[0]
                V.wait(before.get("bt_read"))
                t1 = V.done(V.e.tensor_scalar(bt[:, :], a, half[:, 2 * KT + j:2 * KT + j + 1], omka[:, j:j + 1], ALU.mult, ALU.add))
                yield
                V.wait(t1, kk_m)
                kf = V.done(V.e.tensor_tensor(K[:, j, :], K[:, j, :], bt[:, :], ALU.mult))
                yield
                kb = self.bank.next()
                M.wait(self.bank.read[kb])
                M.wait(rn)
                mk = M.done(M.e.matmul(self.bank[kb][:, :], c("head_row", 16)[:, js], RN[:, :], start=True, stop=True))
                yield
                V.wait(mk, kk_m)
                kn = V.done(V.e.tensor_tensor(kk, kk, self.bank[kb][:, :], ALU.mult))
                self.bank.read[kb] = kn
                self.bank.give_back(kb)
                yield
                V.wait(kf, rm[j], t1)
                bo = V.done(V.e.scalar_tensor_tensor(out=bt[:, :], in0=R[:, j, :], scalar=vec("rwkv_r_k", j),
                                                    in1=K[:, j, :], op0=ALU.mult, op1=ALU.mult))
                yield
                kb = self.bank.next()
                M.wait(self.bank.read[kb])
                M.wait(bo)
                mk = M.done(M.e.matmul(self.bank[kb][:, :], c("blockones"), bt[:, :], start=True, stop=True))
                V.wait(kn, m3, *states_end)
                d["at"] = V.done(V.e.scalar_tensor_tensor(out=AT[i][:, :], in0=kk, scalar=-1.0, in1=e3, op0=ALU.mult, op1=ALU.mult))
                V.wait(kn)
                m = V.done(V.e.scalar_tensor_tensor(out=kk, in0=a, scalar=1.0, in1=kk, op0=ALU.add, op1=ALU.mult))
                yield
                V.wait(m, m2, mk)
                d["bt"] = V.done(V.e.scalar_tensor_tensor(out=bt[:, :], in0=kk, scalar=0.5, in1=e2, op0=ALU.mult, op1=ALU.mult))
                self.scratch.read[rk] = d["bt"]
                yield
                V.wait(mk, d["at"], m)
                bs = V.done(V.e.tensor_copy(a, self.bank[kb][:, :]))
                self.bank.read[kb] = bs
                self.bank.give_back(kb)
                kb = self.bank.next()
                M.wait(self.bank.read[kb])
                M.wait(vm[-1])
                for t in range(NB):
                    mm = M.e.transpose(self.bank[kb][:, t * P:t * P + P], Vt[:, t, js], c("ident"))
                mk = M.done(mm)
                yield
                V.wait(mk, bs)
                bv = V.done(V.e.tensor_tensor(a, a, self.bank[kb][:, :], ALU.mult))
                self.bank.read[kb] = bv
                self.bank.give_back(kb)
                yield
                V.wait(m2, kf)
                kt = V.done(V.e.tensor_tensor(K[:, j, :], K[:, j, :], e2, ALU.mult))
                V.wait(m1, rm[j], bo)
                rt = d["rt"] = V.done(V.e.tensor_tensor(R[:, j, :], R[:, j, :], e1, ALU.mult))
                self.scratch.read[rw] = d["at"]
                self.scratch.read[rd] = kt
                self.scratch.read[r1] = rt
                yield "head"
                for x, (src, mark) in enumerate(((bt, d["bt"]), (K[:, j, :], kt))):
                    kb = self.bank.next()
                    M.wait(self.bank.read[kb])
                    M.wait(mark)
                    for t in range(NB):
                        mm = M.e.transpose(self.bank[kb][:, t * P:t * P + P], src[:, t * P:t * P + P], c("ident"))
                    mk = M.done(mm)
                    A.wait(mk, *states_end)
                    d["bk"] = A.done(A.e.activation(BK[i][:, x, :, :], self.bank[kb][:, :], ACT.Copy))
                    self.bank.read[kb] = d["bk"]
                    self.bank.give_back(kb)
                yield
                d["g"] = [None] * 2
                lt = [None] * 2
                for u in range(2):
                    hs = slice(HD * u, HD * u + HD)
                    for n, (left, right_, mk_, msk) in enumerate((
                            (bt, AT[i], None, "s_lt_t"), (bt, R[:, j, :], None, "s_le_t"),
                            (K[:, j, :], AT[i], None, "s_lt_t"), (K[:, j, :], R[:, j, :], None, "s_le_t"))):
                        kb = self.bank.next()
                        M.wait(self.bank.read[kb])
                        M.wait(d["bt"], d["at"], kt, rt)
                        for t in range(NB):
                            ts = slice(t * P, t * P + P)
                            mm = M.e.matmul(self.bank[kb][:, ts], left[hs, ts], right_[hs, ts], start=True, stop=True)
                        mk = M.done(mm)
                        V.wait(mk, zero, cin)
                        dst = LT[u] if n == 0 else GM[i][u][:, n - 1, :, :]
                        if n:
                            V.wait(*states_end)
                        else:
                            V.wait(pair[j - 2]["lt_read"][u] if j >= 2 else None)
                        m = V.done(V.e.copy_predicated(dst if n else dst[:, :, :], mask(msk),
                                                      self.bank[kb][:, :].rearrange("p (c t) -> p c t", c=NB)))
                        self.bank.read[kb] = m
                        self.bank.give_back(kb)
                        if n == 0:
                            lt[u] = m
                        d["lt"] = lt
                        d["g"][u] = m
                        d["bt_read"] = mk
                        yield
                V.wait(mk, bv)
                d["bv"] = V.done(V.e.tensor_copy(K[:, j, :], a))
                self.scratch.read[ra] = d["bv"]

            def invert(j):
                i = j % 2
                d = pair[j]
                states_end = pair[j - 2]["end"] if j >= 2 else ()
                before = pair[j - 1] if j else {}
                LT, lt = LT_[i], d["lt"]
                x, xt = [None] * 2, [None] * 2
                for u in range(2):
                    G.wait(before.get("x_read"), self.vecs_ready)
                    x[u] = G.done(G.e.tensor_copy(X_[u][:, :].rearrange("p (c t) -> p c t", c=NB), ident4))
                    G.wait(*states_end)
                    xt[u] = G.done(G.e.tensor_copy(XT[i][u][:, :, :], ident4))
                    V.wait(lt[u], xt[u])
                    xt[u] = V.done(V.e.copy_predicated(XT[i][u][:, :, :], mask("level0T"), LT[u][:, :, :]))
                d["lt_read"] = [None] * 2
                for u in range(2):
                    kb = self.bank.next()
                    M.wait(self.bank.read[kb])
                    M.wait(lt[u])
                    for t in range(NB):
                        mm = M.e.transpose(self.bank[kb][:, t * P:t * P + P], LT[u][:, t, :], c("ident"))
                    mk = M.done(mm)
                    V.wait(mk, x[u])
                    x[u] = V.done(V.e.copy_predicated(X_[u][:, :].rearrange("p (c t) -> p c t", c=NB), mask("level0"),
                                                      self.bank[kb][:, :].rearrange("p (c t) -> p c t", c=NB)))
                    self.bank.read[kb] = x[u]
                    yield
                turn, its = [None] * 2, [None] * 2
                for lv in range(1, LEVELS + 1):
                    for u in range(2):
                        if lv < LEVELS:
                            even = lambda ap: ap.rearrange("p (n h b) -> p n h b", h=2, b=1 << lv)[:, :, 0, :]
                            kb = self.bank.next()
                            M.wait(self.bank.read[kb])
                            M.wait(x[u])
                            for t in range(NB):
                                mm = M.e.matmul(self.bank[kb][:, t * HD:t * HD + HD], LT[u][:, t, :],
                                                even(X_[u][:, t * P:t * P + P]), start=True, stop=True)
                            mk = d["lt_read"][u] = M.done(mm)
                            V.wait(mk)
                            m = V.done(V.e.tensor_tensor(MX[u][:, :, :],
                                                         self.bank[kb][:, 0:NB * HD].rearrange("p (c t) -> p c t", c=NB),
                                                         c(f"level{lv}").unsqueeze(1).to_broadcast([P, NB, HD]), ALU.mult))
                            self.bank.read[kb] = m
                            its[u] = m
                        if lv > 1:
                            kb = self.bank.next()
                            M.wait(self.bank.read[kb])
                            M.wait(x[u])
                            for t in range(NB):
                                mm = M.e.transpose(self.bank[kb][:, t * P:t * P + P], X_[u][:, t * P:t * P + P], c("ident"))
                            mk = turn[u] = M.done(mm)
                            A.wait(mk)
                            xt[u] = A.done(A.e.activation(XT[i][u][:, :, :], self.bank[kb][:, :], ACT.Copy))
                            self.bank.read[kb] = xt[u]
                        yield
                    if lv == LEVELS:
                        break
                    for u in range(2):
                        kb = self.bank.next()
                        M.wait(self.bank.read[kb])
                        M.wait(its[u], xt[u])
                        for t in range(NB):
                            mm = M.e.matmul(self.bank[kb][:, t * HD:t * HD + HD], XT[i][u][:, t, :], MX[u][:, t, :],
                                            start=True, stop=True)
                        mk = M.done(mm)
                        V.wait(mk, turn[u])
                        x[u] = V.done(V.e.tensor_tensor(even(X_[u][:, :]), even(X_[u][:, :]),
                                                        self.bank[kb][:, 0:NB * HD].rearrange("p (n b) -> p n b", b=1 << lv),
                                                        ALU.add))
                        self.bank.read[kb] = x[u]
                        yield
                mk = turn[1]
                d["x_read"] = mk
                d["xt"] = xt

            def states(j):
                i = j % 2
                d = pair[j]
                st = None
                for ch in range(NB):
                    cs = slice(ch * P, ch * P + P)
                    S0, S1 = ST[ch % 2], ST[(ch + 1) % 2]
                    kb = self.bank.next()
                    M.wait(self.bank.read[kb])
                    M.wait(st, d["g"][1], d["at"], vm[-1])
                    if ch:
                        M.e.matmul(self.bank[kb][:, 0:P], AT[i][:, cs], S0[:, :], start=True, stop=False)
                    for u in range(2):
                        hs = slice(HD * u, HD * u + HD)
                        v = Vt[:, ch, j * P + HD * u:j * P + HD * u + HD]
                        mm = M.e.matmul(self.bank[kb][:, hs], GM[i][u][:, 1, ch, :], v, start=(ch == 0),
                                        stop=(ch == 0 or u == 1))
                    mk = M.done(mm)
                    A.wait(mk, small[0])
                    rh = A.done(A.e.activation(RH[:, :], self.bank[kb][:, 0:P], ACT.Copy))
                    self.bank.read[kb] = rh
                    self.bank.give_back(kb)
                    yield
                    kb = self.bank.next()
                    M.wait(self.bank.read[kb])
                    M.wait(rh, *d["xt"])
                    for u in range(2):
                        hs = slice(HD * u, HD * u + HD)
                        mm = M.e.matmul(self.bank[kb][:, hs], XT[i][u][:, ch, :], RH[:, hs], start=True, stop=True)
                    xr = mk = M.done(mm)
                    A.wait(mk)
                    sa = A.done(A.e.activation(SA[:, :], self.bank[kb][:, 0:P], ACT.Copy))
                    self.bank.read[kb] = sa
                    self.bank.give_back(kb)
                    yield
                    kb, kc = self.bank.next(), self.bank.next()
                    M.wait(self.bank.read[kb])
                    M.wait(self.bank.read[kc])
                    M.wait(sa, d["bk"], d["rt"])
                    if ch < NB - 1:
                        M.e.matmul(self.bank[kb][:, 0:P], BK[i][:, 0, ch, :], SA[:, :], start=True, stop=False)
                        mk = M.done(M.e.matmul(self.bank[kb][:, 0:P], BK[i][:, 1, ch, :], Vt[:, ch, j * P:j * P + P],
                                              start=False, stop=True))
                        V.wait(mk, st, d["pe"])
                        if ch:
                            m = V.done(V.e.tensor_tensor(S1[:, :], self.bank[kb][:, 0:P], S0[:, :], ALU.add))
                            V.wait(m)
                            src = S1[:, :]
                        else:
                            V.wait(small[0])
                            src = self.bank[kb][:, 0:P]
                        stn = V.done(V.e.scalar_tensor_tensor(out=S1[:, :], in0=src, scalar=PE_[i][:, ch:ch + 1],
                                                             in1=c("blockones"), op0=ALU.mult, op1=ALU.mult))
                        self.bank.read[kb] = stn
                        self.bank.give_back(kb)
                    if ch:
                        M.e.matmul(self.bank[kc][:, 0:P], S0[:, :], R[:, j, cs], start=True, stop=False)
                    for u in range(2):
                        hs = slice(HD * u, HD * u + HD)
                        v = Vt[:, ch, j * P + HD * u:j * P + HD * u + HD]
                        out = self.bank[kc][hs, 0:P]
                        M.e.matmul(out, SA[:, hs], GM[i][u][:, 0, ch, :], start=(ch == 0), stop=False)
                        mm = M.e.matmul(out, v, GM[i][u][:, 2, ch, :], start=False, stop=True)
                    mk = M.done(mm)
                    small[0] = mk
                    A.wait(mk)
                    ym = A.done(A.e.activation(R[:, j, cs], self.bank[kc][:, 0:P], ACT.Copy))
                    self.bank.read[kc] = ym
                    self.bank.give_back(kc)
                    st = stn
                    yield
                d["end"] = (mk, stn)
                kb = self.bank.next()
                M.wait(self.bank.read[kb])
                M.wait(ym)
                mk = M.done(M.e.matmul(self.bank[kb][:, :], c("blockones"), R[:, j, :], start=True, stop=True))
                V.wait(mk, ym)
                rm[j] = V.done(V.e.scalar_tensor_tensor(out=R[:, j, :], in0=self.bank[kb][:, :], scalar=-1.0 / HD,
                                                       in1=R[:, j, :], op0=ALU.mult, op1=ALU.add))
                self.bank.read[kb] = rm[j]
                self.bank.give_back(kb)
                A.wait(rm[j], pair[j - 1]["var"] if j else None)
                m = A.done(A.e.activation(SQ[:, :], R[:, j, :], ACT.Square))
                yield
                M.wait(m)
                mk = M.done(M.e.matmul(self.bank[vb][0:16, :], c("head_col")[:, 16 - 2 * j:32 - 2 * j],
                                      SQ[:, :], start=(j == 0), stop=(j == KT - 1)))
                d["var"] = mk

            def head(steps):
                for x in steps:
                    if x == "head":
                        return
                    yield

            def beside(a, b):
                done = object()
                while True:
                    x, y = next(a, done), next(b, done)
                    if x is done and y is done:
                        break

            preparing = prepare(0)
            for _ in preparing:
                pass
            gate_of = lambda j: Vt[:, :, j * P:(j + 1) * P]

            def gates():
                nonlocal g2_piece, g2
                g2_piece, _, _ = self.piece("g2")
                g2 = self.raw[g2_piece % 3]
                M.wait(lora)
                for j in range(KT - 1):
                    gate[j] = gate_tile(j)
                    yield
                    yield

            def gate_tile(j):
                js = slice(j * P, j * P + P)
                kb = self.bank.next()
                M.wait(self.bank.read[kb])
                M.e.matmul(self.bank[kb][:, :], g2[:, js], SG[:, 0, :], start=True, stop=False)
                mk = M.done(M.e.matmul(self.bank[kb][:, :], g2[0:32, D + j * P:D + j * P + P], SG[0:32, 1, :],
                                      start=False, stop=True))
                g2_read[0] = mk
                A.wait(mk, *pair[j]["end"])
                self.bank.read[kb] = A.done(A.e.activation(gate_of(j), self.bank[kb][:, :], ACT.Copy))
                return self.bank.read[kb]

            g2_piece, g2, g2_read = None, None, [None]
            gate = {}
            for j in range(KT + 1):
                if j == KT:
                    preparing = gates()
                following = prepare(j + 1) if j + 1 < KT else iter(())
                beside(chain(preparing, invert(j) if j < KT else ()), chain(states(j - 1) if j else (), head(following)))
                preparing = following
            A.wait(pair[KT - 1]["var"], rn)
            m = A.done(A.e.activation(RN[:, :], self.bank[vb][0:16, :], ACT.Sqrt, bias=c("eps")[0:16, 1:2], scale=1.0 / HD))
            self.bank.read[vb] = m
            self.bank.give_back(vb)
            V.wait(m)
            rs = V.done(V.e.reciprocal(RN[:, :], RN[:, :]))
            gate[KT - 1] = gate_tile(KT - 1)
            self.end_piece(g2_piece, g2_read[0])
            self.all_wait(pair[KT - 1]["var"], pair[KT - 1]["bv"], *pair[KT - 1]["end"])
        self.open_operands()
        self.hold_split = False
        self.split_piece()
        self.split_piece()
        behind = None
        for j in range(KT):
            kb = self.bank.next()
            M.wait(self.bank.read[kb])
            M.wait(rs)
            mk = M.done(M.e.matmul(self.bank[kb][:, :], self.c("head_row", 16)[:, j * P:j * P + P], RN[:, :],
                                  start=True, stop=True))
            r = self.scratch.next()
            o = self.scratch[r][:, :]
            V.wait(self.scratch.read[r])
            V.wait(mk, rm[j])
            m = V.done(V.e.scalar_tensor_tensor(out=o, in0=R[:, j, :], scalar=self.vec("rwkv_lnx_w", j),
                                               in1=self.bank[kb][:, :], op0=ALU.mult, op1=ALU.mult))
            self.bank.read[kb] = m
            V.wait(m, pair[j]["bv"])
            m = V.done(V.e.scalar_tensor_tensor(out=o, in0=o, scalar=self.vec("rwkv_lnx_b", j), in1=K[:, j, :],
                                               op0=ALU.add, op1=ALU.add))
            V.wait(m, gate[j])
            o3 = o.rearrange("p (c t) -> p c t", c=NB)
            m = V.done(V.e.tensor_tensor(o3, o3, gate_of(j), ALU.mult))
            hi = self.h_hi(j, r, m)
            if behind:
                self.h_lo(*behind)
            behind = (j, r, hi)
        self.h_lo(*behind)
        rwkv_read = self.h_ready[KT - 1]
        self.linear("rwkv_wo", KT, 2, self.Hh, self.Hl, self.add_to_x(True), self.h_wait, self.h_read)
        self.all_wait(mk, rwkv_read)
        right.close()

    def final_norm(self):
        pass

    def two_rstds(self):
        V, M = self.V, self.M
        yield
        b = self.bank.next()
        M.wait(self.bank.read[b])
        M.wait(self.ssq_ready, self.ssq2_ready)
        self.by_token(b, self.ssq, 0, 0)
        mk = self.ssq_used = self.by_token(b, self.ssq2, 1, 0)
        sums = self.bank[b][:, 0:2 * NB].rearrange("p (r t) -> p r t", r=2)
        st = self.stat
        _, m = self.root(sums[:, 0, :], mk, 0, 0)
        V.wait(m)
        s2 = V.done(V.e.tensor_tensor(st[:, 1, :], sums[:, 1, :], st[:, 0, :], ALU.mult))
        self.bank.read[b] = s2
        V.wait(s2)
        s2 = V.done(V.e.tensor_tensor(st[:, 1, :], st[:, 1, :], st[:, 0, :], ALU.mult))
        _, s2 = self.root(st[:, 1, :], s2, 2, 0)
        V.wait(s2)
        s2 = V.done(V.e.tensor_tensor(st[:, 3, :], st[:, 2, :], st[:, 0, :], ALU.mult))
        yield
        b, mk = self.rstd_spread(0, m)
        yield
        V.wait(mk)
        for j in range(KT):
            V.wait(self.x_ready[j], self.h_ready[j])
            self.x_ready[j] = V.done(V.e.scalar_tensor_tensor(out=self.X[:, j, :], in0=self.X[:, j, :],
                                                           scalar=self.vec("final_norm", j), in1=self.bank[b][:, :],
                                                           op0=ALU.mult, op1=ALU.mult))
        self.bank.read[b] = self.x_ready[KT - 1]
        self.keep_rstd(*self.rstd_spread(3, s2))

    def post_norm(self, Y, name, scale):
        V = self.V
        self.split_piece()
        b, mk = self.rstd()
        V.wait(mk)
        for j in range(KT):
            r = self.scratch.next()
            V.wait(self.scratch.read[r])
            m = V.done(V.e.scalar_tensor_tensor(out=self.scratch[r][:, :], in0=Y[:, j, :], scalar=self.vec(name, j),
                                               in1=self.bank[b][:, :], op0=ALU.mult, op1=ALU.mult))
            V.wait(m, self.x_ready[j])
            self.x_ready[j] = V.done(V.e.scalar_tensor_tensor(out=self.X[:, j, :], in0=self.scratch[r][:, :], scalar=scale,
                                                           in1=self.X[:, j, :], op0=ALU.mult, op1=ALU.add))
            self.scratch.read[r] = self.x_ready[j]
            if self.then and j:
                self.square_and_operand(j - 1)
        if self.then:
            self.square_and_operand(KT - 1)
        self.bank.read[b] = m
        return m

    def ffn(self, tag):
        A, V, M = self.A, self.V, self.M
        rstd = self.stepper(self.two_rstds() if tag == "1" else self.rstd_between())
        with ExitStack() as s:
            NU = 12
            Uh, Ul = self.sb(f"f_hi{tag}", [P, NU, T], F32R, s), self.sb(f"f_lo{tag}", [P, NU, T], F32R, s)
            Y = self.sb(f"f_out{tag}", [P, KT, T], F32, s)
            um, ur, ym = [None] * NU, [None] * NU, [None] * KT
            for g, nu in enumerate((NU, D_FF2 // P - NU)):
                gate = {}

                def gate_up(o, b, mark):
                    f, part = o // 4 * 2 + o % 2, o % 4 // 2
                    if part == 0:
                        r = self.scratch.next()
                        V.wait(self.scratch.read[r])
                        V.wait(mark, self.rb_ready)
                        m = V.done(V.e.tensor_tensor(self.scratch[r][:, :], self.bank[b][:, :], self.rb, ALU.mult))
                        self.bank.read[b] = m
                        self.bank.give_back(b)
                        A.wait(m)
                        m = A.done(A.e.activation(self.scratch[r][:, :], self.scratch[r][:, :], ACT.Silu))
                        V.wait(m)
                        m = V.done(V.e.tensor_tensor(self.scratch[r][:, :], self.scratch[r][:, :], self.rb, ALU.mult))
                        gate[f] = (r, m)
                        return
                    r, m = gate[f]
                    V.wait(m, mark)
                    gu = V.done(V.e.tensor_tensor(self.scratch[r][:, :], self.scratch[r][:, :], self.bank[b][:, :], ALU.mult))
                    self.bank.read[b] = gu
                    self.bank.give_back(b)
                    A.wait(gu, ur[f])
                    hi = A.done(A.e.activation(Uh[:, f, :], self.scratch[r][:, :], ACT.Copy))
                    V.wait(hi, ur[f])
                    um[f] = V.done(V.e.tensor_tensor(Ul[:, f, :], self.scratch[r][:, :], Uh[:, f, :], ALU.subtract))
                    self.scratch.read[r] = um[f]
                self.linear("gu", KT, nu // 2, self.Hh, self.Hl, gate_up, self.h_wait, self.h_read if g else None,
                            None, None if g else rstd)

                def u_read(k0, nk, mark):
                    for k in range(k0, k0 + nk):
                        ur[k] = mark

                def out(o, b, mark):
                    V.wait(mark, ym[o])
                    if g == 0:
                        ym[o] = V.done(V.e.tensor_copy(Y[:, o, :], self.bank[b][:, :]))
                    else:
                        ym[o] = V.done(V.e.tensor_tensor(Y[:, o, :], Y[:, o, :], self.bank[b][:, :], ALU.add))
                        self.add_square(o, Y[:, o, :], ym[o])
                    self.bank.read[b] = ym[o]
                    self.bank.give_back(b)
                self.linear("ffn_out", nu, 2, Uh, Ul, out, lambda k: um[k], u_read)
            y_read = self.post_norm(Y, f"norm_ffn{tag}_post_2", 0.5)
            self.all_wait(ur[0], ur[NU - 1], ur[7], y_read)

    def mixer(self):
        A, V, M, G = self.A, self.V, self.M, self.G
        NH, DK = 4, 64
        with ExitStack() as s:
            sb = lambda n, sh: self.sb(n, sh, F32, s)
            cin = self.load_constants("mix", s)
            c = self.c
            QK, Vt, OS = sb("mx_qk", [P, 4, T]), sb("mx_v", [P, NB, T]), sb("mx_o", [P, 4, T])
            U = sb("mx_u", [P, 4, T + 2])
            S_, NS = sb("mx_s", [P, NB, T]), sb("mx_num", [P, 2, NH, T])
            GT = sb("mx_gates", [P, T])
            row = lambda n: sb(f"mx_row_{n}", [HD, T])
            ones_r, lf, e, u, l, dz = row("one"), row("lf"), row("e"), row("u"), row("l"), row("dz")
            cn, nm, en = row("c"), row("nm"), row("en")
            CT = sb("mx_ct", [P, NB, HD])
            V.wait(cin)
            pad = V.done(V.e.memset(U[:, :, 0:T + 2:T + 1], 0.0))
            on = V.done(V.e.memset(ones_r[:, :], 1.0))

            i, wh, wl = self.piece("gates")
            b = self.bank.next()
            M.wait(self.bank.read[b])
            for kt in range(KT):
                M.wait(self.h_ready[kt])
                w = slice(kt * P, kt * P + P)
                mm = self.mm3(self.bank[b][:, :], wh[:, w], wl[:, w], self.Hh[:, kt, :], self.Hl[:, kt, :],
                              kt == 0, kt == KT - 1)
            mk = M.done(mm)
            self.end_piece(i, mk)
            rstd_m = self.rstd_sums()
            self.keep_rstd(*self.rstd_spread(0, rstd_m))
            V.wait(mk, self.rb_ready)
            gm = V.done(V.e.tensor_tensor(GT[:, :], self.bank[b][:, :], self.rb, ALU.mult))
            A.wait(gm)
            gm2 = A.done(A.e.activation(GT[:, :], GT[:, :], ACT.Identity, bias=self.vec("gates", 0)))
            self.bank.read[b] = gm
            self.bank.give_back(b)

            def gate_rows():
                F, B = slice(0, 32), slice(32, 64)

                def v(ins):
                    m = V.done(ins)
                    V.wait(m)
                    return m
                V.wait(gm2, on)
                v(V.e.tensor_copy(cn[F, :], GT[0:32, :]))
                v(V.e.tensor_copy(cn[B, :], GT[32:64, ::-1]))
                v(V.e.tensor_copy(lf[F, :], GT[64:96, :]))
                m = v(V.e.tensor_copy(lf[B, :], GT[96:128, ::-1]))
                yield
                A.wait(m)
                m = A.done(A.e.activation(e[:, :], lf[:, :], ACT.Abs))
                A.wait(m)
                m = A.done(A.e.activation(e[:, :], e[:, :], ACT.Exp, scale=-1.0))
                V.wait(m)
                m = v(V.e.tensor_scalar(u[:, :], e[:, :], 1.0, None, ALU.add))
                A.wait(m)
                lm = A.done(A.e.activation(l[:, :], u[:, :], ACT.Ln))
                yield
                V.wait(lm)
                v(V.e.tensor_scalar(u[:, :], u[:, :], -1.0, None, ALU.add))
                v(V.e.tensor_scalar(dz[:, :], u[:, :], 0.0, None, ALU.is_equal))
                v(V.e.tensor_tensor(u[:, :], u[:, :], dz[:, :], ALU.add))
                v(V.e.reciprocal(u[:, :], u[:, :]))
                yield
                v(V.e.tensor_tensor(l[:, :], l[:, :], u[:, :], ALU.mult))
                v(V.e.tensor_tensor(l[:, :], l[:, :], dz[:, :], ALU.add))
                v(V.e.tensor_tensor(l[:, :], l[:, :], e[:, :], ALU.mult))
                v(V.e.scalar_tensor_tensor(out=lf[:, :], in0=lf[:, :], scalar=0.0, in1=l[:, :],
                                           op0=ALU.min, op1=ALU.subtract))
                v(V.e.tensor_tensor_scan(u[:, :], ones_r[:, :], lf[:, :], 0.0, ALU.mult, ALU.add))
                yield
                v(V.e.tensor_tensor(cn[:, :], cn[:, :], u[:, :], ALU.subtract))
                v(V.e.tensor_tensor_scan(l[:, :], cn[:, :], cn[:, :], -3.0e38, ALU.max, ALU.max))
                v(V.e.tensor_tensor(u[:, :], u[:, :], l[:, :], ALU.add))
                yield
                v(V.e.tensor_copy(e[:, :], cn[:, :]))
                v(V.e.tensor_copy(e[B, :], cn[B, ::-1]))
                v(V.e.tensor_scalar(nm[F, :], l[F, :], -1.0, None, ALU.mult))
                v(V.e.tensor_scalar(nm[B, :], l[B, ::-1], -1.0, None, ALU.mult))
                v(V.e.tensor_copy(dz[F, :], u[F, :]))
                m = v(V.e.tensor_copy(dz[B, :], u[B, ::-1]))
                A.wait(m)
                em = A.done(A.e.activation(en[:, :], dz[:, :], ACT.Exp, scale=-1.0))
                b = self.bank.next()
                M.wait(self.bank.read[b])
                M.wait(m, self.vecs_ready)
                for t in range(NB):
                    mm = M.e.transpose(self.bank[b][:, HD * t:HD * t + HD], e[:, t * P:t * P + P], c("ident", HD)[:, 0:HD])
                mk = M.done(mm)
                V.wait(mk)
                cm = V.done(V.e.tensor_copy(CT[:, :, :], self.bank[b][:, 0:NB * HD]))
                self.bank.read[b] = cm
                self.bank.give_back(b)
                rows.extend([em, cm, m])

            rows = []
            steps = gate_rows()
            step = lambda: next(steps, None)

            qk, vt, og, um, ym = [None] * 4, [None] * NB, [None] * 4, [None] * 4, [None] * 4

            def qk_out(o, b, mark):
                V.wait(mark)
                qk[o] = V.done(V.e.tensor_tensor(QK[:, o, :], self.bank[b][:, :], self.rb, ALU.mult))
                self.bank.read[b] = qk[o]
                self.bank.give_back(b)
            self.linear("mq", KT, 1, self.Hh, self.Hl, qk_out, self.h_wait, None, step)
            banks = [self.bank.next(keep=True) for _ in range(NB)]
            M.wait(*(self.bank.read[x] for x in banks))
            for k0 in range(0, KT, 4):
                i, wh, wl = self.piece("mv")
                for k in range(4):
                    for t in range(NB):
                        kt, ts, w = k0 + k, slice(t * P, t * P + P), slice(k * T, k * T + T)
                        mm = self.mm3(self.bank[banks[t]][:, :], self.Hh[:, kt, ts], self.Hl[:, kt, ts],
                                      wh[:, w], wl[:, w], kt == 0, kt == KT - 1)
                mk = M.done(mm)
                self.end_piece(i, mk)
                step()
            for t in range(NB):
                A.wait(mk)
                vt[t] = A.done(A.e.activation(Vt[:, t, :], self.bank[banks[t]][:, :], ACT.Copy,
                                              scale=self.stat[:, 0, t:t + 1]))
                self.bank.read[banks[t]] = vt[t]
                self.bank.give_back(banks[t])

            def cg_out(o, b, mark):
                V.wait(mark)
                um[o] = V.done(V.e.tensor_tensor(U[:, o, 1:T + 1], self.bank[b][:, :], self.rb, ALU.mult))
                self.bank.read[b] = um[o]
                self.bank.give_back(b)

            def hc_out(o, b, mark):
                V.wait(um[o])
                m = V.done(V.e.tensor_tensor(U[:, o, 1:T + 1], U[:, o, 1:T + 1], self.rb, ALU.mult))
                V.wait(mark, m)
                um[o] = V.done(V.e.tensor_tensor(U[:, o, 1:T + 1], U[:, o, 1:T + 1], self.bank[b][:, :], ALU.mult))
                self.bank.read[b] = um[o]
                self.bank.give_back(b)

            def bg_out(o, b, mark):
                r = self.scratch.next()
                V.wait(self.scratch.read[r])
                y = self.scratch[r][:, :]
                V.wait(um[o], pad)
                m = V.done(V.e.tensor_scalar(y, U[:, o, 0:T], self.vec("conv_w_2", o), self.vec("conv_b_2", o), ALU.mult, ALU.add))
                for tap in (1, 2):
                    V.wait(m)
                    m = V.done(V.e.scalar_tensor_tensor(out=y, in0=U[:, o, tap:tap + T], scalar=self.vec("conv_w_2", 4 * tap + o),
                                                       in1=y, op0=ALU.mult, op1=ALU.add))
                V.wait(m)
                m = V.done(V.e.tensor_tensor(y, y, self.rb, ALU.mult))
                V.wait(m, mark)
                ym[o] = V.done(V.e.tensor_tensor(U[:, o, 1:T + 1], y, self.bank[b][:, :], ALU.mult))
                self.bank.read[b] = ym[o]
                self.bank.give_back(b)
                self.scratch.read[r] = ym[o]

            def o_out(o, b, mark):
                V.wait(mark)
                m = V.done(V.e.tensor_tensor(OS[:, o, :], self.bank[b][:, :], self.rb, ALU.mult))
                self.bank.read[b] = m
                A.wait(m)
                og[o] = A.done(A.e.activation(OS[:, o, :], OS[:, o, :], ACT.Sigmoid))
                self.bank.give_back(b)
            for name, out in (("cg", cg_out), ("hc", hc_out), ("bg", bg_out), ("mo", o_out)):
                self.linear(name, KT, 1, self.Hh, self.Hl, out, self.h_wait, self.h_read if name == "mo" else None, step)
            for _ in steps:
                pass
            em, cm, nmm = rows

            for o in range(4):
                A.wait(ym[o], self.h_used[o])
                hi = A.done(A.e.activation(self.Hh[:, o, :], U[:, o, 1:T + 1], ACT.Copy))
                V.wait(hi)
                self.h_ready[o] = V.done(V.e.tensor_tensor(self.Hl[:, o, :], U[:, o, 1:T + 1], self.Hh[:, o, :], ALU.subtract))

            den = self.bank.next(keep=True)
            M.wait(self.bank.read[den])
            nk, sm, mult = {}, {}, {}
            score = [[S_[:, si, :] for si in range(NB)], [U[:, si, 1:T + 1] for si in range(NB)]]
            items = [(h, d, n, si) for h in range(NH) for d in range(2)
                     for n, si in enumerate(range(NB) if d == 0 else range(NB - 1, -1, -1))]
            weights, run = {}, {}

            def scores(h):
                p0 = DK * (h % 2)
                for si in range(NB):
                    b = self.bank.next()
                    M.wait(self.bank.read[b])
                    M.wait(qk[h // 2], qk[2 + h // 2])
                    mk = M.done(M.e.matmul(self.bank[b][:, :], QK[p0:p0 + DK, 2 + h // 2, si * P:si * P + P],
                                          QK[p0:p0 + DK, h // 2, :], start=True, stop=True))
                    A.wait(mk, mult.get(h - 2) if h >= 2 else self.h_ready[3])
                    sm[h, si] = A.done(A.e.activation(score[h % 2][si], self.bank[b][:, :], ACT.Copy, scale=DK ** -0.5))
                    self.bank.read[b] = sm[h, si]

            def exponents(k):
                h, d, n, si = items[k]
                ts = slice(si * P, T) if d == 0 else slice(0, si * P + P)
                if n == 0:
                    if d == 0:
                        scores(h)
                    rows_d = slice(32 * d, 32 * d + 4)
                    b, nb = self.bank.next(keep=True), self.bank.next(keep=True)
                    M.wait(self.bank.read[b])
                    M.wait(nmm, cin)
                    mk = M.done(M.e.matmul(self.bank[b][:, :], c("row_pick")[rows_d, h * P:h * P + P], nm[rows_d, :],
                                          start=True, stop=True))
                    run[h, d] = (b, nb, mk)
                b, _, mk = run[h, d]
                r = self.scratch.next()
                V.wait(self.scratch.read[r])
                w = self.scratch[r][:, ts]
                V.wait(mk, cm)
                m = V.done(V.e.tensor_scalar(w, self.bank[b][:, ts], CT[:, si, 32 * d + h:32 * d + h + 1], 0.0,
                                             ALU.add, ALU.min))
                if n == NB - 1:
                    self.bank.read[b] = m
                    self.bank.give_back(b)
                A.wait(m)
                m = A.done(A.e.activation(w, w, ACT.Exp))
                G.wait(m, cin)
                dg = self.scratch[r][:, si * P:si * P + P]
                weights[k] = (r, w, ts, G.done(G.e.tensor_tensor(dg, dg, c("s_ge_t" if d else "s_le_t"), ALU.mult)))

            def sums(k):
                h, d, n, si = items[k]
                r, w, ts, masked = weights[k]
                nb = run[h, d][1]
                V.wait(masked, sm[h, si])
                m = mult[h] = V.done(V.e.tensor_tensor(w, w, score[h % 2][si][:, ts], ALU.mult))
                if n == 0:
                    M.wait(self.bank.read[nb])
                M.wait(m, vt[si])
                M.e.matmul(self.bank[nb][:, ts], Vt[:, si, h * P:h * P + P], w, start=(n == 0), stop=(n == NB - 1))
                mm = M.done(M.e.matmul(self.bank[den][32 * d:32 * d + 32, ts], c("one_col")[:, 32 - h:64 - h], w,
                                      start=(n == 0 and h == 0), stop=(n == NB - 1 and h == NH - 1)))
                self.scratch.read[r] = mm
                if n == NB - 1:
                    A.wait(mm)
                    nk[d, h] = A.done(A.e.activation(NS[:, d, h, :], self.bank[nb][:, :], ACT.Copy))
                    self.bank.read[nb] = nk[d, h]
                    self.bank.give_back(nb)
                return mm

            ahead = 3
            for k in range(len(items) + ahead):
                if k < len(items):
                    exponents(k)
                if k >= ahead:
                    mm = sums(k - ahead)
            A.wait(mm)
            m = A.done(A.e.activation(e[:, :], self.bank[den][0:HD, :], ACT.Abs))
            self.bank.read[den] = m
            self.bank.give_back(den)
            V.wait(m, em)
            m = V.done(V.e.tensor_tensor(e[:, :], e[:, :], en[:, :], ALU.max))
            V.wait(m)
            rd = V.done(V.e.reciprocal(e[:, :], e[:, :]))
            ss = self.bank.next(keep=True)
            M.wait(self.bank.read[ss])
            squared = {}
            for h in range(NH + 1):
                if h < NH:
                    for d in range(2):
                        rows_d = slice(32 * d, 32 * d + 4)
                        b = self.bank.next()
                        M.wait(self.bank.read[b])
                        M.wait(rd)
                        mk = M.done(M.e.matmul(self.bank[b][:, :], c("row_pick")[rows_d, h * P:h * P + P], e[rows_d, :],
                                              start=True, stop=True))
                        V.wait(mk, nk[d, h])
                        m = V.done(V.e.tensor_tensor(NS[:, d, h, :], NS[:, d, h, :], self.bank[b][:, :], ALU.mult))
                        self.bank.read[b] = m
                    V.wait(m)
                    nk[0, h] = V.done(V.e.tensor_tensor(NS[:, 0, h, :], NS[:, 0, h, :], NS[:, 1, h, :], ALU.add))
                    r = self.scratch.next()
                    A.wait(self.scratch.read[r])
                    A.wait(nk[0, h])
                    squared[h] = (r, A.done(A.e.activation(self.scratch[r][:, :], NS[:, 0, h, :], ACT.Square)))
                if h:
                    r, m = squared[h - 1]
                    M.wait(m)
                    mk = M.done(M.e.matmul(self.bank[ss][0:32, :], c("one_col")[:, 33 - h:65 - h], self.scratch[r][:, :],
                                          start=(h == 1), stop=(h == NH)))
                    self.scratch.read[r] = mk
            A.wait(mk)
            m = A.done(A.e.activation(u[0:32, :], self.bank[ss][0:32, :], ACT.Sqrt, bias=c("eps")[0:32, 0:1], scale=1.0 / P))
            self.bank.read[ss] = m
            self.bank.give_back(ss)
            V.wait(m)
            rs = V.done(V.e.reciprocal(u[0:32, :], u[0:32, :]))
            for h in range(NH):
                b = self.bank.next()
                M.wait(self.bank.read[b])
                M.wait(rs)
                mk = M.done(M.e.matmul(self.bank[b][:, :], c("row_pick")[0:4, h * P:h * P + P], u[0:4, :],
                                      start=True, stop=True))
                r = self.scratch.next()
                V.wait(self.scratch.read[r])
                V.wait(mk, nk[0, h], og[h])
                m = V.done(V.e.scalar_tensor_tensor(out=self.scratch[r][:, :], in0=NS[:, 0, h, :],
                                                   scalar=self.vec("mlstm_norm_2", h), in1=self.bank[b][:, :],
                                                   op0=ALU.mult, op1=ALU.mult))
                self.bank.read[b] = m
                self.bank.give_back(b)
                V.wait(m)
                m = V.done(V.e.tensor_tensor(self.scratch[r][:, :], self.scratch[r][:, :], OS[:, h, :], ALU.mult))
                self.split_h(4 + h, r, m)

            Y, ym = NS[:, :, :, :].rearrange("p d h t -> p (d h) t"), [None] * KT

            def out(o, b, mark):
                V.wait(mark, self.h_ready[KT - 1])
                ym[o] = V.done(V.e.tensor_copy(Y[:, o, :], self.bank[b][:, :]))
                self.bank.read[b] = ym[o]
                self.bank.give_back(b)
                self.add_square(o, Y[:, o, :], ym[o])
            self.stat_used = vt[-1]
            self.linear("mix_out", KT, 2, self.Hh, self.Hl, out, self.h_wait, self.h_read)
            self.all_wait(self.post_norm(Y, "norm_mix_post_2", 1.0), self.h_used[KT - 1])


_OUT = (1, T, D)
_MATS = ["dsa_w_in", "dsa_w_o", "mlp_w_up", "mlp_w_down", "rwkv_w_rkv", "rwkv_w1", "rwkv_w2", "rwkv_a1", "rwkv_a2",
         "rwkv_g1", "rwkv_g2", "rwkv_w_o", "w_ffn1_in_2", "w_ffn1_out_2", "w_mix_in_2", "w_mix_out_2",
         "w_ffn2_in_2", "w_ffn2_out_2"]


def host_arrays(inputs):
    rows = []
    for name, n in VECS:
        if name == "gates":
            row = np.zeros((1, P), np.float32)
            gi, gf = np.asarray(inputs["gate_i_bias_2"])[0], np.asarray(inputs["gate_f_bias_2"])[0]
            for q, part in enumerate((gi[0:4], gi[4:8], gf[0:4], gf[4:8])):
                row[0, 32 * q:32 * q + 4] = part
            rows.append(row)
        else:
            rows.append(np.asarray(inputs[name]).reshape(n, P))
    arrays = {"x": np.ascontiguousarray(inputs["x"]), "vecs": np.concatenate(rows, 0),
              "rope": rope_table()}
    for g in GROUPS:
        arrays[f"const_{g}"] = const_group(g)
    for name in _MATS:
        arrays[name] = np.ascontiguousarray(inputs[name])
    return arrays


def program(nc, arrays):
    io = {}
    for name, a in arrays.items():
        io[name] = nc.dram_tensor(f"in_{name}", a.shape, F32, kind="ExternalInput").ap()
    io["out"] = nc.dram_tensor("out", _OUT, F32, kind="ExternalOutput").ap()
    Program(nc, io).build()


def kernel(**inputs):
    import concourse.bacc as bacc
    from concourse.bass_utils import run_bass_kernel_spmd
    arrays = host_arrays(inputs)
    nc = bacc.Bacc("TRN2", target_bir_lowering=False, num_devices=1)
    program(nc, arrays)
    r = run_bass_kernel_spmd(nc, [{f"in_{n}": a for n, a in arrays.items()}], core_ids=[0])
    return r.results[0]["out"]
```
